# Optimizing a Trainium2 kernel written in Bass

```python
import jax, jax.numpy as jnp
from jax import lax
import numpy as np

D_MODEL = 1024
BATCH = 1
SEQ = 1024
DEPTH = 1

D_LRU = 1024
LRU_HEADS = 16
LRU_BW = D_LRU // LRU_HEADS
RG_C = 8.0
CONV_K = 4
D_SSD = 1024
SSD_HEAD_DIM = 64
SSD_HEADS = D_SSD // SSD_HEAD_DIM
SSD_GROUPS = 4
SSD_STATE = 128
SSD_CHUNK = 128
SSD_CONV_DIM = D_SSD + 2 * SSD_GROUPS * SSD_STATE
D_MIX = D_LRU + D_SSD
IN_COLS = 2 * D_LRU + D_SSD + SSD_CONV_DIM + SSD_HEADS
MOE_GROUPS = 4
EXPERTS_PER_GROUP = 8
N_EXPERTS = MOE_GROUPS * EXPERTS_PER_GROUP
TOP_K = 2
D_EXPERT = 512
MOE_BLOCK = 128
EPS = 1e-6

kernel_name = "hybrid_rglru_ssd_hmoe_trunk"

def rms_norm(x, w):
    xf = x.astype(jnp.float32)
    y = xf * lax.rsqrt(jnp.mean(xf * xf, axis=-1, keepdims=True) + EPS)
    return (y * w.astype(jnp.float32)).astype(x.dtype)

def causal_dwconv(x, w, b):
    c = x.shape[-1]
    y = lax.conv_general_dilated(
        x, w[:, None, :].astype(x.dtype), window_strides=(1,),
        padding=[(CONV_K - 1, 0)], dimension_numbers=('NWC', 'WIO', 'NWC'),
        feature_group_count=c)
    return y + b.astype(x.dtype)

def linear_recurrence(a, u):
    def combine(l, r):
        a1, b1 = l
        a2, b2 = r
        return a1 * a2, a2 * b1 + b2
    _, h = lax.associative_scan(combine, (a, u), axis=1)
    return h

def rg_lru(u, wa, ba, wx, bx, lam):
    bsz, s, _ = u.shape
    ub = u.reshape(bsz, s, LRU_HEADS, LRU_BW)
    r = jax.nn.sigmoid(jnp.einsum('bshi,hij->bshj', ub, wa.astype(jnp.float32)) + ba).reshape(bsz, s, D_LRU)
    i = jax.nn.sigmoid(jnp.einsum('bshi,hij->bshj', ub, wx.astype(jnp.float32)) + bx).reshape(bsz, s, D_LRU)
    log_a = RG_C * r * jax.nn.log_sigmoid(lam.astype(jnp.float32))
    a = jnp.exp(log_a)
    mult = jnp.sqrt(-jnp.expm1(2.0 * log_a))
    return linear_recurrence(a, mult * (i * u))

def ssd_chunked(x, dt, A, Bm, Cm):
    b, s, h, p = x.shape
    g, n = Bm.shape[2], Bm.shape[3]
    c, l = s // SSD_CHUNK, SSD_CHUNK
    Bh = jnp.repeat(Bm, h // g, axis=2).reshape(b, c, l, h, n)
    Ch = jnp.repeat(Cm, h // g, axis=2).reshape(b, c, l, h, n)
    xdt = (x * dt[..., None]).reshape(b, c, l, h, p)
    a_cs = jnp.cumsum((dt * A).reshape(b, c, l, h), axis=2)
    seg = a_cs[:, :, :, None, :] - a_cs[:, :, None, :, :]
    mask = jnp.tril(jnp.ones((l, l), dtype=bool))[None, None, :, :, None]
    Lmat = jnp.exp(jnp.where(mask, seg, -jnp.inf))
    scores = jnp.einsum('bclhn,bcshn->bclsh', Ch, Bh)
    y_diag = jnp.einsum('bclsh,bcshp->bclhp', scores * Lmat, xdt)
    decay_states = jnp.exp(a_cs[:, :, -1:, :] - a_cs)
    states = jnp.einsum('bclhn,bclh,bclhp->bchpn', Bh, decay_states, xdt)
    chunk_decay = jnp.exp(a_cs[:, :, -1, :])

    def step(prev, inp):
        st, dec = inp
        return prev * dec[:, :, None, None] + st, prev

    _, prev_states = lax.scan(step, jnp.zeros((b, h, p, n), jnp.float32),
                              (states.transpose(1, 0, 2, 3, 4), chunk_decay.transpose(1, 0, 2)))
    prev_states = prev_states.transpose(1, 0, 2, 3, 4)
    y_off = jnp.einsum('bclhn,bchpn,bclh->bclhp', Ch, prev_states, jnp.exp(a_cs))
    return (y_diag + y_off).reshape(b, s, h, p)

def hybrid_mixer(h, w_in, lru_conv_w, lru_conv_b, lru_wa, lru_ba, lru_wx, lru_bx, lru_lambda,
                 lru_norm, ssd_conv_w, ssd_conv_b, ssd_dt_bias, ssd_a_log, ssd_d, ssd_norm, w_out):
    bsz, s, _ = h.shape
    proj = h @ w_in
    o1 = D_LRU
    o2 = o1 + D_LRU
    o3 = o2 + D_SSD
    o4 = o3 + SSD_CONV_DIM
    lru_x, lru_gate, ssd_z, ssd_xbc, ssd_dt = (proj[..., :o1], proj[..., o1:o2], proj[..., o2:o3],
                                               proj[..., o3:o4], proj[..., o4:])
    u = causal_dwconv(lru_x, lru_conv_w, lru_conv_b).astype(jnp.float32)
    hr = rg_lru(u, lru_wa, lru_ba, lru_wx, lru_bx, lru_lambda)
    y_lru = rms_norm((jax.nn.gelu(lru_gate.astype(jnp.float32)) * hr).astype(h.dtype), lru_norm)
    xbc = jax.nn.silu(causal_dwconv(ssd_xbc, ssd_conv_w, ssd_conv_b).astype(jnp.float32))
    xs = xbc[..., :D_SSD].reshape(bsz, s, SSD_HEADS, SSD_HEAD_DIM)
    Bm = xbc[..., D_SSD:D_SSD + SSD_GROUPS * SSD_STATE].reshape(bsz, s, SSD_GROUPS, SSD_STATE)
    Cm = xbc[..., D_SSD + SSD_GROUPS * SSD_STATE:].reshape(bsz, s, SSD_GROUPS, SSD_STATE)
    dt = jax.nn.softplus(ssd_dt.astype(jnp.float32) + ssd_dt_bias.astype(jnp.float32))
    A = -jnp.exp(ssd_a_log.astype(jnp.float32))
    y = ssd_chunked(xs, dt, A, Bm, Cm) + xs * ssd_d.astype(jnp.float32)[:, None]
    y = y.reshape(bsz, s, D_SSD) * jax.nn.silu(ssd_z.astype(jnp.float32))
    y_ssd = rms_norm(y.astype(h.dtype), ssd_norm)
    return jnp.concatenate([y_lru, y_ssd], axis=-1) @ w_out

def hier_moe(h, w_coarse, b_coarse, w_fine, b_fine, w_gate, w_up, w_down):
    bsz, s, d = h.shape
    xt = h.reshape(-1, d)
    n = xt.shape[0]
    xf = xt.astype(jnp.float32)
    c_logits = xf @ w_coarse.astype(jnp.float32) + b_coarse.astype(jnp.float32)
    c_prob = jax.nn.softmax(c_logits, axis=-1)
    g_idx = jnp.argmax(c_logits, axis=-1)
    g_w = jnp.take_along_axis(c_prob, g_idx[:, None], axis=1)[:, 0]
    f_all = jnp.einsum('nd,gde->nge', xf, w_fine.astype(jnp.float32)) + b_fine.astype(jnp.float32)
    f_logits = jnp.take_along_axis(f_all, g_idx[:, None, None], axis=1)[:, 0]
    f_val, f_idx = lax.top_k(f_logits, TOP_K)
    f_w = jax.nn.softmax(f_val, axis=-1)
    expert = (g_idx[:, None] * EXPERTS_PER_GROUP + f_idx).reshape(-1).astype(jnp.int32)
    weight = (g_w[:, None] * f_w).reshape(-1)
    token = jnp.repeat(jnp.arange(n, dtype=jnp.int32), TOP_K)
    n_assign = n * TOP_K
    n_blocks = -(-(n_assign + N_EXPERTS * (MOE_BLOCK - 1)) // MOE_BLOCK)
    n_rows = n_blocks * MOE_BLOCK
    order = jnp.argsort(expert)
    e_sorted = expert[order]
    counts = jnp.bincount(expert, length=N_EXPERTS).astype(jnp.int32)
    padded = (counts + MOE_BLOCK - 1) // MOE_BLOCK * MOE_BLOCK
    pad_end = jnp.cumsum(padded)
    pad_start = pad_end - padded
    start = jnp.cumsum(counts) - counts
    dest = pad_start[e_sorted] + jnp.arange(n_assign, dtype=jnp.int32) - start[e_sorted]
    row_tok = jnp.zeros((n_rows,), jnp.int32).at[dest].set(token[order])
    row_w = jnp.zeros((n_rows,), jnp.float32).at[dest].set(weight[order])
    blk_expert = jnp.minimum(
        jnp.searchsorted(pad_end, jnp.arange(n_blocks, dtype=jnp.int32) * MOE_BLOCK, side='right'),
        N_EXPERTS - 1)
    xb = xt[row_tok].reshape(n_blocks, MOE_BLOCK, d)

    def expert_block(args):
        xi, e = args
        hid = jax.nn.silu(xi @ w_gate[e]) * (xi @ w_up[e])
        return hid @ w_down[e]

    yb = lax.map(expert_block, (xb, blk_expert)).reshape(n_rows, d)
    out = jnp.zeros_like(xt).at[row_tok].add(yb * row_w[:, None].astype(yb.dtype))
    return out.reshape(bsz, s, d)

def setup_inputs(seed: int = 0) -> dict:
    key = jax.random.key(seed)
    ks = jax.random.split(key, 32)
    f32 = jnp.float32
    nrm = lambda k, shape, scale: jax.random.normal(k, shape, f32) * scale
    gain = lambda k, shape: 1.0 + 0.01 * jax.random.normal(k, shape, f32)
    u = jax.random.uniform(ks[9], (DEPTH, D_LRU), f32, 0.9, 0.999)
    s_l = u ** (1.0 / RG_C)
    lam = jnp.log(s_l) - jnp.log1p(-s_l)
    dt0 = jnp.exp(jax.random.uniform(ks[13], (DEPTH, SSD_HEADS), f32) * (jnp.log(0.1) - jnp.log(0.001)) + jnp.log(0.001))
    dt_bias = dt0 + jnp.log(-jnp.expm1(-dt0))
    return {
        "x": jax.random.normal(ks[0], (BATCH, SEQ, D_MODEL), f32),
        "norm_mix": gain(ks[1], (DEPTH, D_MODEL)),
        "w_in": nrm(ks[2], (DEPTH, D_MODEL, IN_COLS), D_MODEL ** -0.5),
        "lru_conv_w": nrm(ks[3], (DEPTH, CONV_K, D_LRU), CONV_K ** -0.5),
        "lru_conv_b": nrm(ks[4], (DEPTH, D_LRU), 0.02),
        "lru_wa": nrm(ks[5], (DEPTH, LRU_HEADS, LRU_BW, LRU_BW), LRU_BW ** -0.5),
        "lru_ba": nrm(ks[6], (DEPTH, LRU_HEADS, LRU_BW), 0.02),
        "lru_wx": nrm(ks[7], (DEPTH, LRU_HEADS, LRU_BW, LRU_BW), LRU_BW ** -0.5),
        "lru_bx": nrm(ks[8], (DEPTH, LRU_HEADS, LRU_BW), 0.02),
        "lru_lambda": lam,
        "lru_norm": gain(ks[10], (DEPTH, D_LRU)),
        "ssd_conv_w": nrm(ks[11], (DEPTH, CONV_K, SSD_CONV_DIM), CONV_K ** -0.5),
        "ssd_conv_b": nrm(ks[12], (DEPTH, SSD_CONV_DIM), 0.02),
        "ssd_dt_bias": dt_bias,
        "ssd_a_log": jnp.log(jax.random.uniform(ks[14], (DEPTH, SSD_HEADS), f32, 1.0, 16.0)),
        "ssd_d": gain(ks[15], (DEPTH, SSD_HEADS)),
        "ssd_norm": gain(ks[16], (DEPTH, D_SSD)),
        "w_out": nrm(ks[17], (DEPTH, D_MIX, D_MODEL), D_MIX ** -0.5),
        "norm_ffn": gain(ks[18], (DEPTH, D_MODEL)),
        "w_coarse": nrm(ks[19], (DEPTH, D_MODEL, MOE_GROUPS), D_MODEL ** -0.5),
        "b_coarse": nrm(ks[20], (DEPTH, MOE_GROUPS), 0.01),
        "w_fine": nrm(ks[21], (DEPTH, MOE_GROUPS, D_MODEL, EXPERTS_PER_GROUP), D_MODEL ** -0.5),
        "b_fine": nrm(ks[22], (DEPTH, MOE_GROUPS, EXPERTS_PER_GROUP), 0.01),
        "w_gate": nrm(ks[23], (DEPTH, N_EXPERTS, D_MODEL, D_EXPERT), D_MODEL ** -0.5),
        "w_up": nrm(ks[24], (DEPTH, N_EXPERTS, D_MODEL, D_EXPERT), D_MODEL ** -0.5),
        "w_down": nrm(ks[25], (DEPTH, N_EXPERTS, D_EXPERT, D_MODEL), D_EXPERT ** -0.5),
        "final_norm": gain(ks[26], (D_MODEL,)),
    }

def reference(x, norm_mix, w_in, lru_conv_w, lru_conv_b, lru_wa, lru_ba, lru_wx, lru_bx, lru_lambda,
              lru_norm, ssd_conv_w, ssd_conv_b, ssd_dt_bias, ssd_a_log, ssd_d, ssd_norm, w_out,
              norm_ffn, w_coarse, b_coarse, w_fine, b_fine, w_gate, w_up, w_down, final_norm):
    for i in range(DEPTH):
        h = rms_norm(x, norm_mix[i])
        x = x + hybrid_mixer(h, w_in[i], lru_conv_w[i], lru_conv_b[i], lru_wa[i], lru_ba[i],
                             lru_wx[i], lru_bx[i], lru_lambda[i], lru_norm[i], ssd_conv_w[i],
                             ssd_conv_b[i], ssd_dt_bias[i], ssd_a_log[i], ssd_d[i], ssd_norm[i], w_out[i])
        h = rms_norm(x, norm_ffn[i])
        x = x + hier_moe(h, w_coarse[i], b_coarse[i], w_fine[i], b_fine[i], w_gate[i], w_up[i], w_down[i])
    return rms_norm(x, final_norm)


_drawn_inputs = setup_inputs


def setup_inputs(seed=0):
    import zlib

    import numpy as np

    out = dict(_drawn_inputs(seed))
    spreads = {}
    factors = {'norm_mix': 2.916,
     'lru_ba': 8.0,
     'lru_bx': 6.25,
     'lru_norm': 4.801,
     'ssd_d': 200.0,
     'ssd_norm': 4.864,
     'norm_ffn': 3.578,
     'b_coarse': 5.469,
     'b_fine': 5.746,
     'final_norm': 175.745}
    for name, (base, spread) in spreads.items():
        noise = np.random.default_rng([zlib.crc32(name.encode()), seed]).standard_normal(out[name].shape)
        drawn = base * np.exp(spread * noise) if base else spread * noise
        out[name] = __import__('jax').numpy.asarray(drawn.astype(out[name].dtype))
    for name, factor in factors.items():
        out[name] = (out[name] * factor).astype(out[name].dtype)
    return out
```

```python
from contextlib import ExitStack

import numpy as np

import concourse.bass as bass
from concourse import mybir

F32 = mybir.dt.float32
I32 = mybir.dt.int32
ALU = mybir.AluOpType
ACT = mybir.ActivationFunctionType
AX_X = mybir.AxisListType.X

P = 128
D = 1024
SEQ = 1024
KT = D // P
TT = SEQ // P
NH = 16
HD = 64
NG = 4
CONV_K = 4
MG, EG = 4, 8
NE = MG * EG
DE = 512
EPS = 1e-6
DT_COL = 5 * D
N_IN = DT_COL // P
T_GATE, T_Z, T_XBC = 8, 16, 24
NR = MG + NE
MAX_OVER = 15
NBLK = NE + MAX_OVER + 1
CH = KT + DE // P

PV_SIZES = dict(norm_mix=8, lru_cw=32, lru_cb=8, lru_ba=8, lru_bx=8, lam=8, lru_norm=8,
                ssd_norm=8, ssd_cw=64, ssd_cb=16, ssd_d=8)
PV = {}
for _n, _s in PV_SIZES.items():
    PV[_n] = sum(PV_SIZES[m] for m in list(PV_SIZES)[:list(PV_SIZES).index(_n)])
NPV = sum(PV_SIZES.values())


class Steps:

    def __init__(self, eng, sem):
        self.eng, self.sem, self.done, self.turn = eng, sem, 0, None

    def link(self, ins):
        ins.then_inc(self.sem, 1)
        self.done += 1
        self.eng.wait_ge(self.sem, self.done if self.turn is None else self.turn + self.done)

    def begin(self, i, per):
        self.turn, self.first, self.per = i * per, self.done, per

    def end(self, trips):
        assert self.done - self.first == self.per, (self.done - self.first, self.per)
        self.turn, self.done = None, self.first + trips * self.per


def link(eng, ins, sem, value):
    ins.then_inc(sem, 1)
    eng.wait_ge(sem, value)


def build(nc, a):
    with ExitStack() as ctx:
        def sb(name, shape, dt=F32):
            return ctx.enter_context(nc.sbuf_tensor(name, shape, dt))

        def sem(name):
            return ctx.enter_context(nc.semaphore(name))

        def dram(name, shape):
            return nc.dram_tensor(name, shape, F32).ap()

        acs_d, ea_d = dram("acs_d", [NH, SEQ]), dram("ea_d", [NH, SEQ])
        h2_d, y_d = dram("h2_d", [SEQ, D]), dram("y_d", [2 * SEQ, D])

        ps = ctx.enter_context(nc.psum_tensor("ps", [P, 8, 512], F32))

        def pair(b):
            return ps[:, b:b + 2, :].rearrange("p b n -> p (b n)")

        hT = sb("hT", [P, KT, SEQ])
        XBC = sb("XBC", [P, 16, SEQ])
        HR = sb("HR", [P, KT, SEQ])
        pv = sb("pv", [P, NPV])
        ident = sb("ident", [P, P])
        ones = sb("ones", [P, P])
        prep = sb("prep", [P, 4, 8])
        eps = sb("eps", [P, 2])
        stat = sb("stat", [P, 8, 16])
        scratch = sb("scratch", [P, 18944])

        def area(at, *dims):
            n = int(np.prod(dims))
            assert at + n <= 18944, (at, dims)
            t = scratch[:, at:at + n]
            if len(dims) == 2:
                return t.rearrange("p (a b) -> p a b", b=dims[1])
            if len(dims) == 3:
                return t.rearrange("p (a b c) -> p a b c", b=dims[1], c=dims[2])
            return t

        win = area(0, 3, KT * P)
        xall = area(3072, KT, D)
        xn = [area(11264, D), area(12288, D)]
        junk = area(13312, D)
        sv = {n: area(3072 + 1024 * k, D)[0:NH, :] for k, n in
              enumerate(["v", "nab", "e", "s", "s2", "p"])}
        DT, ACS, WD, EA = (area(9216 + 1024 * k, D)[0:NH, :] for k in range(4))
        smask = area(13312, D)[0:NH, :]
        wdt = area(14336, KT, NH)
        dd = area(14464, TT, NH)[0:NH]
        dec16 = area(14592, TT)[0:NH, :]
        hpar = area(14608, 2)[0:NH, :]
        lsp = area(14616, 6, 8)
        U, XE, XO = area(3072, D), area(4096, D), area(5120, D)
        TR, TI, AA, TG = (area(k, D) for k in (6144, 7168, 8192, 14720))
        A2 = area(15744, D)
        Q = area(16768, D)
        wblk = area(17792, 2, P)
        XC = area(3072, 12, P)
        L = [area(4608, NH, P), area(6656, NH, P)]
        EAB = area(8704, KT, P)
        XDT, XW = area(9728, D), area(10752, D)
        BT, SM = area(11776, NG, P), area(12288, NG, P)
        STATE, YT = area(12800, D), area(13824, D)
        G, SQ = area(14848, D), area(15872, D)
        ACCL = area(17000, D)
        tri = area(18024, P)
        colv = area(18152, 3, TT, NH)
        decb = area(18536, TT, NH)
        Z = [area(3072, D), area(4096, D)]
        ACCS = area(5120, D)
        WO_L, WO_S = XBC[:, 8:16, :], hT[:, :, :]
        X2 = area(6144, TT, D)
        XR = [area(0, D), area(1024, D)]
        H2 = [area(2048, D), area(3072, D)]
        H2T = area(4096, KT, P)
        wr = area(14336, KT, NR)
        LG = area(14624, TT, NR)
        nrow = area(14912, 2 * D + NR)
        cst = sb("cst", [P, 128 + 16 + 8 + 8 + 128])
        tab_f = sb("tab_f", [P, 2, NBLK])
        tab_i = sb("tab_i", [P, 2, NBLK], I32)
        iota, rowid1 = cst[:, 0:P], cst[:, P:P + 16]
        tokid, falling = cst[:, P + 16:P + 24], cst[:, P + 24:P + 32]
        above = cst[:, P + 32:2 * P + 32]
        over = sb("over", [P, 16])
        over_i = sb("over_i", [P, 16], I32)
        wts = sb("wts", [P, 2, TT])

        const_in, late_in = sem("const_in"), sem("late_in")
        x_in = [sem(f"x_in{t}") for t in range(TT)]
        act_step, dve_step, pool_step = sem("act_step"), sem("dve_step"), sem("pool_step")
        par_done = sem("par_done")
        dev_ready, inv_ready, xn_ready, xt_ready, ht_done = map(
            sem, ("dev_ready", "inv_ready", "xn_ready", "xt_ready", "ht_done"))
        dt_mm, dt_v, sp_arg, sp_exp, dt_ready, scr_out, dec_ready = map(
            sem, ("dt_mm", "dt_v", "sp_arg", "sp_exp", "dt_ready", "scr_out", "dec_ready"))
        w_in_sem = [sem(f"w_in{s}") for s in range(3)]
        wblk_in = sem("wblk_in")
        wc_in = [sem("wc_in0"), sem("wc_in1")]
        lru_mm, xe_mm, xo_mm, gt_mm = map(sem, ("lru_mm", "xe_mm", "xo_mm", "gt_mm"))
        tap_u, tap_e, tap_o, u_ready, cv_e, cv_o = map(
            sem, ("tap_u", "tap_e", "tap_o", "u_ready", "cv_e", "cv_o"))
        gate_act, a2_act, m2_ready, sq_act, lru_done, silu_e, silu_o = map(
            sem, ("gate_act", "a2_act", "m2_ready", "sq_act", "lru_done", "silu_e", "silu_o"))
        prep_mm, prep_done = sem("prep_mm"), sem("prep_done")
        xc_in, ea_in = sem("xc_in"), sem("ea_in")
        l_in = [sem("l_in0"), sem("l_in1")]
        ts_mm, st_mm, yo_mm = map(sem, ("ts_mm", "st_mm", "yo_mm"))
        y_mm, g_mm = [sem("y_mm0"), sem("y_mm1")], [sem("g_mm0"), sem("g_mm1")]
        xw_ready, sm_ready, diff_ready, min_ready, e_ready, m_ready, st_upd, comb = map(
            sem, ("xw_ready", "sm_ready", "diff_ready", "min_ready", "e_ready", "m_ready",
                  "st_upd", "comb"))
        bt_ready, g_act, lru_g, sql, accl, xd_ready, lru_w = map(
            sem, ("bt_ready", "g_act", "lru_g", "sql", "accl", "xd_ready", "lru_w"))
        z_in = [sem("z_in0"), sem("z_in1")]
        z_mm, z_act, zy = ([sem(f"{n}{p}") for p in range(2)] for n in ("z_mm", "z_act", "zy"))
        sqs, accs, ssd_w = sem("sqs"), sem("accs"), sem("ssd_w")
        wo_in = [sem("wo_in0"), sem("wo_in1")]
        xr_in = [sem("xr_in0"), sem("xr_in1")]
        ss_mm, devo, invo = sem("ss_mm"), sem("devo"), sem("invo")
        wol_mm, wos_mm, x2_l, x2_s = map(sem, ("wol_mm", "wos_mm", "x2_l", "x2_s"))
        dev2, inv2, h2_ready = sem("dev2"), sem("inv2"), sem("h2_ready")
        h2_out = [sem("h2_out0"), sem("h2_out1")]
        ht2_mm, ht2_act, lg_mm, lg_done = map(sem, ("ht2_mm", "ht2_act", "lg_mm", "lg_done"))

        rt = XBC[:, 8:16, :].rearrange("p a n -> p (a n)")
        at = [0]

        def route_tile(*dims):
            n = int(np.prod(dims))
            t = rt[:, at[0]:at[0] + n]
            at[0] += n
            if len(dims) == 2:
                return t.rearrange("p (a b) -> p a b", b=dims[1])
            if len(dims) == 3:
                return t.rearrange("p (a b c) -> p a b c", b=dims[1], c=dims[2])
            return t

        r_eq, r_pos, r_oh = (route_tile(TT, MG) for _ in range(3))
        r_fo = route_tile(TT, MG, EG)
        r_f, r_f2, r_eq8, r_pos8 = (route_tile(TT, EG) for _ in range(4))
        r_o = [route_tile(TT, EG) for _ in range(2)]
        r_cmax, r_pm, r_gw, r_w1, r_m1, r_m2 = (route_tile(TT) for _ in range(6))
        r_exp = route_tile(TT * (MG + 1))
        r_M = [route_tile(TT, NE) for _ in range(2)]
        r_sum, r_pre, r_tmp = (route_tile(TT, NE) for _ in range(3))
        r_tot, r_cnt, r_nov, r_oinc, r_ost = (route_tile(NE) for _ in range(5))
        r_rk, r_J, r_slot, r_os, r_eid, r_blk, r_g = (route_tile(2 * TT) for _ in range(7))
        r_A = route_tile(2 * TT, P)
        r_B = route_tile(2 * TT, 2, NBLK)
        r_ge = route_tile(16, NE)
        rt_arg, rt_exp, rk_in, rk_mm, ab_in, tab_mm, tab_ready = map(
            sem, ("rt_arg", "rt_exp", "rk_in", "rk_mm", "ab_in", "tab_mm", "tab_ready"))

        ring = [HR[:, j, :] if j < KT else XBC[:, j - KT, :] for j in range(CH)]
        XB, XT, YB = hT[:, 0, :], hT[:, 1, :], hT[:, 4, :]
        SG, HID, HIDT = hT[:, 2, 0:DE], hT[:, 2, DE:2 * DE], hT[:, 3, 0:DE]
        pad = sb("pad", [P, 2])
        idx_g, idx_s = sb("idx_g", [P, 1], I32), sb("idx_s", [P, 1], I32)
        wch_in = [sem(f"wch_in{j}") for j in range(CH)]
        ch_used, xb_in, xb_mm, xt_act, sg_act, hid_ready, hidt_mm, hidt_done, yb_act, y_out = map(
            sem, ("ch_used", "xb_in", "xb_mm", "xt_act", "sg_act", "hid_ready", "hidt_mm",
                  "hidt_done", "yb_act", "y_out"))
        YL = [XBC[:, 8 + 2 * p:10 + 2 * p, :] for p in range(2)]
        O = [XBC[:, 12 + p, :] for p in range(2)]
        yl_in = [sem("yl_in0"), sem("yl_in1")]
        x3_ready = [sem("x3_ready0"), sem("x3_ready1")]
        dev3, o_ready = sem("dev3"), sem("o_ready")
        out_done = [sem("out_done0"), sem("out_done1")]

        block = ctx.enter_context(nc.Block())

        def param(name, i, k=0):
            return pv[:, bass.ds(i + (PV[name] + k), 1)]

        @block.sync
        def _(sp):
            for t in range(TT):
                sp.dma_start(xall[:, t, :], a["x"][t]).then_inc(x_in[t], 16)
                if t == 1:
                    sp.dma_start(pv[:, :], a["pv"]).then_inc(const_in, 16)
                    sp.dma_start(ident[:, :], a["ident"]).then_inc(const_in, 16)
                    sp.dma_start(wdt, a["wdt"]).then_inc(const_in, 16)
                    sp.dma_start(hpar, a["hpar"]).then_inc(const_in, 16)

            def w_tile(slot, tile, signal):
                sp.dma_start(win[:, slot, :], a["win"][bass.ds(tile, 1)].rearrange(
                    "a p n -> p (a n)")).then_inc(signal, 16)

            with sp.Fori(0, 8) as i:
                sp.wait_ge(lru_mm, i)
                w_tile(0, i, w_in_sem[0])
                sp.wait_ge(xe_mm, i)
                w_tile(1, i * 2 + T_XBC, w_in_sem[1])
                sp.wait_ge(gt_mm, i * 2)
                sp.dma_start(wblk, a["wblk"][bass.ds(i, 1)].rearrange(
                    "a p g n -> p (a g) n")).then_inc(wblk_in, 16)
                sp.wait_ge(xo_mm, i)
                w_tile(2, i * 2 + (T_XBC + 1), w_in_sem[2])
            sp.dma_start(cst[:, :], a["cst"]).then_inc(late_in, 16)
            sp.wait_ge(lru_done, 8)
            sp.dma_start(tri, a["tri"]).then_inc(late_in, 16)
            sp.wait_ge(silu_e, 8)
            sp.wait_ge(silu_o, 8)
            sp.wait_ge(xo_mm, 8)
            sp.wait_ge(prep_done, 2)
            sp.wait_ge(scr_out, 32)
            with sp.Fori(0, 4) as i:
                for p in range(2):
                    c = i * 2 + p
                    sp.wait_ge(g_mm[p], i)
                    w_tile(p, c + T_GATE, wc_in[p])
                    sp.wait_ge(ts_mm, c)
                    sp.dma_start(XC, XBC[:, 0:12, bass.ds(c * P, P)]).then_inc(xc_in, 16)
                    sp.wait_ge(y_mm[p], i)
                    sp.dma_start(L[p], acs_d[:, bass.ds(c * P, P)].partition_broadcast(P)
                                 ).then_inc(l_in[p], 16)
                    sp.wait_ge(comb, c)
                    for q in range(2):
                        sp.dma_start(EAB[HD * q:HD * (q + 1)], ea_d.rearrange(
                            "(j q) s -> q j s", q=2)[q][:, bass.ds(c * P, P)
                            ].partition_broadcast(HD)).then_inc(ea_in, 16)
            sp.wait_ge(yo_mm, 8)
            sp.wait_ge(g_mm[0], 4)
            sp.wait_ge(g_mm[1], 4)
            sp.wait_ge(comb, 8)
            with sp.Fori(0, 4) as i:
                for p in range(2):
                    sp.wait_ge(z_mm[p], i)
                    w_tile(p, i * 2 + (T_Z + p), z_in[p])
            sp.dma_start(WO_L, a["wout"][:, 0:8, :]).then_inc(wo_in[0], 16)
            sp.wait_ge(z_mm[0], 4)
            sp.wait_ge(z_mm[1], 4)
            sp.dma_start(WO_S, a["wout"][:, 8:16, :]).then_inc(wo_in[1], 16)
            sp.wait_ge(accs, 8)
            sp.dma_start(wr, a["wr"]).then_inc(late_in, 16)
            sp.dma_start(nrow, a["nrow"].partition_broadcast(P)).then_inc(late_in, 16)
            for t in range(TT):
                if t >= 2:
                    sp.wait_ge(x2_l, t - 1)
                sp.dma_start(XR[t % 2], a["x"][t]).then_inc(xr_in[t % 2], 16)
                if t >= 1:
                    sp.wait_ge(h2_ready, t)
                    sp.dma_start(h2_d[P * (t - 1):P * t, :], H2[(t - 1) % 2]).then_inc(
                        h2_out[(t - 1) % 2], 16)
            sp.wait_ge(h2_ready, TT)
            sp.dma_start(h2_d[P * (TT - 1):, :], H2[(TT - 1) % 2]).then_inc(
                h2_out[(TT - 1) % 2], 16)
            sp.wait_ge(wol_mm, TT)
            sp.wait_ge(wos_mm, TT)

            def chunk(j, e):
                sp.dma_start(ring[j], a["moe"][bass.ds(e * CH + j, 1)].rearrange(
                    "a p n -> p (a n)")).then_inc(wch_in[j], 16)

            for j in range(CH):
                sp.dma_start(ring[j], a["moe"][j]).then_inc(wch_in[j], 16)
            with sp.Fori(1, NE) as e:
                for j in range(CH):
                    sp.wait_ge(ch_used, e * CH + (j + 1 - CH))
                    chunk(j, e)
            sp.wait_ge(tab_ready, 1)
            n_over = sp.value_load(over_i[0:1, 15:16], min_val=0, max_val=MAX_OVER)
            with sp.Fori(0, MAX_OVER) as o:
                with sp.If(n_over > o):
                    e = sp.value_load(over_i[0:1, bass.ds(o, 1)], min_val=0, max_val=NE - 1)
                    for j in range(CH):
                        sp.wait_ge(ch_used, o * CH + ((NE - 1) * CH + j + 1))
                        chunk(j, e)
            with sp.Fori(0, TT // 2) as i:
                for p in range(2):
                    sp.wait_ge(y_out, n_over * 16 + NE * 16)
                    sp.wait_ge(x3_ready[p], i)
                    sp.dma_start(YL[p], y_d.rearrange("(t p k) d -> t p k d", p=P, k=2)[
                        bass.ds(i * 2 + p, 1)].rearrange("a p k d -> p (a k) d")
                        ).then_inc(yl_in[p], 16)
            sp.wait_ge(out_done[0], 16 * TT // 2)
            sp.wait_ge(out_done[1], 16 * TT // 2)

        @block.tensor
        def _(pe):
            def project(slot, bank, signal):
                for h in range(2):
                    mm = project_half(slot, bank, h)
                mm.then_inc(signal, 1)

            def project_half(slot, bank, h):
                for k in range(KT):
                    mm = pe.matmul(ps[:, bank + h, :], win[:, slot, k * P:(k + 1) * P],
                                   hT[:, k, h * 512:(h + 1) * 512], start=(k == 0),
                                   stop=(k == KT - 1))
                return mm

            pe.wait_ge(const_in, 64)
            for t in range(TT):
                if t >= 2:
                    pe.wait_ge(ht_done, 2 * (t - 1))
                pe.wait_ge(xn_ready, t + 1)
                for k in range(KT):
                    mm = pe.transpose(ps[:, 2 * (t % 2) + k // 4, (k % 4) * P:(k % 4 + 1) * P],
                                      xn[t % 2][:, k * P:(k + 1) * P], ident[:, :])
                mm.then_inc(xt_ready, 1)
            pe.wait_ge(ht_done, 2 * TT)
            for h in range(2):
                for k in range(KT):
                    mm = pe.matmul(ps[0:NH, 4 + h, :], wdt[:, k, :],
                                   hT[:, k, h * 512:(h + 1) * 512], start=(k == 0),
                                   stop=(k == KT - 1))
            mm.then_inc(dt_mm, 1)
            pe.wait_ge(dt_v, 1)
            with pe.Fori(0, 8) as i:
                pe.wait_ge(w_in_sem[0], i * 16 + 16)
                pe.wait_ge(gate_act, i * 2)
                project(0, 4, lru_mm)
                pe.wait_ge(w_in_sem[1], i * 16 + 16)
                pe.wait_ge(cv_e, i)
                project(1, 0, xe_mm)
                pe.wait_ge(u_ready, i + 1)
                pe.wait_ge(wblk_in, i * 16 + 16)
                for g in range(2):
                    for h in range(2):
                        mm = pe.matmul(ps[:, 6 - 2 * g + h, :], wblk[:, g, :],
                                       U[:, h * 512:(h + 1) * 512], start=True, stop=True)
                    mm.then_inc(gt_mm, 1)
                pe.wait_ge(w_in_sem[2], i * 16 + 16)
                pe.wait_ge(cv_o, i)
                project(2, 2, xo_mm)
            pe.wait_ge(dt_ready, 1)
            pe.wait_ge(cv_e, 8)
            for q, rows in enumerate((ACS, DT, WD)):
                for c in range(TT):
                    at = (q * TT + c) * NH
                    mm = pe.transpose(ps[:, 0, at:at + NH], rows[:, c * P:(c + 1) * P],
                                      ident[0:NH, 0:NH])
            mm.then_inc(prep_mm, 1)
            pe.matmul(ps[:, 1, 0:TT * NH], ones[0:NH, :], dd.rearrange("h c k -> h (c k)"),
                      start=True, stop=True).then_inc(prep_mm, 1)
            pe.wait_ge(prep_done, 2)
            pe.wait_ge(cv_o, 8)
            pe.wait_ge(gate_act, 16)
            with pe.Fori(0, 4) as i:
                for p in range(2):
                    c = i * 2 + p
                    pe.wait_ge(xc_in, c * 16 + 16)
                    pe.wait_ge(comb, c)
                    for k in range(KT):
                        pe.transpose(ps[:, 2 + k // 4, (k % 4) * P:(k % 4 + 1) * P],
                                     XC[:, k, :], ident[:, :])
                    for g in range(NG):
                        pe.transpose(ps[:, 4, g * P:(g + 1) * P], XC[:, KT + g, :], ident[:, :])
                    for g in range(NG):
                        mm = pe.matmul(ps[:, 5, g * P:(g + 1) * P], XC[:, KT + g, :],
                                       XBC[:, 12 + g, bass.ds(c * P, P)], start=True, stop=True)
                    mm.then_inc(ts_mm, 1)
                    pe.wait_ge(wc_in[p], i * 16 + 16)
                    pe.wait_ge(g_act, c)
                    project_half(p, 0, 0)
                    pe.wait_ge(xw_ready, c + 1)
                    pe.wait_ge(bt_ready, c + 1)
                    pe.wait_ge(st_upd, c)
                    for g in range(NG):
                        mm = pe.matmul(ps[:, 6 + g // 2, (g % 2) * 256:(g % 2 + 1) * 256],
                                       BT[:, g, :], XW[:, g * 256:(g + 1) * 256],
                                       start=True, stop=True)
                    mm.then_inc(st_mm, 1)
                    pe.wait_ge(sm_ready, c + 1)
                    for j in range(KT):
                        mm = pe.matmul(ps[:, 4 + j // 4, (j % 4) * P:(j % 4 + 1) * P],
                                       STATE[:, j * P:(j + 1) * P],
                                       XBC[:, 12 + j // 2, bass.ds(c * P, P)],
                                       start=True, stop=True)
                    mm.then_inc(yo_mm, 1)
                    pe.wait_ge(m_ready, c + 1)
                    for h in range(NH):
                        j, q = h // 2, h % 2
                        mm = pe.matmul(ps[HD * q:HD * (q + 1), 2 + j // 4,
                                          (j % 4) * P:(j % 4 + 1) * P],
                                       XDT[:, h * HD:(h + 1) * HD], L[p][:, h, :],
                                       start=True, stop=True)
                    mm.then_inc(y_mm[p], 1)
                    project_half(p, 0, 1).then_inc(g_mm[p], 1)
            pe.wait_ge(g_act, 8)
            pe.wait_ge(comb, 8)
            with pe.Fori(0, 4) as i:
                for p in range(2):
                    pe.wait_ge(z_in[p], i * 16 + 16)
                    pe.wait_ge(z_act[p], i)
                    project(p, 2 * p, z_mm[p])
            pe.wait_ge(accl, 8)
            pe.wait_ge(accs, 8)
            for r, acc in enumerate((ACCL, ACCS)):
                for t in range(TT):
                    mm = pe.matmul(ps[:, 6, r * TT + t:r * TT + t + 1],
                                   acc[:, t * P:(t + 1) * P], ones[:, 0:1],
                                   start=True, stop=True)
            mm.then_inc(ss_mm, 1)
            pe.wait_ge(lru_w, 8)
            pe.wait_ge(ssd_w, 8)
            pe.wait_ge(z_act[0], 4)
            pe.wait_ge(z_act[1], 4)
            pe.wait_ge(devo, 1)
            pe.wait_ge(late_in, 64)

            def out_half(t, bank, y, w, signal):
                for h in range(2):
                    for k in range(KT):
                        mm = pe.matmul(ps[:, bank + h, :], y[:, k, t * P:(t + 1) * P],
                                       w[:, k, h * 512:(h + 1) * 512], start=(k == 0),
                                       stop=(k == KT - 1))
                mm.then_inc(signal, 1)

            def turn_h2(t):
                pe.wait_ge(h2_ready, t + 1)
                if t >= 1:
                    pe.wait_ge(ht2_act, t)
                for k in range(KT):
                    mm = pe.transpose(ps[:, 4 + k // 4, (k % 4) * P:(k % 4 + 1) * P],
                                      H2[t % 2][:, k * P:(k + 1) * P], ident[:, :])
                mm.then_inc(ht2_mm, 1)

            def route(t):
                pe.wait_ge(ht2_act, t + 1)
                if t >= 1:
                    pe.wait_ge(lg_done, t)
                for k in range(KT):
                    mm = pe.matmul(ps[:, 6, 0:NR], H2T[:, k, :], wr[:, k, :],
                                   start=(k == 0), stop=(k == KT - 1))
                mm.then_inc(lg_mm, 1)

            pe.wait_ge(wo_in[0], 16)
            for t in range(TT):
                if t >= 1:
                    pe.wait_ge(x2_l, t)
                out_half(t, 0, HR, WO_L, wol_mm)
                if t >= 1:
                    turn_h2(t - 1)
                if t == 0:
                    pe.wait_ge(wo_in[1], 16)
                else:
                    pe.wait_ge(x2_s, t)
                out_half(t, 2, XBC, WO_S, wos_mm)
                if t >= 1:
                    route(t - 1)
            turn_h2(TT - 1)
            route(TT - 1)
            pe.wait_ge(lg_done, TT)
            pe.wait_ge(rk_in, 1)
            flat = lambda t: t.rearrange("p a b -> p (a b)")
            pe.matmul(ps[:, 7, 0:TT * NE], above, flat(r_sum), start=True, stop=False)
            pe.matmul(ps[:, 7, 0:TT * NE], ones[:, :], flat(r_pre), start=False, stop=True)
            pe.matmul(ps[:, 7, TT * NE:TT * NE + NE], ones[:, :], r_tot, start=True,
                      stop=True).then_inc(rk_mm, 1)
            pe.wait_ge(ab_in, 1)
            for n in range(2 * TT):
                mm = pe.matmul(ps[:, 7, 0:2 * NBLK], r_A[:, n, :],
                               r_B[:, n, :, :].rearrange("p a b -> p (a b)"),
                               start=(n == 0), stop=(n == 2 * TT - 1))
            mm.then_inc(tab_mm, 1)

            def turn_rows(count):
                pe.wait_ge(xb_in, count * 16)
                for k in range(KT):
                    mm = pe.transpose(ps[:, 2 + k // 4, (k % 4) * P:(k % 4 + 1) * P],
                                      XB[:, k * P:(k + 1) * P], ident[:, :])
                mm.then_inc(xb_mm, 1)

            def block_products(b):
                pe.wait_ge(xt_act, b + 1)
                pe.wait_ge(hid_ready, b)
                for k in range(KT):
                    pe.wait_ge(wch_in[k], b * 16 + 16)
                    for h in range(2):
                        mm = pe.matmul(ps[:, h, :], XT[:, k * P:(k + 1) * P],
                                       ring[k][:, h * DE:(h + 1) * DE], start=(k == 0),
                                       stop=(k == KT - 1))
                    mm.then_inc(ch_used, 1)
                turn_rows(b + 2)
                pe.wait_ge(hid_ready, b + 1)
                for k in range(DE // P):
                    mm = pe.transpose(ps[:, 4, k * P:(k + 1) * P], HID[:, k * P:(k + 1) * P],
                                      ident[:, :])
                mm.then_inc(hidt_mm, 1)
                pe.wait_ge(hidt_done, b + 1)
                pe.wait_ge(yb_act, b)
                for k in range(DE // P):
                    pe.wait_ge(wch_in[KT + k], b * 16 + 16)
                    for h in range(2):
                        mm = pe.matmul(ps[:, 5 + h, :], HIDT[:, k * P:(k + 1) * P],
                                       ring[KT + k][:, h * 512:(h + 1) * 512],
                                       start=(k == 0), stop=(k == DE // P - 1))
                    mm.then_inc(ch_used, 1)

            turn_rows(1)
            with pe.Fori(0, NE) as b:
                block_products(b)
            n_over = pe.value_load(over_i[0:1, 15:16], min_val=0, max_val=MAX_OVER)
            with pe.Fori(0, MAX_OVER) as o:
                with pe.If(n_over > o):
                    block_products(o + NE)

        @block.scalar
        def _(act):
            st = Steps(act, act_step)
            act.wait_ge(par_done, 1)
            for t in range(TT):
                act.wait_ge(x_in[t], 16)
                st.link(act.activation(junk, xall[:, t, :], ACT.Square,
                                       accum_out=stat[:, 0, t:t + 1]))
                link(act, act.activation(stat[:, 1, t:t + 1], stat[:, 0, t:t + 1], ACT.Sqrt,
                                         bias=eps[:, 0:1], scale=1.0 / D), dev_ready, t + 1)
                act.wait_ge(inv_ready, t + 1)
                if t >= 2:
                    act.wait_ge(xt_ready, t - 1)
                link(act, act.activation(xn[t % 2], xall[:, t, :], ACT.Copy,
                                         scale=stat[:, 2, t:t + 1]), xn_ready, t + 1)
            act.wait_ge(const_in, 64)
            act.wait_ge(dt_mm, 1)
            link(act, act.activation(sv["v"], pair(4)[0:NH, :], ACT.Identity,
                                     bias=hpar[:, 0:1]), dt_v, 1)
            act.wait_ge(sp_arg, 1)
            link(act, act.activation(lsp[:, 2, :], lsp[:, 1, :], ACT.Exp), sp_exp, 1)
            st.link(act.activation(hpar[:, 1:2], hpar[:, 1:2], ACT.Exp))
            act.wait_ge(sp_arg, 2)
            link(act, act.activation(sv["e"], sv["nab"], ACT.Exp), sp_exp, 2)
            act.wait_ge(sp_arg, 3)
            link(act, act.activation(WD, sv["p"], ACT.Exp), sp_exp, 3)
            link(act, act.activation(EA, ACS, ACT.Exp), sp_exp, 4)
            link(act, act.activation(dec16, ACS.rearrange("h (c l) -> h c l", l=P)[:, :, P - 1],
                                     ACT.Exp), sp_exp, 5)
            act.wait_ge(dt_ready, 1)
            with act.Fori(0, 8) as i:
                st.begin(i, 2)
                act.wait_ge(lru_mm, i + 1)
                act.wait_ge(gt_mm, i * 2)
                act.wait_ge(lru_done, i)
                link(act, act.activation(U, pair(4), ACT.Identity, bias=param("lru_cb", i),
                                         scale=param("lru_cw", i, 24)), tap_u, i + 1)
                act.wait_ge(xe_mm, i + 1)
                link(act, act.activation(XE, pair(0), ACT.Identity,
                                         bias=param("ssd_cb", i * 2),
                                         scale=param("ssd_cw", i * 2, 48)), tap_e, i + 1)
                act.wait_ge(cv_e, i + 1)
                link(act, act.activation(XBC[:, bass.ds(i * 2, 1), :].rearrange(
                    "p a n -> p (a n)"), XE, ACT.Silu), silu_e, i + 1)
                act.wait_ge(gt_mm, i * 2 + 1)
                link(act, act.activation(TR, pair(6), ACT.Tanh,
                                         bias=prep[:, 0, bass.ds(i, 1)], scale=0.5),
                     gate_act, i * 2 + 1)
                act.wait_ge(gt_mm, i * 2 + 2)
                link(act, act.activation(TI, pair(4), ACT.Tanh,
                                         bias=prep[:, 1, bass.ds(i, 1)], scale=0.5),
                     gate_act, i * 2 + 2)
                st.link(act.activation(AA, TR, ACT.Exp, bias=prep[:, 2, bass.ds(i, 1)],
                                       scale=prep[:, 2, bass.ds(i, 1)]))
                st.link(act.activation(TG, TR, ACT.Tanh, bias=prep[:, 3, bass.ds(i, 1)],
                                       scale=prep[:, 3, bass.ds(i, 1)]))
                link(act, act.activation(A2, AA, ACT.Square), a2_act, i + 1)
                act.wait_ge(m2_ready, i + 1)
                link(act, act.activation(A2, A2, ACT.Sqrt, bias=eps[:, 1:2]), sq_act, i + 1)
                act.wait_ge(xo_mm, i + 1)
                link(act, act.activation(XO, pair(2), ACT.Identity,
                                         bias=param("ssd_cb", i * 2, 1),
                                         scale=param("ssd_cw", i * 2, 49)), tap_o, i + 1)
                act.wait_ge(cv_o, i + 1)
                link(act, act.activation(XBC[:, bass.ds(i * 2 + 1, 1), :].rearrange(
                    "p a n -> p (a n)"), XO, ACT.Silu), silu_o, i + 1)
            st.end(8)
            with act.Fori(0, 4) as i:
                for p in range(2):
                    c = i * 2 + p
                    act.wait_ge(ts_mm, c + 1)
                    act.wait_ge(st_mm, c)
                    link(act, act.activation(BT.rearrange("p g n -> p (g n)"), ps[:, 4, :],
                                             ACT.Copy), bt_ready, c + 1)
                    act.wait_ge(min_ready, c + 1)
                    link(act, act.activation(L[p], L[p], ACT.Exp), e_ready, c + 1)
                    act.wait_ge(g_mm[p], i + 1)
                    act.wait_ge(lru_g, c)
                    link(act, act.activation(G, pair(0), ACT.Gelu_apprx_tanh), g_act, c + 1)
                    act.wait_ge(lru_g, c + 1)
                    act.wait_ge(accl, c)
                    y = HR[:, bass.ds(c, 1), :].rearrange("p a n -> p (a n)")
                    link(act, act.activation(SQ, y, ACT.Square), sql, c + 1)
                    link(act, act.activation(y, y, ACT.Copy, scale=param("lru_norm", c)),
                         lru_w, c + 1)
            act.wait_ge(accl, 8)
            with act.Fori(0, 4) as i:
                for p in range(2):
                    j = i * 2 + p
                    act.wait_ge(z_mm[p], i + 1)
                    act.wait_ge(zy[p], i)
                    link(act, act.activation(Z[p], pair(2 * p), ACT.Silu), z_act[p], i + 1)
                    act.wait_ge(zy[p], i + 1)
                    act.wait_ge(accs, j)
                    y = XBC[:, bass.ds(j, 1), :].rearrange("p a n -> p (a n)")
                    link(act, act.activation(SQ, y, ACT.Square), sqs, j + 1)
                    link(act, act.activation(y, y, ACT.Copy, scale=param("ssd_norm", j)),
                         ssd_w, j + 1)
            act.wait_ge(ss_mm, 1)
            link(act, act.activation(stat[:, 3, :], ps[:, 6, 0:2 * TT], ACT.Sqrt,
                                     bias=eps[:, 0:1], scale=1.0 / D), devo, 1)
            for t in range(TT):
                act.wait_ge(x2_s, t + 1)
                if t >= 1:
                    act.wait_ge(h2_ready, t)
                st.link(act.activation(ACCS, X2[:, t, :], ACT.Square,
                                       accum_out=stat[:, 0, t:t + 1]))
                link(act, act.activation(stat[:, 1, t:t + 1], stat[:, 0, t:t + 1], ACT.Sqrt,
                                         bias=eps[:, 0:1], scale=1.0 / D), dev2, t + 1)
                act.wait_ge(ht2_mm, t + 1)
                if t >= 1:
                    act.wait_ge(lg_mm, t)
                link(act, act.activation(H2T.rearrange("p k n -> p (k n)"), pair(4), ACT.Copy),
                     ht2_act, t + 1)
            act.wait_ge(rt_arg, 1)
            link(act, act.activation(r_exp, r_exp, ACT.Exp), rt_exp, 1)

            def block_functions(b):
                act.wait_ge(ch_used, b * CH + KT)
                act.wait_ge(hid_ready, b)
                link(act, act.activation(SG, ps[:, 0, :], ACT.Silu), sg_act, b + 1)
                act.wait_ge(xb_mm, b + 2)
                link(act, act.activation(XT, pair(2), ACT.Copy), xt_act, b + 2)
                act.wait_ge(ch_used, b * CH + CH)
                act.wait_ge(y_out, b * 16)
                act.activation(YB, pair(5), ACT.Copy).then_inc(yb_act, 1)

            act.wait_ge(xb_mm, 1)
            link(act, act.activation(XT, pair(2), ACT.Copy), xt_act, 1)
            with act.Fori(0, NE) as b:
                block_functions(b)
            n_over = act.value_load(over_i[0:1, 15:16], min_val=0, max_val=MAX_OVER)
            with act.Fori(0, MAX_OVER) as o:
                with act.If(n_over > o):
                    block_functions(o + NE)
            with act.Fori(0, TT // 2) as i:
                st.begin(i, 2)
                for p in range(2):
                    t = i * 2 + p
                    act.wait_ge(x3_ready[p], i + 1)
                    st.link(act.activation(ACCS, X2[:, bass.ds(t, 1), :].rearrange(
                        "p a n -> p (a n)"), ACT.Square, accum_out=stat[:, 4, p:p + 1]))
                    act.wait_ge(o_ready, t)
                    link(act, act.activation(stat[:, 5, p:p + 1], stat[:, 4, p:p + 1], ACT.Sqrt,
                                             bias=eps[:, 0:1], scale=1.0 / D), dev3, t + 1)
                    act.wait_ge(o_ready, t + 1)
                    act.dma_start(a["out"][bass.ds(t, 1)].rearrange("a p n -> p (a n)"),
                                  O[p]).then_inc(out_done[p], 16)
            st.end(TT // 2)

        @block.vector
        def _(dve):
            st = Steps(dve, dve_step)
            st.link(dve.memset(eps[:, 0:1], EPS))
            dve.memset(eps[:, 1:2], 1e-30).then_inc(par_done, 1)
            st.link(dve.memset(ones[:, :], 1.0))
            for t in range(TT):
                dve.wait_ge(dev_ready, t + 1)
                link(dve, dve.reciprocal(stat[:, 2, t:t + 1], stat[:, 1, t:t + 1]),
                     inv_ready, t + 1)
                if t == 0:
                    dve.wait_ge(const_in, 64)
                dve.wait_ge(xt_ready, t + 1)
                for j in range(2):
                    dve.tensor_tensor(
                        hT[:, 4 * j:4 * j + 4, t * P:(t + 1) * P],
                        ps[:, 2 * (t % 2) + j, :].rearrange("p (k n) -> p k n", n=P),
                        pv[:, PV["norm_mix"] + 4 * j:PV["norm_mix"] + 4 * j + 4].unsqueeze(2)
                        .to_broadcast([P, 4, P]), ALU.mult).then_inc(ht_done, 1)

            def softplus_tail(v, e, s, s2, p, out):
                st.link(dve.tensor_scalar(s, e, 2.0, None, ALU.add))
                st.link(dve.reciprocal(s, s))
                st.link(dve.tensor_tensor(s, s, e, ALU.mult))
                st.link(dve.tensor_tensor(s2, s, s, ALU.mult))
                st.link(dve.tensor_scalar(p, s2, 1.0 / 15, None, ALU.mult))
                for n in (13, 11, 9, 7, 5, 3):
                    st.link(dve.scalar_tensor_tensor(p, p, 1.0 / n, s2, ALU.add, ALU.mult))
                st.link(dve.scalar_tensor_tensor(p, p, 1.0, s, ALU.add, ALU.mult))
                st.link(dve.tensor_scalar(p, p, 2.0, None, ALU.mult))
                st.link(dve.scalar_tensor_tensor(out, v, 0.0, p, ALU.max, ALU.add))

            cols = lambda name: pv[:, PV[name]:PV[name] + 8]
            st.link(dve.tensor_scalar(prep[:, 0, :], cols("lru_ba"), 0.5, None, ALU.mult))
            st.link(dve.tensor_scalar(prep[:, 1, :], cols("lru_bx"), 0.5, None, ALU.mult))
            dve.wait_ge(xn_ready, TT)
            st.link(dve.tensor_scalar(lsp[:, 0, :], cols("lam"), -1.0, None, ALU.mult))
            link(dve, dve.scalar_tensor_tensor(lsp[:, 1, :], lsp[:, 0, :], -1.0, lsp[:, 0, :],
                                               ALU.mult, ALU.min), sp_arg, 1)
            dve.wait_ge(sp_exp, 1)
            softplus_tail(*(lsp[:, k, :] for k in (0, 2, 3, 4, 5)), prep[:, 2, :])
            st.link(dve.tensor_scalar(prep[:, 3, :], prep[:, 2, :], 4.0, None, ALU.mult))
            st.link(dve.tensor_scalar(prep[:, 2, :], prep[:, 2, :], -4.0, None, ALU.mult))
            st.link(dve.memset(smask, 1.0))
            st.link(dve.memset(smask.rearrange("h (c l) -> h c l", l=P)[:, :, 0], 0.0))
            dve.wait_ge(dt_v, 1)
            link(dve, dve.scalar_tensor_tensor(sv["nab"], sv["v"], -1.0, sv["v"],
                                               ALU.mult, ALU.min), sp_arg, 2)
            dve.wait_ge(sp_exp, 2)
            softplus_tail(*(sv[n] for n in ("v", "e", "s", "s2", "p")), DT)
            st.link(dve.tensor_scalar(sv["s"], DT, hpar[:, 1:2], -1.0, ALU.mult, ALU.mult))
            st.link(dve.tensor_tensor_scan(ACS, smask, sv["s"], 0.0, ALU.mult, ALU.add))
            acs3 = ACS.rearrange("h (c l) -> h c l", l=P)
            link(dve, dve.tensor_tensor(sv["p"].rearrange("h (c l) -> h c l", l=P),
                                        acs3[:, :, P - 1:P].to_broadcast([NH, TT, P]), acs3,
                                        ALU.subtract), sp_arg, 3)
            dve.wait_ge(sp_exp, 5)
            st.link(dve.tensor_tensor(WD, WD, DT, ALU.mult))
            link(dve, dve.tensor_tensor(
                dd, ident[0:NH, 0:NH].unsqueeze(1).to_broadcast([NH, TT, NH]),
                dec16.unsqueeze(2).to_broadcast([NH, TT, NH]), ALU.mult), dt_ready, 1)

            def taps(acc, bank, name, i, stride, last_sem, count, col=0):
                for back in (1, 2, 3):
                    w = param(name, i, stride * (3 - back) + col)
                    ins = dve.scalar_tensor_tensor(
                        acc[:, back:], pair(bank)[:, 0:SEQ - back], w, acc[:, back:],
                        ALU.mult, ALU.add)
                    if back < 3:
                        st.link(ins)
                    else:
                        link(dve, ins, last_sem, count)

            with dve.Fori(0, 8) as i:
                st.begin(i, 8)
                dve.wait_ge(tap_u, i + 1)
                taps(U, 4, "lru_cw", i, 8, u_ready, i + 1)
                dve.wait_ge(tap_e, i + 1)
                taps(XE, 0, "ssd_cw", i * 2, 16, cv_e, i + 1)
                dve.wait_ge(a2_act, i + 1)
                link(dve, dve.scalar_tensor_tensor(A2, A2, 1.0, TG, ALU.add, ALU.mult),
                     m2_ready, i + 1)
                st.link(dve.scalar_tensor_tensor(Q, TI, 1.0, U, ALU.add, ALU.mult))
                dve.wait_ge(sq_act, i + 1)
                st.link(dve.scalar_tensor_tensor(Q, Q, 0.5, A2, ALU.mult, ALU.mult))
                link(dve, dve.tensor_tensor_scan(
                    HR[:, bass.ds(i, 1), :].rearrange("p a n -> p (a n)"), AA, Q, 0.0,
                    ALU.mult, ALU.add), lru_done, i + 1)
                dve.wait_ge(tap_o, i + 1)
                taps(XO, 2, "ssd_cw", i * 2, 16, cv_o, i + 1, 1)
            st.end(8)
            dve.wait_ge(prep_mm, 1)
            link(dve, dve.tensor_copy(colv.rearrange("p q c h -> p (q c h)"),
                                      ps[:, 0, 0:3 * TT * NH]), prep_done, 1)
            dve.wait_ge(prep_mm, 2)
            link(dve, dve.tensor_copy(decb.rearrange("p c h -> p (c h)"),
                                      ps[:, 1, 0:TT * NH]), prep_done, 2)
            dve.wait_ge(sq_act, 8)
            dve.wait_ge(gt_mm, 16)
            dve.wait_ge(scr_out, 32)
            st.link(dve.memset(STATE, 0.0))
            dve.wait_ge(late_in, 32)
            s3 = lambda t, n=P: t.rearrange("p (a n) -> p a n", n=n)
            with dve.Fori(0, 4) as i:
                st.begin(i, 8)
                for p in range(2):
                    c = i * 2 + p
                    col = lambda q: colv[:, q, bass.ds(c, 1), :].rearrange(
                        "p a h -> p (a h)").unsqueeze(2).to_broadcast([P, NH, HD])
                    dve.wait_ge(ts_mm, c + 1)
                    dve.wait_ge(y_mm[1 - p], i + p)
                    dve.wait_ge(st_mm, c)
                    st.link(dve.tensor_tensor(s3(XDT, HD), s3(pair(2), HD), col(1), ALU.mult))
                    link(dve, dve.tensor_tensor(s3(XW, HD), s3(pair(2), HD), col(2), ALU.mult),
                         xw_ready, c + 1)
                    link(dve, dve.tensor_tensor(SM, s3(ps[:, 5, :]), tri.unsqueeze(1)
                                                .to_broadcast([P, NG, P]), ALU.mult),
                         sm_ready, c + 1)
                    dve.wait_ge(diff_ready, c + 1)
                    link(dve, dve.tensor_scalar(L[p], L[p], 0.0, None, ALU.min),
                         min_ready, c + 1)
                    dve.wait_ge(e_ready, c + 1)
                    link(dve, dve.tensor_tensor(
                        L[p].rearrange("p (g k) l -> p g k l", g=NG),
                        L[p].rearrange("p (g k) l -> p g k l", g=NG),
                        SM.unsqueeze(2).to_broadcast([P, NG, NG, P]), ALU.mult),
                        m_ready, c + 1)
                    dve.wait_ge(yo_mm, c + 1)
                    st.link(dve.tensor_tensor(s3(STATE, HD), s3(STATE, HD),
                                              decb[:, bass.ds(c, 1), :].rearrange(
                                                  "p a h -> p (a h)").unsqueeze(2)
                                              .to_broadcast([P, NH, HD]), ALU.mult))
                    dve.wait_ge(st_mm, c + 1)
                    link(dve, dve.tensor_tensor(STATE, STATE, pair(6), ALU.add), st_upd, c + 1)
                    dve.wait_ge(ea_in, c * 32 + 32)
                    st.link(dve.tensor_tensor(s3(YT), s3(pair(4)), EAB, ALU.mult))
                    dve.wait_ge(y_mm[p], i + 1)
                    st.link(dve.tensor_tensor(YT, YT, pair(2), ALU.add))
                    dve.wait_ge(xd_ready, c + 1)
                    y = XBC[:, 0:KT, bass.ds(c * P, P)]
                    link(dve, dve.tensor_tensor(y, y, s3(YT), ALU.add), comb, c + 1)
                    dve.wait_ge(g_act, c + 1)
                    y = HR[:, bass.ds(c, 1), :].rearrange("p a n -> p (a n)")
                    link(dve, dve.tensor_tensor(y, y, G, ALU.mult), lru_g, c + 1)
            st.end(4)
            with dve.Fori(0, 4) as i:
                for p in range(2):
                    dve.wait_ge(z_act[p], i + 1)
                    y = XBC[:, bass.ds(i * 2 + p, 1), :].rearrange("p a n -> p (a n)")
                    link(dve, dve.tensor_tensor(y, y, Z[p], ALU.mult), zy[p], i + 1)

            def logits(t):
                dve.wait_ge(lg_mm, t + 1)
                link(dve, dve.tensor_tensor(LG[:, t, :], ps[:, 6, 0:NR], nrow[:, 2 * D:],
                                            ALU.add), lg_done, t + 1)

            dve.wait_ge(late_in, 64)
            dve.wait_ge(devo, 1)
            link(dve, dve.reciprocal(stat[:, 4, :], stat[:, 3, :]), invo, 1)
            for t in range(TT):
                dve.wait_ge(wol_mm, t + 1)
                dve.wait_ge(xr_in[t % 2], 16 * (t // 2 + 1))
                link(dve, dve.scalar_tensor_tensor(X2[:, t, :], pair(0), stat[:, 4, t:t + 1],
                                                   XR[t % 2], ALU.mult, ALU.add), x2_l, t + 1)
                dve.wait_ge(wos_mm, t + 1)
                link(dve, dve.scalar_tensor_tensor(X2[:, t, :], pair(2),
                                                   stat[:, 4, TT + t:TT + t + 1],
                                                   X2[:, t, :], ALU.mult, ALU.add), x2_s, t + 1)
                dve.wait_ge(dev2, t + 1)
                st.link(dve.reciprocal(stat[:, 2, t:t + 1], stat[:, 1, t:t + 1]))
                if t >= 2:
                    dve.wait_ge(h2_out[t % 2], 16 * (t // 2))
                    dve.wait_ge(ht2_mm, t - 1)
                link(dve, dve.scalar_tensor_tensor(H2[t % 2], X2[:, t, :], stat[:, 2, t:t + 1],
                                                   nrow[:, 0:D], ALU.mult, ALU.mult),
                     h2_ready, t + 1)
                if t >= 1:
                    logits(t - 1)
            logits(TT - 1)
            b3 = lambda t, w: t.unsqueeze(2).to_broadcast([P, TT, w])

            def first_max(vals, w, mx, eq, pos, out):
                st.link(dve.tensor_reduce(mx, vals, AX_X, ALU.max))
                st.link(dve.tensor_tensor(eq, vals, b3(mx, w), ALU.is_equal))
                st.link(dve.tensor_tensor(pos, eq, falling[:, 0:w].unsqueeze(1)
                                          .to_broadcast([P, TT, w]), ALU.mult))
                st.link(dve.tensor_reduce(r_pm, pos, AX_X, ALU.max))
                st.link(dve.tensor_tensor(out, pos, b3(r_pm, w), ALU.is_equal))

            coarse, fine = LG[:, :, 0:MG], LG[:, :, MG:NR].rearrange("p t (g e) -> p t g e", e=EG)
            first_max(coarse, MG, r_cmax, r_eq, r_pos, r_oh)
            st.link(dve.tensor_tensor(r_exp[:, 0:TT * MG].rearrange("p (t g) -> p t g", g=MG),
                                      coarse, b3(r_cmax, MG), ALU.subtract))
            st.link(dve.tensor_tensor(r_fo, fine, r_oh.unsqueeze(3).to_broadcast(
                [P, TT, MG, EG]), ALU.mult))
            st.link(dve.tensor_reduce(r_f, r_fo.rearrange("p t g e -> p t e g"), AX_X, ALU.add))
            first_max(r_f, EG, r_m1, r_eq8, r_pos8, r_o[0])
            st.link(dve.scalar_tensor_tensor(r_f2, r_o[0], -1e30, r_f, ALU.mult, ALU.add))
            first_max(r_f2, EG, r_m2, r_eq8, r_pos8, r_o[1])
            link(dve, dve.tensor_tensor(r_exp[:, TT * MG:], r_m2, r_m1, ALU.subtract), rt_arg, 1)
            for k in range(2):
                st.link(dve.tensor_tensor(
                    r_M[k].rearrange("p t (g e) -> p t g e", e=EG),
                    r_oh.unsqueeze(3).to_broadcast([P, TT, MG, EG]),
                    r_o[k].unsqueeze(2).to_broadcast([P, TT, MG, EG]), ALU.mult))
            st.link(dve.tensor_tensor(r_sum, r_M[0], r_M[1], ALU.add))
            st.link(dve.memset(r_pre[:, 0, :], 0.0))
            for t in range(1, TT):
                st.link(dve.tensor_tensor(r_pre[:, t, :], r_pre[:, t - 1, :], r_sum[:, t - 1, :],
                                          ALU.add))
            link(dve, dve.tensor_tensor(r_tot, r_pre[:, TT - 1, :], r_sum[:, TT - 1, :],
                                        ALU.add), rk_in, 1)
            dve.wait_ge(rt_exp, 1)
            st.link(dve.tensor_reduce(r_gw, r_exp[:, 0:TT * MG].rearrange(
                "p (t g) -> p t g", g=MG), AX_X, ALU.add))
            st.link(dve.scalar_tensor_tensor(r_w1, r_exp[:, TT * MG:], 1.0, r_gw, ALU.add,
                                             ALU.mult))
            st.link(dve.reciprocal(wts[:, 0, :], r_w1))
            st.link(dve.tensor_tensor(wts[:, 1, :], wts[:, 0, :], r_exp[:, TT * MG:], ALU.mult))
            dve.wait_ge(rk_mm, 1)

            def per_choice(table, out):
                for k in range(2):
                    st.link(dve.tensor_tensor(r_tmp, r_M[k], table, ALU.mult))
                    st.link(dve.tensor_reduce(out[:, k * TT:(k + 1) * TT], r_tmp, AX_X, ALU.add))

            def multiples(vals, op, out):
                st.link(dve.tensor_scalar(out, vals, float(P), None, op))
                for m in range(2, TT):
                    st.link(dve.scalar_tensor_tensor(out, vals, float(P * m), out, op, ALU.add))

            per_choice(s3(ps[:, 7, 0:TT * NE], NE), r_rk)
            st.link(dve.tensor_copy(r_cnt, ps[:, 7, TT * NE:TT * NE + NE]))
            multiples(r_rk, ALU.is_ge, r_J)
            st.link(dve.scalar_tensor_tensor(r_slot, r_J, -float(P), r_rk, ALU.mult, ALU.add))
            multiples(r_cnt, ALU.is_gt, r_nov)
            st.link(dve.tensor_tensor_scan(r_oinc, ones[:, 0:NE], r_nov, 0.0, ALU.mult, ALU.add))
            st.link(dve.tensor_tensor(r_ost, r_oinc, r_nov, ALU.subtract))
            bt = lambda row: row.unsqueeze(1).to_broadcast([P, TT, NE])
            per_choice(bt(r_ost), r_os)
            per_choice(bt(iota[:, 0:NE]), r_eid)
            st.link(dve.tensor_tensor(r_os, r_os, r_J, ALU.add))
            st.link(dve.tensor_tensor(r_os, r_os, r_eid, ALU.subtract))
            st.link(dve.tensor_scalar(r_g, r_J, 0.0, None, ALU.is_gt))
            st.link(dve.scalar_tensor_tensor(r_os, r_os, NE - 1.0, r_g, ALU.add, ALU.mult))
            st.link(dve.tensor_tensor(r_blk, r_os, r_eid, ALU.add))
            bn = lambda t, w: t.unsqueeze(2).to_broadcast([P, 2 * TT, w])
            bi = lambda w: iota[:, 0:w].unsqueeze(1).to_broadcast([P, 2 * TT, w])
            st.link(dve.tensor_tensor(r_A, bi(P), bn(r_slot, P), ALU.is_equal))
            st.link(dve.tensor_tensor(r_B[:, :, 1, :], bi(NBLK), bn(r_blk, NBLK), ALU.is_equal))
            st.link(dve.tensor_tensor(r_B[:, :, 0, :], r_B[:, :, 1, :], bn(rowid1, NBLK),
                                      ALU.mult))
            for k in range(2):
                half = r_B[:, k * TT:(k + 1) * TT, 1, :]
                ins = dve.tensor_tensor(half, half, b3(tokid, NBLK), ALU.mult)
                if k == 0:
                    st.link(ins)
                else:
                    link(dve, ins, ab_in, 1)
            st.link(dve.tensor_tensor(r_ge, iota[:, 0:16].unsqueeze(2).to_broadcast([P, 16, NE]),
                                      r_oinc.unsqueeze(1).to_broadcast([P, 16, NE]), ALU.is_ge))
            st.link(dve.tensor_reduce(over[:, :], r_ge, AX_X, ALU.add))
            st.link(dve.tensor_scalar(over[:, :], over[:, :], NE - 1.0, None, ALU.min))
            st.link(dve.tensor_copy(over[:, 15:16], r_oinc[:, NE - 1:NE]))
            st.link(dve.tensor_copy(over_i[:, :], over[:, :]))
            dve.wait_ge(tab_mm, 1)
            st.link(dve.tensor_scalar(tab_f[:, 0, :], ps[:, 7, 0:NBLK], 0.0, 8192.0,
                                      ALU.is_equal, ALU.mult))
            st.link(dve.scalar_tensor_tensor(tab_f[:, 0, :], ps[:, 7, 0:NBLK], -1.0,
                                             tab_f[:, 0, :], ALU.add, ALU.add))
            st.link(dve.tensor_copy(tab_f[:, 1, :], ps[:, 7, NBLK:2 * NBLK]))
            link(dve, dve.tensor_copy(tab_i[:, :, :], tab_f[:, :, :]), tab_ready, 1)

            def block_parts(b):
                dve.wait_ge(sg_act, b + 1)
                link(dve, dve.tensor_tensor(HID, SG, ps[:, 1, :], ALU.mult), hid_ready, b + 1)
                dve.wait_ge(hidt_mm, b + 1)
                dve.tensor_copy(HIDT, ps[:, 4, :]).then_inc(hidt_done, 1)

            with dve.Fori(0, NE) as b:
                block_parts(b)
            n_over = dve.value_load(over_i[0:1, 15:16], min_val=0, max_val=MAX_OVER)
            with dve.Fori(0, MAX_OVER) as o:
                with dve.If(n_over > o):
                    block_parts(o + NE)
            with dve.Fori(0, TT // 2) as i:
                st.begin(i, 4)
                for p in range(2):
                    t = i * 2 + p
                    x2 = X2[:, bass.ds(t, 1), :].rearrange("p a n -> p (a n)")
                    dve.wait_ge(yl_in[p], i * 16 + 16)
                    st.link(dve.scalar_tensor_tensor(x2, YL[p][:, 0, :],
                                                     wts[:, 0, bass.ds(t, 1)], x2,
                                                     ALU.mult, ALU.add))
                    link(dve, dve.scalar_tensor_tensor(x2, YL[p][:, 1, :],
                                                       wts[:, 1, bass.ds(t, 1)], x2,
                                                       ALU.mult, ALU.add), x3_ready[p], i + 1)
                    dve.wait_ge(dev3, t + 1)
                    st.link(dve.reciprocal(stat[:, 6, p:p + 1], stat[:, 5, p:p + 1]))
                    dve.wait_ge(out_done[p], i * 16)
                    link(dve, dve.scalar_tensor_tensor(O[p], x2, stat[:, 6, p:p + 1],
                                                       nrow[:, D:2 * D], ALU.mult, ALU.mult),
                         o_ready, t + 1)
            st.end(TT // 2)

        @block.gpsimd
        def _(pool):
            st = Steps(pool, pool_step)
            pool.wait_ge(dt_ready, 1)
            pool.wait_ge(sp_exp, 4)
            pool.dma_start(acs_d, ACS).then_inc(scr_out, 16)
            pool.dma_start(ea_d, EA).then_inc(scr_out, 16)
            pool.wait_ge(lru_done, 8)
            st.link(pool.memset(ACCL, 0.0))
            dch = pv[:, PV["ssd_d"]:PV["ssd_d"] + KT].unsqueeze(2).to_broadcast([P, KT, P])
            with pool.Fori(0, 4) as i:
                for p in range(2):
                    c = i * 2 + p
                    pool.wait_ge(l_in[p], i * 16 + 16)
                    link(pool, pool.tensor_tensor(
                        L[p], L[p], colv[:, 0, bass.ds(c, 1), :].rearrange("p a h -> p (a h)")
                        .unsqueeze(2).to_broadcast([P, NH, P]), ALU.subtract), diff_ready, c + 1)
                    pool.wait_ge(xc_in, c * 16 + 16)
                    y = XBC[:, 0:KT, bass.ds(c * P, P)]
                    link(pool, pool.tensor_tensor(y, y, dch, ALU.mult), xd_ready, c + 1)
                    pool.wait_ge(sql, c + 1)
                    link(pool, pool.tensor_tensor(ACCL, ACCL, SQ, ALU.add), accl, c + 1)
            pool.wait_ge(y_mm[1], 4)
            st.link(pool.memset(ACCS, 0.0))
            with pool.Fori(0, 8) as j:
                pool.wait_ge(sqs, j + 1)
                link(pool, pool.tensor_tensor(ACCS, ACCS, SQ, ALU.add), accs, j + 1)
            pool.wait_ge(tab_ready, 1)
            pool.wait_ge(h2_out[0], 16 * TT // 2)
            pool.wait_ge(h2_out[1], 16 * TT // 2)
            pool.wait_ge(wos_mm, TT)

            one = ones[:, 0:1]

            def gather(b, count):
                st.link(pool.tensor_copy(idx_g[:, :], tab_i[:, 1, bass.ds(b, 1)]))
                pool.tensor_tensor(pad[:, 0:1], one, one, ALU.mult)
                pool.indirect_dma_start(
                    out=XB, out_offset=None, in_=h2_d,
                    in_offset=bass.IndirectOffsetOnAxis(ap=idx_g[:, 0:1], axis=0)).then_inc(xb_in, 16)

            def block_rows(b):
                pool.wait_ge(xb_mm, b + 1)
                gather(b + 1, b + 2)
                pool.wait_ge(yb_act, b + 1)
                pool.wait_ge(y_out, b * 16)
                st.link(pool.tensor_copy(idx_s[:, :], tab_i[:, 0, bass.ds(b, 1)]))
                pool.tensor_tensor(pad[:, 1:2], one, one, ALU.mult)
                pool.indirect_dma_start(
                    out=y_d, out_offset=bass.IndirectOffsetOnAxis(ap=idx_s[:, 0:1], axis=0),
                    in_=YB, in_offset=None, bounds_check=2 * SEQ - 1,
                    oob_is_err=False).then_inc(y_out, 16)

            gather(0, 1)
            with pool.Fori(0, NE) as b:
                st.begin(b, 2)
                block_rows(b)
            st.end(NE)
            pool.wait_ge(tab_ready, 1)
            n_over = pool.value_load(over_i[0:1, 15:16], min_val=0, max_val=MAX_OVER)
            with pool.Fori(0, MAX_OVER) as o:
                with pool.If(n_over > o):
                    st.begin(o, 2)
                    block_rows(o + NE)
            pool.wait_ge(y_out, n_over * 16 + NE * 16)
            pool.wait_ge(scr_out, 32)


def kernel(**inputs):
    import concourse.bacc as bacc
    from concourse.bass_utils import run_bass_kernel_spmd

    f = {k: np.asarray(v) for k, v in inputs.items()}
    rows = lambda v: v.reshape(-1, P).T
    w_in = f["w_in"][0]
    win = w_in[:, :DT_COL].reshape(KT, P, N_IN, P).transpose(2, 1, 0, 3).reshape(N_IN, P, KT * P)
    wdt = w_in[:, DT_COL:].reshape(KT, P, NH).transpose(1, 0, 2)
    wblk = np.zeros((KT, P, 2, P), np.float32)
    for g, name in enumerate(("lru_wa", "lru_wx")):
        for q in range(2):
            s = slice(HD * q, HD * (q + 1))
            wblk[:, s, g, s] = f[name][0].reshape(KT, 2, HD, HD)[:, q]
    pv = np.concatenate([
        rows(f["norm_mix"][0]), rows(f["lru_conv_w"][0]), rows(f["lru_conv_b"][0]),
        rows(f["lru_ba"][0].reshape(-1)), rows(f["lru_bx"][0].reshape(-1)),
        rows(f["lru_lambda"][0]), rows(f["lru_norm"][0]), rows(f["ssd_norm"][0]),
        rows(f["ssd_conv_w"][0]), rows(f["ssd_conv_b"][0]),
        rows(np.repeat(f["ssd_d"][0], HD))], axis=1)
    hpar = np.stack([f["ssd_dt_bias"][0], f["ssd_a_log"][0]], axis=1)
    wout = f["w_out"][0].reshape(2 * KT, P, D).transpose(1, 0, 2)
    fine = f["w_fine"][0].transpose(1, 0, 2).reshape(D, NE)
    wr = np.concatenate([f["w_coarse"][0], fine], axis=1).reshape(KT, P, NR).transpose(1, 0, 2)
    nrow = np.concatenate([f["norm_ffn"][0], f["final_norm"], f["b_coarse"][0],
                           f["b_fine"][0].reshape(-1)])
    gu = np.stack([f["w_gate"][0].reshape(NE, KT, P, DE), f["w_up"][0].reshape(NE, KT, P, DE)],
                  axis=3).reshape(NE, KT, P, 2 * DE)
    moe = np.concatenate([gu, f["w_down"][0].reshape(NE, DE // P, P, D)], axis=1)
    n = np.arange(P, dtype=np.float32)
    tok = np.arange(TT)[None, :] * P + np.arange(P)[:, None]
    cst = np.concatenate([
        np.broadcast_to(n, (P, P)), 2 * tok + 1, 2 * tok + 2, tok,
        np.broadcast_to(EG - np.arange(EG), (P, EG)), n[:, None] < n[None, :]],
        axis=1).astype(np.float32)
    tri = (n[None, :] >= n[:, None]).astype(np.float32)
    arrays = {
        "x": f["x"].reshape(TT, P, D), "win": win, "wdt": wdt, "wblk": wblk, "pv": pv,
        "hpar": hpar, "wout": wout, "wr": wr, "nrow": nrow, "moe": moe.reshape(NE * CH, P, D),
        "cst": cst, "tri": tri, "ident": np.eye(P, dtype=np.float32)}
    nc = bacc.Bacc("TRN2", target_bir_lowering=False, num_devices=1)
    a, feeds = {}, {}
    for name, v in arrays.items():
        feeds["in_" + name] = np.ascontiguousarray(v)
        a[name] = nc.dram_tensor("in_" + name, v.shape, F32, kind="ExternalInput").ap()
    a["out"] = nc.dram_tensor("out_x", (TT, P, D), F32, kind="ExternalOutput").ap()
    build(nc, a)
    r = run_bass_kernel_spmd(nc, [feeds], core_ids=[0])
    return r.results[0]["out_x"].reshape(1, SEQ, D)
```

```python
from contextlib import ExitStack

import numpy as np

import concourse.bass as bass
from concourse import mybir

F32 = mybir.dt.float32
F32R = mybir.dt.float32r
I32 = mybir.dt.int32
ALU = mybir.AluOpType
ACT = mybir.ActivationFunctionType
AX_X = mybir.AxisListType.X

P = 128
D = 1024
SEQ = 1024
KT = D // P
TT = SEQ // P
NH = 16
HD = 64
NG = 4
CONV_K = 4
MG, EG = 4, 8
NE = MG * EG
DE = 512
EPS = 1e-6
DT_COL = 5 * D
N_IN = DT_COL // P
T_GATE, T_Z, T_XBC = 8, 16, 24
NR = MG + NE
MAX_OVER = 15
NBLK = NE + MAX_OVER + 1
CH = KT + DE // P
KD = DE // P
HL = 6
GU_AT, DN_AT = KT - CH, KT
DN_LAST = (NE - 1) * CH + KT
OVER_AT = NE * CH

PV_SIZES = dict(norm_mix=8, lru_cw=32, lru_cb=8, lru_ba=8, lru_bx=8, lam=8, lru_norm=8,
                ssd_norm=8, ssd_cw=64, ssd_cb=16, ssd_d=8)
PV = {}
for _n, _s in PV_SIZES.items():
    PV[_n] = sum(PV_SIZES[m] for m in list(PV_SIZES)[:list(PV_SIZES).index(_n)])
NPV = sum(PV_SIZES.values())


class Steps:

    def __init__(self, eng, sem):
        self.eng, self.sem, self.done, self.turn = eng, sem, 0, None

    def link(self, ins):
        ins.then_inc(self.sem, 1)
        self.done += 1
        self.eng.wait_ge(self.sem, self.done if self.turn is None else self.turn + self.done)

    def begin(self, i, per):
        self.turn, self.first, self.per = i * per, self.done, per

    def end(self, trips):
        assert self.done - self.first == self.per, (self.done - self.first, self.per)
        self.turn, self.done = None, self.first + trips * self.per


def link(eng, ins, sem, value):
    ins.then_inc(sem, 1)
    eng.wait_ge(sem, value)


def build(nc, a):
    with ExitStack() as ctx:
        def sb(name, shape, dt=F32):
            return ctx.enter_context(nc.sbuf_tensor(name, shape, dt))

        def sem(name):
            return ctx.enter_context(nc.semaphore(name))

        def dram(name, shape):
            return nc.dram_tensor(name, shape, F32).ap()

        acs_d, ea_d = dram("acs_d", [NH, SEQ]), dram("ea_d", [NH, SEQ])
        h2_d, y_d = dram("h2_d", [SEQ, D]), dram("y_d", [2 * SEQ, D])

        ps = ctx.enter_context(nc.psum_tensor("ps", [P, 8, 512], F32))

        def pair(b):
            return ps[:, b:b + 2, :].rearrange("p b n -> p (b n)")

        pv = sb("pv", [P, NPV])
        ident = sb("ident", [P, P])
        ones = sb("ones", [P, P])
        prep = sb("prep", [P, 4, 8])
        eps = sb("eps", [P, 2])
        stat = sb("stat", [P, 8, 16])
        cst = sb("cst", [P, 128 + 16 + 8 + 8 + 128])
        tab_f = sb("tab_f", [P, 2, NBLK])
        tab_i = sb("tab_i", [P, 2, NBLK], I32)
        over = sb("over", [P, 16])
        over_i = sb("over_i", [P, 16], I32)
        wts = sb("wts", [P, 2, TT])
        pad = sb("pad", [P, 2])
        idx_g, idx_s = sb("idx_g", [P, 1], I32), sb("idx_s", [P, 1], I32)

        mixer = ExitStack()

        def mixer_sb(name, shape):
            return mixer.enter_context(nc.sbuf_tensor(name, shape, F32))

        hT = mixer_sb("hT", [P, KT, SEQ])
        XBC = mixer_sb("XBC", [P, 16, SEQ])
        HR = mixer_sb("HR", [P, KT, SEQ])
        scratch = mixer_sb("scratch", [P, 18944])

        def area(at, *dims):
            n = int(np.prod(dims))
            assert at + n <= 18944, (at, dims)
            t = scratch[:, at:at + n]
            if len(dims) == 2:
                return t.rearrange("p (a b) -> p a b", b=dims[1])
            if len(dims) == 3:
                return t.rearrange("p (a b c) -> p a b c", b=dims[1], c=dims[2])
            return t

        win = area(0, 3, KT * P)
        xall = area(3072, KT, D)
        xn = [area(11264, D), area(12288, D)]
        junk = area(13312, D)
        sv = {n: area(3072 + 1024 * k, D)[0:NH, :] for k, n in
              enumerate(["v", "nab", "e", "s", "s2", "p"])}
        DT, ACS, WD, EA = (area(9216 + 1024 * k, D)[0:NH, :] for k in range(4))
        smask = area(13312, D)[0:NH, :]
        wdt = area(14336, KT, NH)
        dd = area(14464, TT, NH)[0:NH]
        dec16 = area(14592, TT)[0:NH, :]
        hpar = area(14608, 2)[0:NH, :]
        lsp = area(14616, 6, 8)
        U, XE, XO = area(3072, D), area(4096, D), area(5120, D)
        TR, TI, AA, TG = (area(k, D) for k in (6144, 7168, 8192, 14720))
        A2 = area(15744, D)
        Q = area(16768, D)
        wblk = area(17792, 2, P)
        XC = area(3072, 12, P)
        L = [area(4608, NH, P), area(6656, NH, P)]
        EAB = area(8704, KT, P)
        XDT, XW = area(9728, D), area(10752, D)
        BT, SM = area(11776, NG, P), area(12288, NG, P)
        STATE, YT = area(12800, D), area(13824, D)
        G, SQ = area(14848, D), area(15872, D)
        ACCL = area(17000, D)
        tri = area(18024, P)
        colv = area(18152, 3, TT, NH)
        decb = area(18536, TT, NH)
        Z = [area(3072, D), area(4096, D)]
        ACCS = area(5120, D)
        WO_L, WO_S = XBC[:, 8:16, :], hT[:, :, :]
        XR = [area(0, D), area(1024, D)]
        H2 = [area(2048, D), area(3072, D)]
        H2T = area(4096, KT, P)
        iota, rowid1 = cst[:, 0:P], cst[:, P:P + 16]
        tokid, falling = cst[:, P + 16:P + 24], cst[:, P + 24:P + 32]
        above = cst[:, P + 32:2 * P + 32]

        mixer.close()
        XB, YB, SGH = sb("XB", [P, D]), sb("YB", [P, D]), sb("SGH", [P, 2 * DE])
        SG, HID = SGH[:, 0:DE], SGH[:, DE:2 * DE]
        XTH, XTL = sb("XTH", [P, D], F32R), sb("XTL", [P, D], F32R)
        HTH, HTL = sb("HTH", [P, DE], F32R), sb("HTL", [P, DE], F32R)
        split_a = sb("split_a", [P, 2, D], F32R)
        ring_dn = sb("ring_dn", [P, KD, D])
        split_b = sb("split_b", [P, 4, D], F32R)
        late = sb("late", [P, 8, D])
        ring_gu = sb("ring_gu", [P, KT, D])
        split_c = sb("split_c", [P, 6, D], F32R)
        stay = sb("stay", [P, 18944 - 6 * D])
        ring = [ring_gu[:, j, :] if j < KT else ring_dn[:, j - KT, :] for j in range(CH)]
        parts = [t[:, n, :] for t, m in ((split_a, 2), (split_b, 4), (split_c, 6))
                 for n in range(m)]
        WH, WL = parts[0::2], parts[1::2]
        X2 = stay[:, 0:TT * D].rearrange("p (t d) -> p t d", d=D)
        wr = stay[:, 8192:8192 + KT * NR].rearrange("p (k n) -> p k n", n=NR)
        LG = stay[:, 8480:8480 + TT * NR].rearrange("p (t n) -> p t n", n=NR)
        nrow = stay[:, 8768:8768 + 2 * D + NR]

        const_in, late_in = sem("const_in"), sem("late_in")
        x_in = [sem(f"x_in{t}") for t in range(TT)]
        act_step, dve_step, pool_step = sem("act_step"), sem("dve_step"), sem("pool_step")
        par_done = sem("par_done")
        dev_ready, inv_ready, xn_ready, xt_ready, ht_done = map(
            sem, ("dev_ready", "inv_ready", "xn_ready", "xt_ready", "ht_done"))
        dt_mm, dt_v, sp_arg, sp_exp, dt_ready, scr_out, dec_ready = map(
            sem, ("dt_mm", "dt_v", "sp_arg", "sp_exp", "dt_ready", "scr_out", "dec_ready"))
        w_in_sem = [sem(f"w_in{s}") for s in range(3)]
        wblk_in = sem("wblk_in")
        wc_in = [sem("wc_in0"), sem("wc_in1")]
        lru_mm, xe_mm, xo_mm, gt_mm = map(sem, ("lru_mm", "xe_mm", "xo_mm", "gt_mm"))
        tap_u, tap_e, tap_o, u_ready, cv_e, cv_o = map(
            sem, ("tap_u", "tap_e", "tap_o", "u_ready", "cv_e", "cv_o"))
        gate_act, a2_act, m2_ready, sq_act, lru_done, silu_e, silu_o = map(
            sem, ("gate_act", "a2_act", "m2_ready", "sq_act", "lru_done", "silu_e", "silu_o"))
        prep_mm, prep_done = sem("prep_mm"), sem("prep_done")
        xc_in, ea_in = sem("xc_in"), sem("ea_in")
        l_in = [sem("l_in0"), sem("l_in1")]
        ts_mm, st_mm, yo_mm = map(sem, ("ts_mm", "st_mm", "yo_mm"))
        y_mm, g_mm = [sem("y_mm0"), sem("y_mm1")], [sem("g_mm0"), sem("g_mm1")]
        xw_ready, sm_ready, diff_ready, min_ready, e_ready, m_ready, st_upd, comb = map(
            sem, ("xw_ready", "sm_ready", "diff_ready", "min_ready", "e_ready", "m_ready",
                  "st_upd", "comb"))
        bt_ready, g_act, lru_g, sql, accl, xd_ready, lru_w = map(
            sem, ("bt_ready", "g_act", "lru_g", "sql", "accl", "xd_ready", "lru_w"))
        z_in = [sem("z_in0"), sem("z_in1")]
        z_mm, z_act, zy = ([sem(f"{n}{p}") for p in range(2)] for n in ("z_mm", "z_act", "zy"))
        sqs, accs, ssd_w = sem("sqs"), sem("accs"), sem("ssd_w")
        wo_in = [sem("wo_in0"), sem("wo_in1")]
        xr_in = [sem("xr_in0"), sem("xr_in1")]
        ss_mm, devo, invo = sem("ss_mm"), sem("devo"), sem("invo")
        wol_mm, wos_mm, x2_l, x2_s = map(sem, ("wol_mm", "wos_mm", "x2_l", "x2_s"))
        dev2, inv2, h2_ready = sem("dev2"), sem("inv2"), sem("h2_ready")
        h2_out = [sem("h2_out0"), sem("h2_out1")]
        ht2_mm, ht2_act, lg_mm, lg_done = map(sem, ("ht2_mm", "ht2_act", "lg_mm", "lg_done"))

        rt = late[:, :, :].rearrange("p a n -> p (a n)")
        at = [0]

        def route_tile(*dims):
            n = int(np.prod(dims))
            t = rt[:, at[0]:at[0] + n]
            at[0] += n
            if len(dims) == 2:
                return t.rearrange("p (a b) -> p a b", b=dims[1])
            if len(dims) == 3:
                return t.rearrange("p (a b c) -> p a b c", b=dims[1], c=dims[2])
            return t

        r_eq, r_pos, r_oh = (route_tile(TT, MG) for _ in range(3))
        r_fo = route_tile(TT, MG, EG)
        r_f, r_f2, r_eq8, r_pos8 = (route_tile(TT, EG) for _ in range(4))
        r_o = [route_tile(TT, EG) for _ in range(2)]
        r_cmax, r_pm, r_gw, r_w1, r_m1, r_m2 = (route_tile(TT) for _ in range(6))
        r_exp = route_tile(TT * (MG + 1))
        r_M = [route_tile(TT, NE) for _ in range(2)]
        r_sum, r_pre, r_tmp = (route_tile(TT, NE) for _ in range(3))
        r_tot, r_cnt, r_nov, r_oinc, r_ost = (route_tile(NE) for _ in range(5))
        r_rk, r_J, r_slot, r_os, r_eid, r_blk, r_g = (route_tile(2 * TT) for _ in range(7))
        r_A = route_tile(2 * TT, P)
        r_B = route_tile(2 * TT, 2, NBLK)
        r_ge = route_tile(16, NE)
        rt_arg, rt_exp, rk_in, rk_mm, ab_in, tab_mm, tab_ready = map(
            sem, ("rt_arg", "rt_exp", "rk_in", "rk_mm", "ab_in", "tab_mm", "tab_ready"))

        wch_in = [sem(f"wch_in{j}") for j in range(CH)]
        hi_made, lo_made, ch_used, xb_in, xb_mm, xt_hi, xt_lo, sg_act, hid_ready = map(
            sem, ("hi_made", "lo_made", "ch_used", "xb_in", "xb_mm", "xt_hi", "xt_lo", "sg_act",
                  "hid_ready"))
        hidt_mm, ht_hi, ht_lo, yb_act, y_out = map(
            sem, ("hidt_mm", "ht_hi", "ht_lo", "yb_act", "y_out"))
        YL = [late[:, 2 * p:2 * p + 2, :] for p in range(2)]
        FSQ = late[:, 6, :]
        yl_in = [sem("yl_in0"), sem("yl_in1")]
        x3_ready, dev3, o_ready, out_done = map(sem, ("x3_ready", "dev3", "o_ready", "out_done"))

        block = ctx.enter_context(nc.Block())

        def param(name, i, k=0):
            return pv[:, bass.ds(i + (PV[name] + k), 1)]

        @block.sync
        def _(sp):
            for t in range(TT):
                sp.dma_start(xall[:, t, :], a["x"][t]).then_inc(x_in[t], 16)
                if t == 1:
                    sp.dma_start(pv[:, :], a["pv"]).then_inc(const_in, 16)
                    sp.dma_start(ident[:, :], a["ident"]).then_inc(const_in, 16)
                    sp.dma_start(wdt, a["wdt"]).then_inc(const_in, 16)
                    sp.dma_start(hpar, a["hpar"]).then_inc(const_in, 16)

            def w_tile(slot, tile, signal):
                sp.dma_start(win[:, slot, :], a["win"][bass.ds(tile, 1)].rearrange(
                    "a p n -> p (a n)")).then_inc(signal, 16)

            with sp.Fori(0, 8) as i:
                sp.wait_ge(lru_mm, i)
                w_tile(0, i, w_in_sem[0])
                sp.wait_ge(xe_mm, i)
                w_tile(1, i * 2 + T_XBC, w_in_sem[1])
                sp.wait_ge(gt_mm, i * 2)
                sp.dma_start(wblk, a["wblk"][bass.ds(i, 1)].rearrange(
                    "a p g n -> p (a g) n")).then_inc(wblk_in, 16)
                sp.wait_ge(xo_mm, i)
                w_tile(2, i * 2 + (T_XBC + 1), w_in_sem[2])
            sp.dma_start(cst[:, :], a["cst"]).then_inc(late_in, 16)
            sp.wait_ge(lru_done, 8)
            sp.dma_start(tri, a["tri"]).then_inc(late_in, 16)
            sp.wait_ge(silu_e, 8)
            sp.wait_ge(silu_o, 8)
            sp.wait_ge(xo_mm, 8)
            sp.wait_ge(prep_done, 2)
            sp.wait_ge(scr_out, 32)
            with sp.Fori(0, 4) as i:
                for p in range(2):
                    c = i * 2 + p
                    sp.wait_ge(g_mm[p], i)
                    w_tile(p, c + T_GATE, wc_in[p])
                    sp.wait_ge(ts_mm, c)
                    sp.dma_start(XC, XBC[:, 0:12, bass.ds(c * P, P)]).then_inc(xc_in, 16)
                    sp.wait_ge(y_mm[p], i)
                    sp.dma_start(L[p], acs_d[:, bass.ds(c * P, P)].partition_broadcast(P)
                                 ).then_inc(l_in[p], 16)
                    sp.wait_ge(comb, c)
                    for q in range(2):
                        sp.dma_start(EAB[HD * q:HD * (q + 1)], ea_d.rearrange(
                            "(j q) s -> q j s", q=2)[q][:, bass.ds(c * P, P)
                            ].partition_broadcast(HD)).then_inc(ea_in, 16)
            sp.wait_ge(yo_mm, 8)
            sp.wait_ge(g_mm[0], 4)
            sp.wait_ge(g_mm[1], 4)
            sp.wait_ge(comb, 8)
            with sp.Fori(0, 4) as i:
                for p in range(2):
                    sp.wait_ge(z_mm[p], i)
                    w_tile(p, i * 2 + (T_Z + p), z_in[p])
            sp.dma_start(WO_L, a["wout"][:, 0:8, :]).then_inc(wo_in[0], 16)
            sp.wait_ge(z_mm[0], 4)
            sp.wait_ge(z_mm[1], 4)
            sp.dma_start(WO_S, a["wout"][:, 8:16, :]).then_inc(wo_in[1], 16)
            sp.wait_ge(accs, 8)
            sp.dma_start(wr, a["wr"]).then_inc(late_in, 16)
            sp.dma_start(nrow, a["nrow"].partition_broadcast(P)).then_inc(late_in, 16)
            for t in range(TT):
                if t >= 2:
                    sp.wait_ge(x2_l, t - 1)
                sp.dma_start(XR[t % 2], a["x"][t]).then_inc(xr_in[t % 2], 16)
                if t >= 1:
                    sp.wait_ge(h2_ready, t)
                    sp.dma_start(h2_d[P * (t - 1):P * t, :], H2[(t - 1) % 2]).then_inc(
                        h2_out[(t - 1) % 2], 16)
            sp.wait_ge(h2_ready, TT)
            sp.dma_start(h2_d[P * (TT - 1):, :], H2[(TT - 1) % 2]).then_inc(
                h2_out[(TT - 1) % 2], 16)
            sp.wait_ge(wol_mm, TT)
            sp.wait_ge(wos_mm, TT)

            def load(j, e):
                sp.dma_start(ring[j], a["moe"][bass.ds(e * CH + j, 1)].rearrange(
                    "a p n -> p (a n)")).then_inc(wch_in[j], 16)

            for j in range(KT):
                sp.dma_start(ring[j], a["moe"][j]).then_inc(wch_in[j], 16)
            for j in range(KT):
                sp.wait_ge(lo_made, j + 1)
                sp.dma_start(ring[j], a["moe"][CH + j]).then_inc(wch_in[j], 16)
            for j in range(KT, CH):
                sp.dma_start(ring[j], a["moe"][j]).then_inc(wch_in[j], 16)
            with sp.Fori(2, NE) as e:
                for j in range(KT):
                    sp.wait_ge(lo_made, e * CH + (GU_AT - CH + j + 1))
                    load(j, e)
                for j in range(KT, CH):
                    sp.wait_ge(lo_made, e * CH + (DN_AT - 2 * CH + j + 1))
                    load(j, e - 1)
            for j in range(KT, CH):
                sp.wait_ge(lo_made, (NE - 1) * CH + DN_AT - CH + j + 1)
                sp.dma_start(ring[j], a["moe"][(NE - 1) * CH + j]).then_inc(wch_in[j], 16)
            sp.wait_ge(tab_ready, 1)
            n_over = sp.value_load(over_i[0:1, 15:16], min_val=0, max_val=MAX_OVER)
            with sp.Fori(0, MAX_OVER) as o:
                with sp.If(n_over > o):
                    e = sp.value_load(over_i[0:1, bass.ds(o, 1)], min_val=0, max_val=NE - 1)
                    for j in range(CH):
                        sp.wait_ge(lo_made, o * CH + (OVER_AT - CH + 1 + j))
                        load(j, e)
            sp.wait_ge(y_out, n_over * 16 + NE * 16)
            for t in range(TT):
                if t >= 2:
                    sp.wait_ge(x3_ready, t - 1)
                sp.dma_start(YL[t % 2], y_d.rearrange("(t p k) d -> t p k d", p=P, k=2)[t]
                             ).then_inc(yl_in[t % 2], 16)
            sp.wait_ge(out_done, 16 * TT)

        @block.tensor
        def _(pe):
            def project(slot, bank, signal):
                for h in range(2):
                    mm = project_half(slot, bank, h)
                mm.then_inc(signal, 1)

            def project_half(slot, bank, h):
                for k in range(KT):
                    mm = pe.matmul(ps[:, bank + h, :], win[:, slot, k * P:(k + 1) * P],
                                   hT[:, k, h * 512:(h + 1) * 512], start=(k == 0),
                                   stop=(k == KT - 1))
                return mm

            pe.wait_ge(const_in, 64)
            for t in range(TT):
                if t >= 2:
                    pe.wait_ge(ht_done, 2 * (t - 1))
                pe.wait_ge(xn_ready, t + 1)
                for k in range(KT):
                    mm = pe.transpose(ps[:, 2 * (t % 2) + k // 4, (k % 4) * P:(k % 4 + 1) * P],
                                      xn[t % 2][:, k * P:(k + 1) * P], ident[:, :])
                mm.then_inc(xt_ready, 1)
            pe.wait_ge(ht_done, 2 * TT)
            for h in range(2):
                for k in range(KT):
                    mm = pe.matmul(ps[0:NH, 4 + h, :], wdt[:, k, :],
                                   hT[:, k, h * 512:(h + 1) * 512], start=(k == 0),
                                   stop=(k == KT - 1))
            mm.then_inc(dt_mm, 1)
            pe.wait_ge(dt_v, 1)
            with pe.Fori(0, 8) as i:
                pe.wait_ge(w_in_sem[0], i * 16 + 16)
                pe.wait_ge(gate_act, i * 2)
                project(0, 4, lru_mm)
                pe.wait_ge(w_in_sem[1], i * 16 + 16)
                pe.wait_ge(cv_e, i)
                project(1, 0, xe_mm)
                pe.wait_ge(u_ready, i + 1)
                pe.wait_ge(wblk_in, i * 16 + 16)
                for g in range(2):
                    for h in range(2):
                        mm = pe.matmul(ps[:, 6 - 2 * g + h, :], wblk[:, g, :],
                                       U[:, h * 512:(h + 1) * 512], start=True, stop=True)
                    mm.then_inc(gt_mm, 1)
                pe.wait_ge(w_in_sem[2], i * 16 + 16)
                pe.wait_ge(cv_o, i)
                project(2, 2, xo_mm)
            pe.wait_ge(dt_ready, 1)
            pe.wait_ge(cv_e, 8)
            for q, rows in enumerate((ACS, DT, WD)):
                for c in range(TT):
                    at = (q * TT + c) * NH
                    mm = pe.transpose(ps[:, 0, at:at + NH], rows[:, c * P:(c + 1) * P],
                                      ident[0:NH, 0:NH])
            mm.then_inc(prep_mm, 1)
            pe.matmul(ps[:, 1, 0:TT * NH], ones[0:NH, :], dd.rearrange("h c k -> h (c k)"),
                      start=True, stop=True).then_inc(prep_mm, 1)
            pe.wait_ge(prep_done, 2)
            pe.wait_ge(cv_o, 8)
            pe.wait_ge(gate_act, 16)
            with pe.Fori(0, 4) as i:
                for p in range(2):
                    c = i * 2 + p
                    pe.wait_ge(xc_in, c * 16 + 16)
                    pe.wait_ge(comb, c)
                    for k in range(KT):
                        pe.transpose(ps[:, 2 + k // 4, (k % 4) * P:(k % 4 + 1) * P],
                                     XC[:, k, :], ident[:, :])
                    for g in range(NG):
                        pe.transpose(ps[:, 4, g * P:(g + 1) * P], XC[:, KT + g, :], ident[:, :])
                    for g in range(NG):
                        mm = pe.matmul(ps[:, 5, g * P:(g + 1) * P], XC[:, KT + g, :],
                                       XBC[:, 12 + g, bass.ds(c * P, P)], start=True, stop=True)
                    mm.then_inc(ts_mm, 1)
                    pe.wait_ge(wc_in[p], i * 16 + 16)
                    pe.wait_ge(g_act, c)
                    project_half(p, 0, 0)
                    pe.wait_ge(xw_ready, c + 1)
                    pe.wait_ge(bt_ready, c + 1)
                    pe.wait_ge(st_upd, c)
                    for g in range(NG):
                        mm = pe.matmul(ps[:, 6 + g // 2, (g % 2) * 256:(g % 2 + 1) * 256],
                                       BT[:, g, :], XW[:, g * 256:(g + 1) * 256],
                                       start=True, stop=True)
                    mm.then_inc(st_mm, 1)
                    pe.wait_ge(sm_ready, c + 1)
                    for j in range(KT):
                        mm = pe.matmul(ps[:, 4 + j // 4, (j % 4) * P:(j % 4 + 1) * P],
                                       STATE[:, j * P:(j + 1) * P],
                                       XBC[:, 12 + j // 2, bass.ds(c * P, P)],
                                       start=True, stop=True)
                    mm.then_inc(yo_mm, 1)
                    pe.wait_ge(m_ready, c + 1)
                    for h in range(NH):
                        j, q = h // 2, h % 2
                        mm = pe.matmul(ps[HD * q:HD * (q + 1), 2 + j // 4,
                                          (j % 4) * P:(j % 4 + 1) * P],
                                       XDT[:, h * HD:(h + 1) * HD], L[p][:, h, :],
                                       start=True, stop=True)
                    mm.then_inc(y_mm[p], 1)
                    project_half(p, 0, 1).then_inc(g_mm[p], 1)
            pe.wait_ge(g_act, 8)
            pe.wait_ge(comb, 8)
            with pe.Fori(0, 4) as i:
                for p in range(2):
                    pe.wait_ge(z_in[p], i * 16 + 16)
                    pe.wait_ge(z_act[p], i)
                    project(p, 2 * p, z_mm[p])
            pe.wait_ge(accl, 8)
            pe.wait_ge(accs, 8)
            for r, acc in enumerate((ACCL, ACCS)):
                for t in range(TT):
                    mm = pe.matmul(ps[:, 6, r * TT + t:r * TT + t + 1],
                                   acc[:, t * P:(t + 1) * P], ones[:, 0:1],
                                   start=True, stop=True)
            mm.then_inc(ss_mm, 1)
            pe.wait_ge(lru_w, 8)
            pe.wait_ge(ssd_w, 8)
            pe.wait_ge(z_act[0], 4)
            pe.wait_ge(z_act[1], 4)
            pe.wait_ge(devo, 1)
            pe.wait_ge(late_in, 64)

            def out_half(t, bank, y, w, signal):
                for h in range(2):
                    for k in range(KT):
                        mm = pe.matmul(ps[:, bank + h, :], y[:, k, t * P:(t + 1) * P],
                                       w[:, k, h * 512:(h + 1) * 512], start=(k == 0),
                                       stop=(k == KT - 1))
                mm.then_inc(signal, 1)

            def turn_h2(t):
                pe.wait_ge(h2_ready, t + 1)
                if t >= 1:
                    pe.wait_ge(ht2_act, t)
                for k in range(KT):
                    mm = pe.transpose(ps[:, 4 + k // 4, (k % 4) * P:(k % 4 + 1) * P],
                                      H2[t % 2][:, k * P:(k + 1) * P], ident[:, :])
                mm.then_inc(ht2_mm, 1)

            def route(t):
                pe.wait_ge(ht2_act, t + 1)
                if t >= 1:
                    pe.wait_ge(lg_done, t)
                for k in range(KT):
                    mm = pe.matmul(ps[:, 6, 0:NR], H2T[:, k, :], wr[:, k, :],
                                   start=(k == 0), stop=(k == KT - 1))
                mm.then_inc(lg_mm, 1)

            pe.wait_ge(wo_in[0], 16)
            for t in range(TT):
                if t >= 1:
                    pe.wait_ge(x2_l, t)
                out_half(t, 0, HR, WO_L, wol_mm)
                if t >= 1:
                    turn_h2(t - 1)
                if t == 0:
                    pe.wait_ge(wo_in[1], 16)
                else:
                    pe.wait_ge(x2_s, t)
                out_half(t, 2, XBC, WO_S, wos_mm)
                if t >= 1:
                    route(t - 1)
            turn_h2(TT - 1)
            route(TT - 1)
            pe.wait_ge(lg_done, TT)
            pe.wait_ge(rk_in, 1)
            flat = lambda t: t.rearrange("p a b -> p (a b)")
            pe.matmul(ps[:, 7, 0:TT * NE], above, flat(r_sum), start=True, stop=False)
            pe.matmul(ps[:, 7, 0:TT * NE], ones[:, :], flat(r_pre), start=False, stop=True)
            pe.matmul(ps[:, 7, TT * NE:TT * NE + NE], ones[:, :], r_tot, start=True,
                      stop=True).then_inc(rk_mm, 1)
            pe.wait_ge(ab_in, 1)
            for n in range(2 * TT):
                mm = pe.matmul(ps[:, 7, 0:2 * NBLK], r_A[:, n, :],
                               r_B[:, n, :, :].rearrange("p a b -> p (a b)"),
                               start=(n == 0), stop=(n == 2 * TT - 1))
            mm.then_inc(tab_mm, 1)

            def turn_rows(count):
                pe.wait_ge(xb_in, count * 16)
                for k in range(KT):
                    mm = pe.transpose(ps[:, 2 + k // 4, (k % 4) * P:(k % 4 + 1) * P],
                                      XB[:, k * P:(k + 1) * P], ident[:, :])
                mm.then_inc(xb_mm, 1)

            def split_product(bank, hi, lo, k, at, slot, last):
                pe.wait_ge(lo_made, at + 1)
                rows = slice(k * P, (k + 1) * P)
                for n, (x, w) in enumerate(((hi, WH), (hi, WL), (lo, WH))):
                    for h in range(2):
                        mm = pe.matmul(ps[:, bank + h, :], x[:, rows],
                                       w[slot % HL][:, h * 512:(h + 1) * 512],
                                       start=(k == 0 and n == 0), stop=(last and n == 2))
                mm.then_inc(ch_used, 1)

            def gate_up(b, at, slot):
                pe.wait_ge(xt_lo, b + 1)
                pe.wait_ge(hid_ready, b)
                for k in range(KT):
                    split_product(0, XTH, XTL, k, at + k, slot + k, k == KT - 1)

            def down(b, at, slot):
                pe.wait_ge(ht_lo, b + 1)
                pe.wait_ge(yb_act, b)
                for k in range(KD):
                    split_product(5, HTH, HTL, k, at + k, slot + k, k == KD - 1)

            def turn_hidden(b):
                pe.wait_ge(hid_ready, b + 1)
                for k in range(KD):
                    mm = pe.transpose(ps[:, 4, k * P:(k + 1) * P], HID[:, k * P:(k + 1) * P],
                                      ident[:, :])
                mm.then_inc(hidt_mm, 1)

            turn_rows(1)
            gate_up(0, 0, 0)
            turn_rows(2)
            turn_hidden(0)
            with pe.Fori(1, NE) as b:
                gate_up(b, b * CH + GU_AT, GU_AT)
                turn_rows(b + 2)
                down(b - 1, b * CH + DN_AT - CH + KT, DN_AT - CH + KT)
                turn_hidden(b)
            down(NE - 1, DN_LAST, DN_LAST)
            n_over = pe.value_load(over_i[0:1, 15:16], min_val=0, max_val=MAX_OVER)
            with pe.Fori(0, MAX_OVER) as o:
                with pe.If(n_over > o):
                    gate_up(o + NE, o * CH + OVER_AT, 0)
                    turn_rows(o + (NE + 2))
                    turn_hidden(o + NE)
                    down(o + NE, o * CH + (OVER_AT + KT), KT)

        @block.scalar
        def _(act):
            st = Steps(act, act_step)
            act.wait_ge(par_done, 1)
            for t in range(TT):
                act.wait_ge(x_in[t], 16)
                st.link(act.activation(junk, xall[:, t, :], ACT.Square,
                                       accum_out=stat[:, 0, t:t + 1]))
            link(act, act.activation(stat[:, 1, 0:TT], stat[:, 0, 0:TT], ACT.Sqrt,
                                     bias=eps[:, 0:1], scale=1.0 / D), dev_ready, 1)
            act.wait_ge(inv_ready, 1)
            for t in range(TT):
                if t >= 2:
                    act.wait_ge(xt_ready, t - 1)
                act.activation(xn[t % 2], xall[:, t, :], ACT.Copy,
                               scale=stat[:, 2, t:t + 1]).then_inc(xn_ready, 1)
            act.wait_ge(xn_ready, TT)
            act.wait_ge(const_in, 64)
            act.wait_ge(dt_mm, 1)
            link(act, act.activation(sv["v"], pair(4)[0:NH, :], ACT.Identity,
                                     bias=hpar[:, 0:1]), dt_v, 1)
            act.wait_ge(sp_arg, 1)
            link(act, act.activation(lsp[:, 2, :], lsp[:, 1, :], ACT.Exp), sp_exp, 1)
            st.link(act.activation(hpar[:, 1:2], hpar[:, 1:2], ACT.Exp))
            act.wait_ge(sp_arg, 2)
            link(act, act.activation(sv["e"], sv["nab"], ACT.Exp), sp_exp, 2)
            act.wait_ge(sp_arg, 3)
            link(act, act.activation(WD, sv["p"], ACT.Exp), sp_exp, 3)
            link(act, act.activation(EA, ACS, ACT.Exp), sp_exp, 4)
            link(act, act.activation(dec16, ACS.rearrange("h (c l) -> h c l", l=P)[:, :, P - 1],
                                     ACT.Exp), sp_exp, 5)
            act.wait_ge(dt_ready, 1)
            with act.Fori(0, 8) as i:
                st.begin(i, 2)
                act.wait_ge(lru_mm, i + 1)
                act.wait_ge(gt_mm, i * 2)
                act.wait_ge(lru_done, i)
                link(act, act.activation(U, pair(4), ACT.Identity, bias=param("lru_cb", i),
                                         scale=param("lru_cw", i, 24)), tap_u, i + 1)
                act.wait_ge(xe_mm, i + 1)
                link(act, act.activation(XE, pair(0), ACT.Identity,
                                         bias=param("ssd_cb", i * 2),
                                         scale=param("ssd_cw", i * 2, 48)), tap_e, i + 1)
                act.wait_ge(cv_e, i + 1)
                link(act, act.activation(XBC[:, bass.ds(i * 2, 1), :].rearrange(
                    "p a n -> p (a n)"), XE, ACT.Silu), silu_e, i + 1)
                act.wait_ge(gt_mm, i * 2 + 1)
                link(act, act.activation(TR, pair(6), ACT.Tanh,
                                         bias=prep[:, 0, bass.ds(i, 1)], scale=0.5),
                     gate_act, i * 2 + 1)
                act.wait_ge(gt_mm, i * 2 + 2)
                link(act, act.activation(TI, pair(4), ACT.Tanh,
                                         bias=prep[:, 1, bass.ds(i, 1)], scale=0.5),
                     gate_act, i * 2 + 2)
                st.link(act.activation(AA, TR, ACT.Exp, bias=prep[:, 2, bass.ds(i, 1)],
                                       scale=prep[:, 2, bass.ds(i, 1)]))
                st.link(act.activation(TG, TR, ACT.Tanh, bias=prep[:, 3, bass.ds(i, 1)],
                                       scale=prep[:, 3, bass.ds(i, 1)]))
                link(act, act.activation(A2, AA, ACT.Square), a2_act, i + 1)
                act.wait_ge(m2_ready, i + 1)
                link(act, act.activation(A2, A2, ACT.Sqrt, bias=eps[:, 1:2]), sq_act, i + 1)
                act.wait_ge(xo_mm, i + 1)
                link(act, act.activation(XO, pair(2), ACT.Identity,
                                         bias=param("ssd_cb", i * 2, 1),
                                         scale=param("ssd_cw", i * 2, 49)), tap_o, i + 1)
                act.wait_ge(cv_o, i + 1)
                link(act, act.activation(XBC[:, bass.ds(i * 2 + 1, 1), :].rearrange(
                    "p a n -> p (a n)"), XO, ACT.Silu), silu_o, i + 1)
            st.end(8)
            def decay_exp(c, p):
                act.wait_ge(min_ready, c + 1)
                link(act, act.activation(L[p], L[p], ACT.Exp), e_ready, c + 1)

            def chunk(i, p, last=False):
                c = i * 2 + p
                act.wait_ge(ts_mm, c + 1)
                if not (isinstance(c, int) and c == 0):
                    act.wait_ge(st_mm, c)
                link(act, act.activation(BT.rearrange("p g n -> p (g n)"), ps[:, 4, :],
                                         ACT.Copy), bt_ready, c + 1)
                act.wait_ge(g_mm[p], i + 1)
                act.wait_ge(lru_g, c)
                link(act, act.activation(G, pair(0), ACT.Gelu_apprx_tanh), g_act, c + 1)
                if not last:
                    decay_exp(c + 1, 1 - p)
                act.wait_ge(lru_g, c + 1)
                act.wait_ge(accl, c)
                y = HR[:, bass.ds(c, 1), :].rearrange("p a n -> p (a n)")
                link(act, act.activation(SQ, y, ACT.Square), sql, c + 1)
                link(act, act.activation(y, y, ACT.Copy, scale=param("lru_norm", c)),
                     lru_w, c + 1)

            decay_exp(0, 0)
            with act.Fori(0, 3) as i:
                chunk(i, 0)
                chunk(i, 1)
            chunk(3, 0)
            chunk(3, 1, last=True)
            act.wait_ge(accl, 8)
            with act.Fori(0, 4) as i:
                for p in range(2):
                    j = i * 2 + p
                    act.wait_ge(z_mm[p], i + 1)
                    act.wait_ge(zy[p], i)
                    link(act, act.activation(Z[p], pair(2 * p), ACT.Silu), z_act[p], i + 1)
                    act.wait_ge(zy[p], i + 1)
                    act.wait_ge(accs, j)
                    y = XBC[:, bass.ds(j, 1), :].rearrange("p a n -> p (a n)")
                    link(act, act.activation(SQ, y, ACT.Square), sqs, j + 1)
                    link(act, act.activation(y, y, ACT.Copy, scale=param("ssd_norm", j)),
                         ssd_w, j + 1)
            act.wait_ge(ss_mm, 1)
            link(act, act.activation(stat[:, 3, :], ps[:, 6, 0:2 * TT], ACT.Sqrt,
                                     bias=eps[:, 0:1], scale=1.0 / D), devo, 1)
            for t in range(TT):
                act.wait_ge(x2_s, t + 1)
                if t >= 1:
                    act.wait_ge(h2_ready, t)
                st.link(act.activation(ACCS, X2[:, t, :], ACT.Square,
                                       accum_out=stat[:, 0, t:t + 1]))
                link(act, act.activation(stat[:, 1, t:t + 1], stat[:, 0, t:t + 1], ACT.Sqrt,
                                         bias=eps[:, 0:1], scale=1.0 / D), dev2, t + 1)
                act.wait_ge(ht2_mm, t + 1)
                if t >= 1:
                    act.wait_ge(lg_mm, t)
                link(act, act.activation(H2T.rearrange("p k n -> p (k n)"), pair(4), ACT.Copy),
                     ht2_act, t + 1)
            act.wait_ge(rt_arg, 1)
            link(act, act.activation(r_exp, r_exp, ACT.Exp), rt_exp, 1)

            def to_hi(j, b, at, slot):
                act.wait_ge(wch_in[j], b * 16 + 16)
                if not (isinstance(at, int) and at < HL):
                    act.wait_ge(ch_used, at + (1 - HL))
                act.activation(WH[slot % HL], ring[j], ACT.Copy).then_inc(hi_made, 1)

            def gates(b, used):
                act.wait_ge(ch_used, used)
                if not (isinstance(b, int) and b == 0):
                    act.wait_ge(hid_ready, b)
                act.activation(SG, ps[:, 0, :], ACT.Silu).then_inc(sg_act, 1)

            def rows_hi(b):
                act.wait_ge(xb_mm, b + 1)
                act.activation(XTH[:, :], pair(2), ACT.Copy).then_inc(xt_hi, 1)

            def hidden_hi(b):
                act.wait_ge(hidt_mm, b + 1)
                act.activation(HTH[:, :], ps[:, 4, :], ACT.Copy).then_inc(ht_hi, 1)

            def rows_out(b, used):
                act.wait_ge(ch_used, used)
                act.wait_ge(y_out, b * 16)
                act.activation(YB[:, :], pair(5), ACT.Copy).then_inc(yb_act, 1)

            rows_hi(0)
            for j in range(KT):
                to_hi(j, 0, j, j)
            gates(0, KT)
            rows_hi(1)
            for j in range(KT // 2):
                to_hi(j, 1, CH + GU_AT + j, GU_AT + j)
            hidden_hi(0)

            def turn(b, last):
                for j in range(KT // 2, KT):
                    to_hi(j, b, b * CH + (GU_AT + j), GU_AT + j)
                for j in range(KT, CH):
                    to_hi(j, b - 1, b * CH + (DN_AT - CH + j), DN_AT - CH + j)
                gates(b, b * CH + (GU_AT + KT))
                rows_hi(b + 1)
                if not last:
                    for j in range(KT // 2):
                        to_hi(j, b + 1, b * CH + (CH + GU_AT + j), GU_AT + j)
                hidden_hi(b)
                rows_out(b - 1, b * CH + DN_AT)

            with act.Fori(1, NE - 1) as b:
                turn(b, False)
            turn(NE - 1, True)
            for j in range(KT, CH):
                to_hi(j, NE - 1, DN_LAST - KT + j, DN_LAST - KT + j)
            rows_out(NE - 1, DN_LAST + KD)
            n_over = act.value_load(over_i[0:1, 15:16], min_val=0, max_val=MAX_OVER)
            with act.Fori(0, MAX_OVER) as o:
                with act.If(n_over > o):
                    for j in range(KT):
                        to_hi(j, o + NE, o * CH + (OVER_AT + j), j)
                    gates(o + NE, o * CH + (OVER_AT + KT))
                    rows_hi(o + (NE + 1))
                    for j in range(KT, CH):
                        to_hi(j, o + NE, o * CH + (OVER_AT + j), j)
                    hidden_hi(o + NE)
                    rows_out(o + NE, o * CH + (OVER_AT + CH))
            for t in range(TT):
                act.wait_ge(x3_ready, t + 1)
                st.link(act.activation(FSQ, X2[:, t, :], ACT.Square,
                                       accum_out=stat[:, 4, t:t + 1]))
                if t % 4 == 3:
                    half = slice(t - 3, t + 1)
                    link(act, act.activation(stat[:, 5, half], stat[:, 4, half], ACT.Sqrt,
                                             bias=eps[:, 0:1], scale=1.0 / D), dev3, t // 4 + 1)
            for t in range(TT):
                act.wait_ge(o_ready, t + 1)
                act.dma_start(a["out"][t], X2[:, t, :]).then_inc(out_done, 16)

        @block.vector
        def _(dve):
            st = Steps(dve, dve_step)
            st.link(dve.memset(eps[:, 0:1], EPS))
            dve.memset(eps[:, 1:2], 1e-30).then_inc(par_done, 1)
            st.link(dve.memset(ones[:, :], 1.0))
            dve.wait_ge(dev_ready, 1)
            link(dve, dve.reciprocal(stat[:, 2, 0:TT], stat[:, 1, 0:TT]), inv_ready, 1)
            dve.wait_ge(const_in, 64)
            for t in range(TT):
                dve.wait_ge(xt_ready, t + 1)
                for j in range(2):
                    dve.tensor_tensor(
                        hT[:, 4 * j:4 * j + 4, t * P:(t + 1) * P],
                        ps[:, 2 * (t % 2) + j, :].rearrange("p (k n) -> p k n", n=P),
                        pv[:, PV["norm_mix"] + 4 * j:PV["norm_mix"] + 4 * j + 4].unsqueeze(2)
                        .to_broadcast([P, 4, P]), ALU.mult).then_inc(ht_done, 1)

            def softplus_tail(v, e, s, s2, p, out):
                st.link(dve.tensor_scalar(s, e, 2.0, None, ALU.add))
                st.link(dve.reciprocal(s, s))
                st.link(dve.tensor_tensor(s, s, e, ALU.mult))
                st.link(dve.tensor_tensor(s2, s, s, ALU.mult))
                st.link(dve.tensor_scalar(p, s2, 1.0 / 15, None, ALU.mult))
                for n in (13, 11, 9, 7, 5, 3):
                    st.link(dve.scalar_tensor_tensor(p, p, 1.0 / n, s2, ALU.add, ALU.mult))
                st.link(dve.scalar_tensor_tensor(p, p, 1.0, s, ALU.add, ALU.mult))
                st.link(dve.tensor_scalar(p, p, 2.0, None, ALU.mult))
                st.link(dve.scalar_tensor_tensor(out, v, 0.0, p, ALU.max, ALU.add))

            cols = lambda name: pv[:, PV[name]:PV[name] + 8]
            st.link(dve.tensor_scalar(prep[:, 0, :], cols("lru_ba"), 0.5, None, ALU.mult))
            st.link(dve.tensor_scalar(prep[:, 1, :], cols("lru_bx"), 0.5, None, ALU.mult))
            dve.wait_ge(xn_ready, TT)
            st.link(dve.tensor_scalar(lsp[:, 0, :], cols("lam"), -1.0, None, ALU.mult))
            link(dve, dve.scalar_tensor_tensor(lsp[:, 1, :], lsp[:, 0, :], -1.0, lsp[:, 0, :],
                                               ALU.mult, ALU.min), sp_arg, 1)
            dve.wait_ge(sp_exp, 1)
            softplus_tail(*(lsp[:, k, :] for k in (0, 2, 3, 4, 5)), prep[:, 2, :])
            st.link(dve.tensor_scalar(prep[:, 3, :], prep[:, 2, :], 4.0, None, ALU.mult))
            st.link(dve.tensor_scalar(prep[:, 2, :], prep[:, 2, :], -4.0, None, ALU.mult))
            st.link(dve.memset(smask, 1.0))
            st.link(dve.memset(smask.rearrange("h (c l) -> h c l", l=P)[:, :, 0], 0.0))
            dve.wait_ge(dt_v, 1)
            link(dve, dve.scalar_tensor_tensor(sv["nab"], sv["v"], -1.0, sv["v"],
                                               ALU.mult, ALU.min), sp_arg, 2)
            dve.wait_ge(sp_exp, 2)
            softplus_tail(*(sv[n] for n in ("v", "e", "s", "s2", "p")), DT)
            st.link(dve.tensor_scalar(sv["s"], DT, hpar[:, 1:2], -1.0, ALU.mult, ALU.mult))
            st.link(dve.tensor_tensor_scan(ACS, smask, sv["s"], 0.0, ALU.mult, ALU.add))
            acs3 = ACS.rearrange("h (c l) -> h c l", l=P)
            link(dve, dve.tensor_tensor(sv["p"].rearrange("h (c l) -> h c l", l=P),
                                        acs3[:, :, P - 1:P].to_broadcast([NH, TT, P]), acs3,
                                        ALU.subtract), sp_arg, 3)
            dve.wait_ge(sp_exp, 5)
            st.link(dve.tensor_tensor(WD, WD, DT, ALU.mult))
            link(dve, dve.tensor_tensor(
                dd, ident[0:NH, 0:NH].unsqueeze(1).to_broadcast([NH, TT, NH]),
                dec16.unsqueeze(2).to_broadcast([NH, TT, NH]), ALU.mult), dt_ready, 1)

            def taps(acc, bank, name, i, stride, last_sem, count, col=0):
                for back in (1, 2, 3):
                    w = param(name, i, stride * (3 - back) + col)
                    ins = dve.scalar_tensor_tensor(
                        acc[:, back:], pair(bank)[:, 0:SEQ - back], w, acc[:, back:],
                        ALU.mult, ALU.add)
                    if back < 3:
                        st.link(ins)
                    else:
                        link(dve, ins, last_sem, count)

            with dve.Fori(0, 8) as i:
                st.begin(i, 8)
                dve.wait_ge(tap_u, i + 1)
                taps(U, 4, "lru_cw", i, 8, u_ready, i + 1)
                dve.wait_ge(tap_e, i + 1)
                taps(XE, 0, "ssd_cw", i * 2, 16, cv_e, i + 1)
                dve.wait_ge(a2_act, i + 1)
                link(dve, dve.scalar_tensor_tensor(A2, A2, 1.0, TG, ALU.add, ALU.mult),
                     m2_ready, i + 1)
                st.link(dve.scalar_tensor_tensor(Q, TI, 1.0, U, ALU.add, ALU.mult))
                dve.wait_ge(sq_act, i + 1)
                st.link(dve.scalar_tensor_tensor(Q, Q, 0.5, A2, ALU.mult, ALU.mult))
                link(dve, dve.tensor_tensor_scan(
                    HR[:, bass.ds(i, 1), :].rearrange("p a n -> p (a n)"), AA, Q, 0.0,
                    ALU.mult, ALU.add), lru_done, i + 1)
                dve.wait_ge(tap_o, i + 1)
                taps(XO, 2, "ssd_cw", i * 2, 16, cv_o, i + 1, 1)
            st.end(8)
            dve.wait_ge(prep_mm, 1)
            link(dve, dve.tensor_copy(colv.rearrange("p q c h -> p (q c h)"),
                                      ps[:, 0, 0:3 * TT * NH]), prep_done, 1)
            dve.wait_ge(prep_mm, 2)
            link(dve, dve.tensor_copy(decb.rearrange("p c h -> p (c h)"),
                                      ps[:, 1, 0:TT * NH]), prep_done, 2)
            dve.wait_ge(sq_act, 8)
            dve.wait_ge(gt_mm, 16)
            dve.wait_ge(scr_out, 32)
            st.link(dve.memset(STATE, 0.0))
            dve.wait_ge(late_in, 32)
            s3 = lambda t, n=P: t.rearrange("p (a n) -> p a n", n=n)
            def decay_min(c, p):
                dve.wait_ge(diff_ready, c + 1)
                link(dve, dve.tensor_scalar(L[p], L[p], 0.0, None, ALU.min), min_ready, c + 1)

            def chunk(i, p, last=False):
                c = i * 2 + p
                col = lambda q: colv[:, q, bass.ds(c, 1), :].rearrange(
                    "p a h -> p (a h)").unsqueeze(2).to_broadcast([P, NH, HD])
                dve.wait_ge(ts_mm, c + 1)
                dve.wait_ge(y_mm[1 - p], i + p)
                dve.wait_ge(st_mm, c)
                st.link(dve.tensor_tensor(s3(XDT, HD), s3(pair(2), HD), col(1), ALU.mult))
                link(dve, dve.tensor_tensor(s3(XW, HD), s3(pair(2), HD), col(2), ALU.mult),
                     xw_ready, c + 1)
                link(dve, dve.tensor_tensor(SM, s3(ps[:, 5, :]), tri.unsqueeze(1)
                                            .to_broadcast([P, NG, P]), ALU.mult),
                     sm_ready, c + 1)
                dve.wait_ge(e_ready, c + 1)
                link(dve, dve.tensor_tensor(
                    L[p].rearrange("p (g k) l -> p g k l", g=NG),
                    L[p].rearrange("p (g k) l -> p g k l", g=NG),
                    SM.unsqueeze(2).to_broadcast([P, NG, NG, P]), ALU.mult),
                    m_ready, c + 1)
                dve.wait_ge(yo_mm, c + 1)
                st.link(dve.tensor_tensor(s3(STATE, HD), s3(STATE, HD),
                                          decb[:, bass.ds(c, 1), :].rearrange(
                                              "p a h -> p (a h)").unsqueeze(2)
                                          .to_broadcast([P, NH, HD]), ALU.mult))
                dve.wait_ge(st_mm, c + 1)
                link(dve, dve.tensor_tensor(STATE, STATE, pair(6), ALU.add), st_upd, c + 1)
                dve.wait_ge(ea_in, c * 32 + 32)
                st.link(dve.tensor_tensor(s3(YT), s3(pair(4)), EAB, ALU.mult))
                dve.wait_ge(y_mm[p], i + 1)
                st.link(dve.tensor_tensor(YT, YT, pair(2), ALU.add))
                dve.wait_ge(xd_ready, c + 1)
                y = XBC[:, 0:KT, bass.ds(c * P, P)]
                link(dve, dve.tensor_tensor(y, y, s3(YT), ALU.add), comb, c + 1)
                if not last:
                    decay_min(c + 1, 1 - p)
                dve.wait_ge(g_act, c + 1)
                y = HR[:, bass.ds(c, 1), :].rearrange("p a n -> p (a n)")
                link(dve, dve.tensor_tensor(y, y, G, ALU.mult), lru_g, c + 1)

            decay_min(0, 0)
            with dve.Fori(0, 3) as i:
                st.begin(i, 8)
                chunk(i, 0)
                chunk(i, 1)
            st.end(3)
            chunk(3, 0)
            chunk(3, 1, last=True)
            with dve.Fori(0, 4) as i:
                for p in range(2):
                    dve.wait_ge(z_act[p], i + 1)
                    y = XBC[:, bass.ds(i * 2 + p, 1), :].rearrange("p a n -> p (a n)")
                    link(dve, dve.tensor_tensor(y, y, Z[p], ALU.mult), zy[p], i + 1)

            def logits(t):
                dve.wait_ge(lg_mm, t + 1)
                link(dve, dve.tensor_tensor(LG[:, t, :], ps[:, 6, 0:NR], nrow[:, 2 * D:],
                                            ALU.add), lg_done, t + 1)

            dve.wait_ge(late_in, 64)
            dve.wait_ge(devo, 1)
            link(dve, dve.reciprocal(stat[:, 4, :], stat[:, 3, :]), invo, 1)
            for t in range(TT):
                dve.wait_ge(wol_mm, t + 1)
                dve.wait_ge(xr_in[t % 2], 16 * (t // 2 + 1))
                link(dve, dve.scalar_tensor_tensor(X2[:, t, :], pair(0), stat[:, 4, t:t + 1],
                                                   XR[t % 2], ALU.mult, ALU.add), x2_l, t + 1)
                dve.wait_ge(wos_mm, t + 1)
                link(dve, dve.scalar_tensor_tensor(X2[:, t, :], pair(2),
                                                   stat[:, 4, TT + t:TT + t + 1],
                                                   X2[:, t, :], ALU.mult, ALU.add), x2_s, t + 1)
                dve.wait_ge(dev2, t + 1)
                st.link(dve.reciprocal(stat[:, 2, t:t + 1], stat[:, 1, t:t + 1]))
                if t >= 2:
                    dve.wait_ge(h2_out[t % 2], 16 * (t // 2))
                    dve.wait_ge(ht2_mm, t - 1)
                link(dve, dve.scalar_tensor_tensor(H2[t % 2], X2[:, t, :], stat[:, 2, t:t + 1],
                                                   nrow[:, 0:D], ALU.mult, ALU.mult),
                     h2_ready, t + 1)
                if t >= 1:
                    logits(t - 1)
            logits(TT - 1)
            b3 = lambda t, w: t.unsqueeze(2).to_broadcast([P, TT, w])

            def first_max(vals, w, mx, eq, pos, out):
                st.link(dve.tensor_reduce(mx, vals, AX_X, ALU.max))
                st.link(dve.tensor_tensor(eq, vals, b3(mx, w), ALU.is_equal))
                st.link(dve.tensor_tensor(pos, eq, falling[:, 0:w].unsqueeze(1)
                                          .to_broadcast([P, TT, w]), ALU.mult))
                st.link(dve.tensor_reduce(r_pm, pos, AX_X, ALU.max))
                st.link(dve.tensor_tensor(out, pos, b3(r_pm, w), ALU.is_equal))

            coarse, fine = LG[:, :, 0:MG], LG[:, :, MG:NR].rearrange("p t (g e) -> p t g e", e=EG)
            first_max(coarse, MG, r_cmax, r_eq, r_pos, r_oh)
            st.link(dve.tensor_tensor(r_exp[:, 0:TT * MG].rearrange("p (t g) -> p t g", g=MG),
                                      coarse, b3(r_cmax, MG), ALU.subtract))
            st.link(dve.tensor_tensor(r_fo, fine, r_oh.unsqueeze(3).to_broadcast(
                [P, TT, MG, EG]), ALU.mult))
            st.link(dve.tensor_reduce(r_f, r_fo.rearrange("p t g e -> p t e g"), AX_X, ALU.add))
            first_max(r_f, EG, r_m1, r_eq8, r_pos8, r_o[0])
            st.link(dve.scalar_tensor_tensor(r_f2, r_o[0], -1e30, r_f, ALU.mult, ALU.add))
            first_max(r_f2, EG, r_m2, r_eq8, r_pos8, r_o[1])
            link(dve, dve.tensor_tensor(r_exp[:, TT * MG:], r_m2, r_m1, ALU.subtract), rt_arg, 1)
            for k in range(2):
                st.link(dve.tensor_tensor(
                    r_M[k].rearrange("p t (g e) -> p t g e", e=EG),
                    r_oh.unsqueeze(3).to_broadcast([P, TT, MG, EG]),
                    r_o[k].unsqueeze(2).to_broadcast([P, TT, MG, EG]), ALU.mult))
            st.link(dve.tensor_tensor(r_sum, r_M[0], r_M[1], ALU.add))
            st.link(dve.memset(r_pre[:, 0, :], 0.0))
            for t in range(1, TT):
                st.link(dve.tensor_tensor(r_pre[:, t, :], r_pre[:, t - 1, :], r_sum[:, t - 1, :],
                                          ALU.add))
            link(dve, dve.tensor_tensor(r_tot, r_pre[:, TT - 1, :], r_sum[:, TT - 1, :],
                                        ALU.add), rk_in, 1)
            dve.wait_ge(rt_exp, 1)
            st.link(dve.tensor_reduce(r_gw, r_exp[:, 0:TT * MG].rearrange(
                "p (t g) -> p t g", g=MG), AX_X, ALU.add))
            st.link(dve.scalar_tensor_tensor(r_w1, r_exp[:, TT * MG:], 1.0, r_gw, ALU.add,
                                             ALU.mult))
            st.link(dve.reciprocal(wts[:, 0, :], r_w1))
            st.link(dve.tensor_tensor(wts[:, 1, :], wts[:, 0, :], r_exp[:, TT * MG:], ALU.mult))
            dve.wait_ge(rk_mm, 1)

            def per_choice(table, out):
                for k in range(2):
                    st.link(dve.tensor_tensor(r_tmp, r_M[k], table, ALU.mult))
                    st.link(dve.tensor_reduce(out[:, k * TT:(k + 1) * TT], r_tmp, AX_X, ALU.add))

            def multiples(vals, op, out):
                st.link(dve.tensor_scalar(out, vals, float(P), None, op))
                for m in range(2, TT):
                    st.link(dve.scalar_tensor_tensor(out, vals, float(P * m), out, op, ALU.add))

            per_choice(s3(ps[:, 7, 0:TT * NE], NE), r_rk)
            st.link(dve.tensor_copy(r_cnt, ps[:, 7, TT * NE:TT * NE + NE]))
            multiples(r_rk, ALU.is_ge, r_J)
            st.link(dve.scalar_tensor_tensor(r_slot, r_J, -float(P), r_rk, ALU.mult, ALU.add))
            multiples(r_cnt, ALU.is_gt, r_nov)
            st.link(dve.tensor_tensor_scan(r_oinc, ones[:, 0:NE], r_nov, 0.0, ALU.mult, ALU.add))
            st.link(dve.tensor_tensor(r_ost, r_oinc, r_nov, ALU.subtract))
            bt = lambda row: row.unsqueeze(1).to_broadcast([P, TT, NE])
            per_choice(bt(r_ost), r_os)
            per_choice(bt(iota[:, 0:NE]), r_eid)
            st.link(dve.tensor_tensor(r_os, r_os, r_J, ALU.add))
            st.link(dve.tensor_tensor(r_os, r_os, r_eid, ALU.subtract))
            st.link(dve.tensor_scalar(r_g, r_J, 0.0, None, ALU.is_gt))
            st.link(dve.scalar_tensor_tensor(r_os, r_os, NE - 1.0, r_g, ALU.add, ALU.mult))
            st.link(dve.tensor_tensor(r_blk, r_os, r_eid, ALU.add))
            bn = lambda t, w: t.unsqueeze(2).to_broadcast([P, 2 * TT, w])
            bi = lambda w: iota[:, 0:w].unsqueeze(1).to_broadcast([P, 2 * TT, w])
            st.link(dve.tensor_tensor(r_A, bi(P), bn(r_slot, P), ALU.is_equal))
            st.link(dve.tensor_tensor(r_B[:, :, 1, :], bi(NBLK), bn(r_blk, NBLK), ALU.is_equal))
            st.link(dve.tensor_tensor(r_B[:, :, 0, :], r_B[:, :, 1, :], bn(rowid1, NBLK),
                                      ALU.mult))
            for k in range(2):
                half = r_B[:, k * TT:(k + 1) * TT, 1, :]
                ins = dve.tensor_tensor(half, half, b3(tokid, NBLK), ALU.mult)
                if k == 0:
                    st.link(ins)
                else:
                    link(dve, ins, ab_in, 1)
            st.link(dve.tensor_tensor(r_ge, iota[:, 0:16].unsqueeze(2).to_broadcast([P, 16, NE]),
                                      r_oinc.unsqueeze(1).to_broadcast([P, 16, NE]), ALU.is_ge))
            st.link(dve.tensor_reduce(over[:, :], r_ge, AX_X, ALU.add))
            st.link(dve.tensor_scalar(over[:, :], over[:, :], NE - 1.0, None, ALU.min))
            st.link(dve.tensor_copy(over[:, 15:16], r_oinc[:, NE - 1:NE]))
            st.link(dve.tensor_copy(over_i[:, :], over[:, :]))
            dve.wait_ge(tab_mm, 1)
            st.link(dve.tensor_scalar(tab_f[:, 0, :], ps[:, 7, 0:NBLK], 0.0, 8192.0,
                                      ALU.is_equal, ALU.mult))
            st.link(dve.tensor_tensor(tab_f[:, 1, :], ps[:, 7, NBLK:2 * NBLK], tab_f[:, 0, :],
                                      ALU.add))
            st.link(dve.scalar_tensor_tensor(tab_f[:, 0, :], ps[:, 7, 0:NBLK], -1.0,
                                             tab_f[:, 0, :], ALU.add, ALU.add))
            link(dve, dve.tensor_copy(tab_i[:, :, :], tab_f[:, :, :]), tab_ready, 1)

            def normed_rows(half):
                at = slice(4 * half, 4 * half + 4)
                dve.wait_ge(dev3, half + 1)
                st.link(dve.reciprocal(stat[:, 6, at], stat[:, 5, at]))
                for t in range(4 * half, 4 * half + 4):
                    dve.scalar_tensor_tensor(X2[:, t, :], X2[:, t, :], stat[:, 6, t:t + 1],
                                             nrow[:, D:2 * D], ALU.mult, ALU.mult
                                             ).then_inc(o_ready, 1)

            def to_lo(j, at, slot):
                dve.wait_ge(hi_made, at + 1)
                dve.tensor_tensor(WL[slot % HL], ring[j], WH[slot % HL].bitcast(F32),
                                  ALU.subtract).then_inc(lo_made, 1)

            def hidden(b):
                dve.wait_ge(sg_act, b + 1)
                dve.tensor_tensor(HID, SG, ps[:, 1, :], ALU.mult).then_inc(hid_ready, 1)

            def rows_lo(b):
                dve.wait_ge(xt_hi, b + 1)
                dve.tensor_tensor(XTL[:, :], pair(2), XTH[:, :].bitcast(F32),
                                  ALU.subtract).then_inc(xt_lo, 1)

            def hidden_lo(b):
                dve.wait_ge(ht_hi, b + 1)
                dve.tensor_tensor(HTL[:, :], ps[:, 4, :], HTH[:, :].bitcast(F32),
                                  ALU.subtract).then_inc(ht_lo, 1)

            rows_lo(0)
            for j in range(KT):
                to_lo(j, j, j)
            hidden(0)
            rows_lo(1)
            for j in range(KT // 2):
                to_lo(j, CH + GU_AT + j, GU_AT + j)
            hidden_lo(0)

            def turn(b, last):
                for j in range(KT // 2, KT):
                    to_lo(j, b * CH + (GU_AT + j), GU_AT + j)
                for j in range(KT, CH):
                    to_lo(j, b * CH + (DN_AT - CH + j), DN_AT - CH + j)
                hidden(b)
                rows_lo(b + 1)
                if not last:
                    for j in range(KT // 2):
                        to_lo(j, b * CH + (CH + GU_AT + j), GU_AT + j)
                hidden_lo(b)

            with dve.Fori(1, NE - 1) as b:
                turn(b, False)
            turn(NE - 1, True)
            for j in range(KT, CH):
                to_lo(j, DN_LAST - KT + j, DN_LAST - KT + j)
            n_over = dve.value_load(over_i[0:1, 15:16], min_val=0, max_val=MAX_OVER)
            with dve.Fori(0, MAX_OVER) as o:
                with dve.If(n_over > o):
                    for j in range(KT):
                        to_lo(j, o * CH + (OVER_AT + j), j)
                    hidden(o + NE)
                    rows_lo(o + (NE + 1))
                    for j in range(KT, CH):
                        to_lo(j, o * CH + (OVER_AT + j), j)
                    hidden_lo(o + NE)
            for t in range(TT):
                dve.wait_ge(yl_in[t % 2], 16 * (t // 2 + 1))
                for k in range(2):
                    ins = dve.scalar_tensor_tensor(X2[:, t, :], YL[t % 2][:, k, :],
                                                   wts[:, k, t:t + 1], X2[:, t, :],
                                                   ALU.mult, ALU.add)
                    if k == 0:
                        st.link(ins)
                    else:
                        ins.then_inc(x3_ready, 1)
                if t == 5:
                    normed_rows(0)
            normed_rows(1)

        @block.gpsimd
        def _(pool):
            st = Steps(pool, pool_step)
            pool.wait_ge(dt_ready, 1)
            pool.wait_ge(sp_exp, 4)
            pool.dma_start(acs_d, ACS).then_inc(scr_out, 16)
            pool.dma_start(ea_d, EA).then_inc(scr_out, 16)
            pool.wait_ge(lru_done, 8)
            st.link(pool.memset(ACCL, 0.0))
            dch = pv[:, PV["ssd_d"]:PV["ssd_d"] + KT].unsqueeze(2).to_broadcast([P, KT, P])
            def decays(c, p, i):
                pool.wait_ge(l_in[p], i * 16 + 16)
                link(pool, pool.tensor_tensor(
                    L[p], L[p], colv[:, 0, bass.ds(c, 1), :].rearrange("p a h -> p (a h)")
                    .unsqueeze(2).to_broadcast([P, NH, P]), ALU.subtract), diff_ready, c + 1)

            def chunk(i, p, last=False):
                c = i * 2 + p
                pool.wait_ge(xc_in, c * 16 + 16)
                y = XBC[:, 0:KT, bass.ds(c * P, P)]
                link(pool, pool.tensor_tensor(y, y, dch, ALU.mult), xd_ready, c + 1)
                if not last:
                    decays(c + 1, 1 - p, i + p)
                pool.wait_ge(sql, c + 1)
                link(pool, pool.tensor_tensor(ACCL, ACCL, SQ, ALU.add), accl, c + 1)

            decays(0, 0, 0)
            with pool.Fori(0, 3) as i:
                chunk(i, 0)
                chunk(i, 1)
            chunk(3, 0)
            chunk(3, 1, last=True)
            pool.wait_ge(y_mm[1], 4)
            st.link(pool.memset(ACCS, 0.0))
            with pool.Fori(0, 8) as j:
                pool.wait_ge(sqs, j + 1)
                link(pool, pool.tensor_tensor(ACCS, ACCS, SQ, ALU.add), accs, j + 1)
            pool.wait_ge(tab_ready, 1)
            pool.wait_ge(h2_out[0], 16 * TT // 2)
            pool.wait_ge(h2_out[1], 16 * TT // 2)
            pool.wait_ge(wos_mm, TT)

            one = ones[:, 0:1]

            def gather(b):
                if not (isinstance(b, int) and b == 0):
                    pool.wait_ge(xb_mm, b)
                st.link(pool.tensor_copy(idx_g[:, :], tab_i[:, 1, bass.ds(b, 1)]))
                pool.tensor_tensor(pad[:, 0:1], one, one, ALU.mult)
                pool.indirect_dma_start(
                    out=XB[:, :], out_offset=None, in_=h2_d,
                    in_offset=bass.IndirectOffsetOnAxis(ap=idx_g[:, 0:1], axis=0),
                    bounds_check=SEQ - 1, oob_is_err=False).then_inc(xb_in, 16)

            def scatter(b):
                pool.wait_ge(yb_act, b + 1)
                pool.wait_ge(y_out, b * 16)
                st.link(pool.tensor_copy(idx_s[:, :], tab_i[:, 0, bass.ds(b, 1)]))
                pool.tensor_tensor(pad[:, 1:2], one, one, ALU.mult)
                pool.indirect_dma_start(
                    out=y_d, out_offset=bass.IndirectOffsetOnAxis(ap=idx_s[:, 0:1], axis=0),
                    in_=YB[:, :], in_offset=None, bounds_check=2 * SEQ - 1,
                    oob_is_err=False).then_inc(y_out, 16)

            st.link(pool.memset(XB[:, :], 0.0))
            gather(0)
            gather(1)
            with pool.Fori(1, NE) as b:
                st.begin(b - 1, 2)
                gather(b + 1)
                scatter(b - 1)
            st.end(NE - 1)
            scatter(NE - 1)
            n_over = pool.value_load(over_i[0:1, 15:16], min_val=0, max_val=MAX_OVER)
            with pool.Fori(0, MAX_OVER) as o:
                with pool.If(n_over > o):
                    st.begin(o, 2)
                    gather(o + (NE + 1))
                    scatter(o + NE)
            pool.wait_ge(y_out, n_over * 16 + NE * 16)
            pool.wait_ge(scr_out, 32)


def kernel(**inputs):
    import concourse.bacc as bacc
    from concourse.bass_utils import run_bass_kernel_spmd

    f = {k: np.asarray(v) for k, v in inputs.items()}
    rows = lambda v: v.reshape(-1, P).T
    w_in = f["w_in"][0]
    win = w_in[:, :DT_COL].reshape(KT, P, N_IN, P).transpose(2, 1, 0, 3).reshape(N_IN, P, KT * P)
    wdt = w_in[:, DT_COL:].reshape(KT, P, NH).transpose(1, 0, 2)
    wblk = np.zeros((KT, P, 2, P), np.float32)
    for g, name in enumerate(("lru_wa", "lru_wx")):
        for q in range(2):
            s = slice(HD * q, HD * (q + 1))
            wblk[:, s, g, s] = f[name][0].reshape(KT, 2, HD, HD)[:, q]
    pv = np.concatenate([
        rows(f["norm_mix"][0]), rows(f["lru_conv_w"][0]), rows(f["lru_conv_b"][0]),
        rows(f["lru_ba"][0].reshape(-1)), rows(f["lru_bx"][0].reshape(-1)),
        rows(f["lru_lambda"][0]), rows(f["lru_norm"][0]), rows(f["ssd_norm"][0]),
        rows(f["ssd_conv_w"][0]), rows(f["ssd_conv_b"][0]),
        rows(np.repeat(f["ssd_d"][0], HD))], axis=1)
    hpar = np.stack([f["ssd_dt_bias"][0], f["ssd_a_log"][0]], axis=1)
    wout = f["w_out"][0].reshape(2 * KT, P, D).transpose(1, 0, 2)
    fine = f["w_fine"][0].transpose(1, 0, 2).reshape(D, NE)
    wr = np.concatenate([f["w_coarse"][0], fine], axis=1).reshape(KT, P, NR).transpose(1, 0, 2)
    nrow = np.concatenate([f["norm_ffn"][0], f["final_norm"], f["b_coarse"][0],
                           f["b_fine"][0].reshape(-1)])
    gu = np.stack([f["w_gate"][0].reshape(NE, KT, P, DE), f["w_up"][0].reshape(NE, KT, P, DE)],
                  axis=3).reshape(NE, KT, P, 2 * DE)
    moe = np.concatenate([gu, f["w_down"][0].reshape(NE, DE // P, P, D)], axis=1)
    n = np.arange(P, dtype=np.float32)
    tok = np.arange(TT)[None, :] * P + np.arange(P)[:, None]
    cst = np.concatenate([
        np.broadcast_to(n, (P, P)), 2 * tok + 1, 2 * tok + 2, tok,
        np.broadcast_to(EG - np.arange(EG), (P, EG)), n[:, None] < n[None, :]],
        axis=1).astype(np.float32)
    tri = (n[None, :] >= n[:, None]).astype(np.float32)
    arrays = {
        "x": f["x"].reshape(TT, P, D), "win": win, "wdt": wdt, "wblk": wblk, "pv": pv,
        "hpar": hpar, "wout": wout, "wr": wr, "nrow": nrow, "moe": moe.reshape(NE * CH, P, D),
        "cst": cst, "tri": tri, "ident": np.eye(P, dtype=np.float32)}
    nc = bacc.Bacc("TRN2", target_bir_lowering=False, num_devices=1)
    a, feeds = {}, {}
    for name, v in arrays.items():
        feeds["in_" + name] = np.ascontiguousarray(v)
        a[name] = nc.dram_tensor("in_" + name, v.shape, F32, kind="ExternalInput").ap()
    a["out"] = nc.dram_tensor("out_x", (TT, P, D), F32, kind="ExternalOutput").ap()
    build(nc, a)
    r = run_bass_kernel_spmd(nc, [feeds], core_ids=[0])
    return r.results[0]["out_x"].reshape(1, SEQ, D)
```

```python
from contextlib import ExitStack

import numpy as np

import concourse.bass as bass
from concourse import mybir

F32 = mybir.dt.float32
F32R = mybir.dt.float32r
I32 = mybir.dt.int32
ALU = mybir.AluOpType
ACT = mybir.ActivationFunctionType
AX_X = mybir.AxisListType.X

P = 128
D = 1024
SEQ = 1024
KT = D // P
TT = SEQ // P
NH = 16
HD = 64
NG = 4
CONV_K = 4
MG, EG = 4, 8
NE = MG * EG
DE = 512
EPS = 1e-6
DT_COL = 5 * D
GR = KT * P // 2
RAW, SPL = 5, 2
B_AT = 4
B_PER = 10
N_GR = B_AT + 8 * B_PER - 2
W_ORDER = list(range(2 * KT)) + [n + q * KT for n in range(2 * KT, 3 * KT) for q in range(2)]
NR = MG + NE
MAX_OVER = 15
NBLK = NE + MAX_OVER + 1
CH = KT + DE // P
KD = DE // P
HL = 6
GU_AT, DN_AT = KT - CH, KT
DN_LAST = (NE - 1) * CH + KT
OVER_AT = NE * CH

PV_SIZES = dict(norm_mix=8, lru_cw=32, lru_cb=8, lru_ba=8, lru_bx=8, lam=8, lru_norm=8,
                ssd_norm=8, ssd_cw=64, ssd_cb=16, ssd_d=8)
PV = {}
for _n, _s in PV_SIZES.items():
    PV[_n] = sum(PV_SIZES[m] for m in list(PV_SIZES)[:list(PV_SIZES).index(_n)])
NPV = sum(PV_SIZES.values())


class Steps:

    def __init__(self, eng, sem):
        self.eng, self.sem, self.done, self.turn = eng, sem, 0, None

    def link(self, ins):
        ins.then_inc(self.sem, 1)
        self.done += 1
        self.eng.wait_ge(self.sem, self.done if self.turn is None else self.turn + self.done)

    def begin(self, i, per):
        self.turn, self.first, self.per = i * per, self.done, per

    def end(self, trips):
        assert self.done - self.first == self.per, (self.done - self.first, self.per)
        self.turn, self.done = None, self.first + trips * self.per


def link(eng, ins, sem, value):
    ins.then_inc(sem, 1)
    eng.wait_ge(sem, value)


def wait(eng, sem, value):
    if not (isinstance(value, int) and value <= 0):
        eng.wait_ge(sem, value)


def turns(eng, first, count, body, st=None, per=0):
    body(first)
    with eng.Fori(first + 1, first + count - 1) as i:
        if st:
            st.begin(i - (first + 1), per)
        body(i)
    if st:
        st.end(count - 2)
    body(first + count - 1)


def overflow_blocks(eng, n_over, body):
    def some(lo, hi):
        with eng.Fori(lo, hi) as o:
            with eng.If(n_over > o):
                body(o)

    some(0, 3)
    with eng.If(n_over > 3):
        some(3, MAX_OVER)


def build(nc, a):
    with ExitStack() as ctx:
        def sb(name, shape, dt=F32):
            return ctx.enter_context(nc.sbuf_tensor(name, shape, dt))

        def sem(name):
            return ctx.enter_context(nc.semaphore(name))

        def dram(name, shape):
            return nc.dram_tensor(name, shape, F32).ap()

        acs_d, ea_d = dram("acs_d", [NH, SEQ]), dram("ea_d", [NH, SEQ])
        z_d = dram("z_d", [D, SEQ])
        h2_d, y_d = dram("h2_d", [SEQ, D]), dram("y_d", [2 * SEQ, D])

        ps = ctx.enter_context(nc.psum_tensor("ps", [P, 8, 512], F32))

        def pair(b):
            return ps[:, b:b + 2, :].rearrange("p b n -> p (b n)")

        pv = sb("pv", [P, NPV])
        ident = sb("ident", [P, P])
        ones = sb("ones", [P, P])
        prep = sb("prep", [P, 4, 8])
        eps = sb("eps", [P, 2])
        stat = sb("stat", [P, 8, 16])
        cst = sb("cst", [P, 128 + 16 + 8 + 128])
        tri = sb("tri", [P, P])
        tab_f = sb("tab_f", [P, 2, NBLK])
        tab_i = sb("tab_i", [P, 2, NBLK], I32)
        over = sb("over", [P, 16])
        over_i = sb("over_i", [P, 16], I32)
        wts = sb("wts", [P, 2, TT])
        pad = sb("pad", [P, 2])
        idx_g, idx_s = sb("idx_g", [P, 1], I32), sb("idx_s", [P, 1], I32)

        mixer = ExitStack()

        def hold(stack, name, shape, dt=F32):
            return stack.enter_context(nc.sbuf_tensor(name, shape, dt))

        XBC = hold(mixer, "XBC", [P, 16, SEQ])
        HR = hold(mixer, "HR", [P, KT, SEQ])

        def area_of(tile):
            def area(at, *dims):
                n = int(np.prod(dims))
                assert at + n <= tile.shape[1], (at, dims)
                t = tile[:, at:at + n]
                if len(dims) == 2:
                    return t.rearrange("p (a b) -> p a b", b=dims[1])
                if len(dims) == 3:
                    return t.rearrange("p (a b c) -> p a b c", b=dims[1], c=dims[2])
                return t
            return area

        first = ExitStack()
        XH = hold(first, "XH", [P, KT, SEQ], F32R)
        XL = hold(first, "XL", [P, KT, SEQ], F32R)
        tmp = hold(first, "tmp", [P, 8448])
        GH = hold(first, "GH", [P, SPL, GR], F32R)
        GL = hold(first, "GL", [P, SPL, GR], F32R)
        area = area_of(tmp)
        TR, AA, TI, A2, G = (area(1024 * k, D) for k in range(5))
        raw = area(5120, RAW, GR)
        colv = area(7680, 3, TT, NH)
        decb = area(8064, TT, NH)
        wblk = area(8192, 2, P)
        xall = XBC[:, 6:14, :]
        xn = [HR[:, k, :] for k in range(2)]
        HF = [HR[:, 2 + k, :].rearrange("p (k n) -> p k n", n=P) for k in range(2)]
        junk = HR[:, 4, :]
        NS = TT * NH
        sv = {n: HR[:, 5, 136 * k:136 * (k + 1)] for k, n in
              enumerate(["v", "nab", "e", "s", "s2", "p", "out"])}
        hrow = junk[:, 0:2 * NH].rearrange("p (a b) -> p a b", b=NH)
        VR, ACS, EA = HR[0:NH, 6, :], HR[0:NH, 7, :], XBC[0:NH, 15, :]
        first.close()

        second = ExitStack()
        c_hi = hold(second, "c_hi", [P, 8 * D])
        YLH = hold(second, "YLH", [P, KT, SEQ], F32R)
        c_lo = hold(second, "c_lo", [P, 8448 + 2 * SPL * GR])
        area = area_of(c_hi)
        XDT, XW, SQL = area(0, D), area(1024, D), area(2048, D)
        BT, SM = area(3072, NG, P), area(3584, NG, P)
        EAB, STATE, YT, SQ = area(4096, KT, P), area(5120, D), area(6144, D), area(7168, D)
        area = area_of(c_lo)
        ZC = [area(1024 * k, KT, P) for k in range(2)]
        L = [area(2048, NH, P), area(8448, NH, P)]
        ACCL, ACCS = area(4096, D), area(5120, D)
        XC = area(6144, 12, P)
        XR = [area(at, 512) for at in (0, 512, 1024, 1536, 4096, 4608, 5120, 5632)]
        H2 = [area(0, D), area(1024, D)]
        H2T = area(4096, KT, P)
        JUNK = area(5120, D)
        wraw = area(6144, 3, 512)
        second.close()
        mixer.close()

        third = ExitStack()
        YSL = hold(third, "YSL", [P, KT, SEQ], F32R)
        hold(third, "over_x2", [P, KT, SEQ])
        YLL = hold(third, "YLL", [P, KT, SEQ], F32R)
        YSH = hold(third, "YSH", [P, KT, SEQ], F32R)
        LW = hold(third, "LW", [P, 2, KT, 512], F32R)
        hold(third, "over_h2", [P, 2048])
        SW = hold(third, "SW", [P, 2, 2, 512], F32R)
        third.close()

        iota, rowid1 = cst[:, 0:P], cst[:, P:P + 16]
        falling, above = cst[:, P + 16:P + 24], cst[:, P + 24:2 * P + 24]

        ring_dn = sb("ring_dn", [P, KD, D])
        split_b = sb("split_b", [P, 4, D], F32R)
        X2 = sb("X2", [P, TT, D])
        ring_gu = sb("ring_gu", [P, KT, D])
        XB, YB, SGH = sb("XB", [P, D]), sb("YB", [P, D]), sb("SGH", [P, 2 * DE])
        SG, HID = SGH[:, 0:DE], SGH[:, DE:2 * DE]
        XTH, XTL = sb("XTH", [P, D], F32R), sb("XTL", [P, D], F32R)
        HTH, HTL = sb("HTH", [P, DE], F32R), sb("HTL", [P, DE], F32R)
        split_a = sb("split_a", [P, 2, D], F32R)
        late = sb("late", [P, 8, D])
        split_c = sb("split_c", [P, 6, D], F32R)
        stay = sb("stay", [P, 8448 + 2 * SPL * GR - 6 * D])
        ring = [ring_gu[:, j, :] if j < KT else ring_dn[:, j - KT, :] for j in range(CH)]
        parts = [t[:, n, :] for t, m in ((split_a, 2), (split_b, 4), (split_c, 6))
                 for n in range(m)]
        WH, WL = parts[0::2], parts[1::2]
        wr = stay[:, 1536:1536 + KT * NR].rearrange("p (k n) -> p k n", n=NR)
        LG = stay[:, 1824:1824 + TT * NR].rearrange("p (t n) -> p t n", n=NR)
        nrow = stay[:, 2112:2112 + 2 * D + NR]

        const_in, late_in = sem("const_in"), sem("late_in")
        x_in = [sem(f"x_in{t}") for t in range(TT)]
        act_step, dve_step, pool_step = sem("act_step"), sem("dve_step"), sem("pool_step")
        par_done, ones_ready, hrow_in = map(sem, ("par_done", "ones_ready", "hrow_in"))
        dev_ready, inv_ready, xn_ready, xt_ready, hf_ready, xh_ready, xl_ready = map(
            sem, ("dev_ready", "inv_ready", "xn_ready", "xt_ready", "hf_ready", "xh_ready",
                  "xl_ready"))
        vr_ready, vt_mm, acs_mm, row_mm, sp_arg, sp_exp, dt_ready, scr_out = map(
            sem, ("vr_ready", "vt_mm", "acs_mm", "row_mm", "sp_arg", "sp_exp", "dt_ready",
                  "scr_out"))
        g_in = [sem(f"g_in{k}") for k in range(RAW)]
        g_hi, g_lo, g_used = map(sem, ("g_hi", "g_lo", "g_used"))
        wblk_in, gt_mm, z_out = map(sem, ("wblk_in", "gt_mm", "z_out"))
        tap_u, tap_e, tap_o, u_ready, cv_e, cv_o = map(
            sem, ("tap_u", "tap_e", "tap_o", "u_ready", "cv_e", "cv_o"))
        gate_act, a2_act, m2_ready, sq_act, lru_done, silu_e, silu_o, g_act, lru_g, z_act = map(
            sem, ("gate_act", "a2_act", "m2_ready", "sq_act", "lru_done", "silu_e", "silu_o",
                  "g_act", "lru_g", "z_act"))
        xc_in, ea_in = sem("xc_in"), sem("ea_in")
        l_in = [sem("l_in0"), sem("l_in1")]
        zc_in = [sem("zc_in0"), sem("zc_in1")]
        xp_mm, ts_mm, st_mm, yo_mm, y_mm = map(sem, ("xp_mm", "ts_mm", "st_mm", "yo_mm", "y_mm"))
        xw_ready, sm_ready, diff_ready, clamped, e_ready, m_ready, st_upd, yt_done, comb = map(
            sem, ("xw_ready", "sm_ready", "diff_ready", "clamped", "e_ready", "m_ready",
                  "st_upd", "yt_done", "comb"))
        xdt_ready = sem("xdt_ready")
        bt_ready, sql, accl, xd_ready, lru_w, sqs, accs, ssd_w = map(
            sem, ("bt_ready", "sql", "accl", "xd_ready", "lru_w", "sqs", "accs", "ssd_w"))
        ylh_act, yll_done, ysh_act, ysl_done = map(
            sem, ("ylh_act", "yll_done", "ysh_act", "ysl_done"))
        w_in3 = [sem(f"w_in{k}") for k in range(3)]
        w_hi, w_lo, w_used, pass_mm, last_mm, evac, x2_done = map(
            sem, ("w_hi", "w_lo", "w_used", "pass_mm", "last_mm", "evac", "x2_done"))
        ss_mm, devo = sem("ss_mm"), sem("devo")
        dev2, inv2, h2_ready = sem("dev2"), sem("inv2"), sem("h2_ready")
        h2_out = [sem("h2_out0"), sem("h2_out1")]
        ht2_mm, ht2_act, lg_mm, lg_done = map(sem, ("ht2_mm", "ht2_act", "lg_mm", "lg_done"))

        rt = late[:, :, :].rearrange("p a n -> p (a n)")
        at = [0]

        def route_tile(*dims):
            n = int(np.prod(dims))
            t = rt[:, at[0]:at[0] + n]
            at[0] += n
            if len(dims) == 2:
                return t.rearrange("p (a b) -> p a b", b=dims[1])
            if len(dims) == 3:
                return t.rearrange("p (a b c) -> p a b c", b=dims[1], c=dims[2])
            return t

        r_eq, r_pos, r_oh = (route_tile(TT, MG) for _ in range(3))
        r_fo = route_tile(TT, MG, EG)
        r_f, r_f2, r_eq8, r_pos8 = (route_tile(TT, EG) for _ in range(4))
        r_o = [route_tile(TT, EG) for _ in range(2)]
        r_cmax, r_pm, r_gw, r_w1, r_m1, r_m2 = (route_tile(TT) for _ in range(6))
        r_exp = route_tile(TT * (MG + 1))
        r_M = [route_tile(TT, NE) for _ in range(2)]
        r_sum, r_pre, r_tmp = (route_tile(TT, NE) for _ in range(3))
        r_tot, r_cnt, r_nov, r_oinc, r_ost = (route_tile(NE) for _ in range(5))
        r_rk, r_J, r_slot, r_os, r_eid, r_blk, r_g = (route_tile(2 * TT) for _ in range(7))
        r_A = route_tile(2 * TT, P)
        r_B = route_tile(2 * TT, NBLK)
        r_ge = route_tile(16, NE)
        rt_arg, rt_exp, rk_in, rk_mm, ab_in, tab_mm, tab_ready = map(
            sem, ("rt_arg", "rt_exp", "rk_in", "rk_mm", "ab_in", "tab_mm", "tab_ready"))

        wch_in = [sem(f"wch_in{j}") for j in range(CH)]
        hi_made, lo_made, ch_used, xb_in, xb_mm, xt_hi, xt_lo, sg_act, hid_ready = map(
            sem, ("hi_made", "lo_made", "ch_used", "xb_in", "xb_mm", "xt_hi", "xt_lo", "sg_act",
                  "hid_ready"))
        hidt_mm, ht_hi, ht_lo, yb_act, y_out = map(
            sem, ("hidt_mm", "ht_hi", "ht_lo", "yb_act", "y_out"))
        YL = [(late if t < 3 else ring_gu)[:, 2 * (t % 3):2 * (t % 3) + 2, :]
              for t in range(TT - 2)]
        YL += [ring_dn[:, 0:2, :], ring_dn[:, 2:4, :]]
        FSQ = late[:, 6, :]
        x3_ready, dev3, inv3, scaled, o_early, o_ready, out_done = map(
            sem, ("x3_ready", "dev3", "inv3", "scaled", "o_early", "o_ready", "out_done"))

        block = ctx.enter_context(nc.Block())

        def param(name, i, k=0):
            return pv[:, bass.ds(i + (PV[name] + k), 1)]

        @block.sync
        def _(sp):
            for t in range(TT):
                sp.dma_start(xall[:, t, :], a["x"][t]).then_inc(x_in[t], 16)
                if t == 1:
                    sp.dma_start(pv[:, :], a["pv"]).then_inc(const_in, 16)
                    sp.dma_start(ident[:, :], a["ident"]).then_inc(const_in, 16)
                    sp.dma_start(tri[:, :], a["tri"]).then_inc(const_in, 16)

            def granule(at, slot):
                sp.dma_start(raw[:, slot % RAW, :], a["win"][bass.ds(at, 1)].rearrange(
                    "a p n -> p (a n)")).then_inc(g_in[slot % RAW], 16)

            def blocks(i):
                sp.dma_start(wblk, a["wblk"][bass.ds(i, 1)].rearrange(
                    "a p g n -> p (a g) n")).then_inc(wblk_in, 16)

            for g in range(RAW):
                granule(g, g)
            blocks(0)
            with sp.Fori(1, 8) as i:
                for g in range(B_PER):
                    sp.wait_ge(g_lo, i * B_PER + (g + 1 - B_PER))
                    granule(i * B_PER + (g + RAW - B_PER), g)
                    if g == 7:
                        sp.wait_ge(gt_mm, i * 2)
                        blocks(i)
            for at in range(RAW + 7 * B_PER, N_GR):
                sp.wait_ge(g_lo, at + 1 - RAW)
                granule(at, at)
            sp.dma_start(cst[:, :], a["cst"]).then_inc(late_in, 16)
            sp.wait_ge(scr_out, 32)
            sp.wait_ge(g_lo, N_GR)
            sp.wait_ge(silu_e, 8)
            sp.wait_ge(silu_o, 7)
            sp.wait_ge(z_out, 16 * 8)

            def chunk_loads(c, p):
                wait(sp, ts_mm, c)
                sp.dma_start(XC, XBC[:, 0:12, bass.ds(c * P, P)]).then_inc(xc_in, 16)
                if isinstance(c, int) and c == 0:
                    sp.wait_ge(lru_done, 8)
                elif isinstance(c, int) and c == 1:
                    sp.wait_ge(g_used, N_GR)
                wait(sp, y_mm, c - 1)
                sp.dma_start(L[p], acs_d[:, bass.ds(c * P, P)].partition_broadcast(P)
                             ).then_inc(l_in[p], 16)

            def two_chunks(i):
                for p in range(2):
                    chunk_loads(i * 2 + p, p)

            two_chunks(0)
            with sp.Fori(1, 4) as i:
                two_chunks(i)

            def w_granule(at):
                sp.dma_start(wraw[:, at % 3, :], a["wout"][at]).then_inc(w_in3[at % 3], 16)

            def x_half(m):
                sp.dma_start(XR[m % 8], a["x"][m % 8][:, m // 8 * 512:(m // 8 + 1) * 512]
                             ).then_inc(x_in[m % 8], 16)

            sp.wait_ge(ts_mm, 8)
            for at in range(3):
                w_granule(at)
            sp.wait_ge(comb, 8)
            for m in range(4):
                x_half(m)
            sp.dma_start(wr, a["wr"]).then_inc(late_in, 16)
            sp.dma_start(nrow, a["nrow"].partition_broadcast(P)).then_inc(late_in, 16)
            sp.wait_ge(ss_mm, 1)
            for m in range(4, 8):
                x_half(m)
            for at in range(3, 4 * KT):
                sp.wait_ge(w_lo, at - 2)
                w_granule(at)
                if 8 <= at - 3 < 16:
                    sp.wait_ge(evac, at - 10)
                    x_half(at - 3)
                if at == 4 * KT - 1:
                    sp.wait_ge(pass_mm, 16)
                    for j in range(KT):
                        sp.dma_start(ring[j], a["moe"][j]).then_inc(wch_in[j], 16)
            for t in range(TT):
                sp.wait_ge(h2_ready, t + 1)
                sp.dma_start(h2_d[P * t:P * (t + 1), :], H2[t % 2]).then_inc(h2_out[t % 2], 16)
            sp.wait_ge(last_mm, TT)
            for j in range(KT, CH):
                sp.dma_start(ring[j], a["moe"][j]).then_inc(wch_in[j], 16)

            def load(j, e):
                sp.dma_start(ring[j], a["moe"][bass.ds(e * CH + j, 1)].rearrange(
                    "a p n -> p (a n)")).then_inc(wch_in[j], 16)

            for j in range(KT):
                sp.wait_ge(lo_made, j + 1)
                sp.dma_start(ring[j], a["moe"][CH + j]).then_inc(wch_in[j], 16)
            with sp.Fori(2, NE) as e:
                for j in range(KT):
                    sp.wait_ge(lo_made, e * CH + (GU_AT - CH + j + 1))
                    load(j, e)
                for j in range(KT, CH):
                    sp.wait_ge(lo_made, e * CH + (DN_AT - 2 * CH + j + 1))
                    load(j, e - 1)
            for j in range(KT, CH):
                sp.wait_ge(lo_made, (NE - 1) * CH + DN_AT - CH + j + 1)
                sp.dma_start(ring[j], a["moe"][(NE - 1) * CH + j]).then_inc(wch_in[j], 16)
            sp.wait_ge(tab_ready, 1)
            n_over = sp.value_load(over_i[0:1, 15:16], min_val=0, max_val=MAX_OVER)

            def overflow_block(o):
                e = sp.value_load(over_i[0:1, bass.ds(o, 1)], min_val=0, max_val=NE - 1)
                for j in range(CH):
                    sp.wait_ge(lo_made, o * CH + (OVER_AT - CH + 1 + j))
                    load(j, e)
            overflow_blocks(sp, n_over, overflow_block)
            sp.wait_ge(y_out, n_over * 16 + NE * 16)
            for t in range(TT):
                sp.dma_start(YL[t], y_d.rearrange("(k t p) d -> t p k d", p=P, k=2)[t]
                             ).then_inc(x_in[t], 16)
            for t in range(TT):
                if t < TT // 2:
                    sp.wait_ge(o_early, t + 1)
                else:
                    sp.wait_ge(o_ready, t - TT // 2 + 1)
                sp.dma_start(a["out"][t], X2[:, t, :]).then_inc(out_done, 16)
            sp.wait_ge(out_done, 16 * TT)

        @block.tensor
        def _(pe):
            def project(at, slot, bank):
                for q in range(2):
                    pe.wait_ge(g_lo, at + (q + 1))
                    w = (slot + q) % SPL
                    for k in range(KT // 2):
                        col = slice(k * P, (k + 1) * P)
                        kk = q * (KT // 2) + k
                        for n, (wp, x) in enumerate(((GH, XH), (GH, XL), (GL, XH))):
                            for h in range(2):
                                mm = pe.matmul(ps[:, bank + h, :], wp[:, w, col],
                                               x[:, kk, h * 512:(h + 1) * 512],
                                               start=(kk == 0 and n == 0),
                                               stop=(kk == KT - 1 and n == 2))
                    mm.then_inc(g_used, 1)

            pe.wait_ge(const_in, 48)
            for t in range(TT):
                if t >= 2:
                    pe.wait_ge(hf_ready, 2 * (t - 1))
                pe.wait_ge(xn_ready, t + 1)
                for k in range(KT):
                    mm = pe.transpose(ps[:, 2 * (t % 2) + k // 4, (k % 4) * P:(k % 4 + 1) * P],
                                      xn[t % 2][:, k * P:(k + 1) * P], ident[:, :])
                mm.then_inc(xt_ready, 1)
            pe.wait_ge(xl_ready, TT)
            project(0, 0, 6)
            pe.wait_ge(vr_ready, 1)
            for c in range(TT):
                mm = pe.transpose(ps[:, 4, c * NH:(c + 1) * NH], VR[:, c * P:(c + 1) * P],
                                  ident[0:NH, 0:NH])
            mm.then_inc(vt_mm, 1)
            project(2, 0, 2)
            pe.wait_ge(sp_arg, 2)
            pe.matmul(ps[:, 5, 0:NS], tri[:, :], sv["s"][:, 0:NS], start=True, stop=True)
            pe.matmul(ps[:, 5, NS:2 * NS], ones[:, :], sv["s"][:, 0:NS], start=True,
                      stop=True).then_inc(acs_mm, 1)
            pe.wait_ge(sp_arg, 3)
            for c in range(TT):
                mm = pe.transpose(ps[0:NH, 6 + c // 4, (c % 4) * P:(c % 4 + 1) * P],
                                  colv[:, 0, c, :], ident[:, :])
            mm.then_inc(row_mm, 1)
            pe.wait_ge(sp_exp, 3)

            def turn(i):
                at = i * B_PER + B_AT
                wait(pe, gate_act, i * 2)
                project(at, 0, 4)
                wait(pe, g_act, i)
                project(at + 2, 0, 0)
                pe.wait_ge(u_ready, i + 1)
                pe.wait_ge(wblk_in, i * 16 + 16)
                if isinstance(i, int) and i == 0:
                    pe.wait_ge(sp_exp, 5)
                for g in range(2):
                    for h in range(2):
                        mm = pe.matmul(ps[:, 6 - 2 * g + h, :], wblk[:, g, :],
                                       HR[:, bass.ds(i, 1), h * 512:(h + 1) * 512].rearrange(
                                           "p a n -> p (a n)"), start=True, stop=True)
                    mm.then_inc(gt_mm, 1)
                pe.wait_ge(z_act, i + 1)
                project(at + 4, 0, 2)
                pe.wait_ge(cv_e, i + 1)
                project(at + 6, 0, 0)
                if not (isinstance(i, int) and i == 7):
                    pe.wait_ge(cv_o, i + 1)
                    project(at + 8, 0, 2)

            turns(pe, 0, 8, turn)
            pe.wait_ge(g_act, 8)
            pe.wait_ge(cv_o, 8)
            pe.wait_ge(gate_act, 16)
            pe.wait_ge(silu_o, 8)

            def chunk(c):
                pe.wait_ge(xc_in, c * 16 + 16)
                wait(pe, xdt_ready, c)
                for k in range(KT):
                    mm = pe.transpose(ps[:, k // 4, (k % 4) * P:(k % 4 + 1) * P],
                                      XC[:, k, :], ident[:, :])
                mm.then_inc(xp_mm, 1)
                wait(pe, yt_done, c)
                for g in range(NG):
                    pe.transpose(ps[:, 4, g * P:(g + 1) * P], XC[:, KT + g, :], ident[:, :])
                for g in range(NG):
                    mm = pe.matmul(ps[:, 5, g * P:(g + 1) * P], XC[:, KT + g, :],
                                   XBC[:, 12 + g, bass.ds(c * P, P)], start=True, stop=True)
                mm.then_inc(ts_mm, 1)
                pe.wait_ge(xw_ready, c + 1)
                pe.wait_ge(bt_ready, c + 1)
                wait(pe, st_upd, c)
                for g in range(NG):
                    mm = pe.matmul(ps[:, 6 + g // 2, (g % 2) * 256:(g % 2 + 1) * 256],
                                   BT[:, g, :], XW[:, g * 256:(g + 1) * 256],
                                   start=True, stop=True)
                mm.then_inc(st_mm, 1)
                pe.wait_ge(sm_ready, c + 1)
                for j in range(KT):
                    mm = pe.matmul(ps[:, 4 + j // 4, (j % 4) * P:(j % 4 + 1) * P],
                                   STATE[:, j * P:(j + 1) * P],
                                   XBC[:, 12 + j // 2, bass.ds(c * P, P)],
                                   start=True, stop=True)
                mm.then_inc(yo_mm, 1)
                pe.wait_ge(m_ready, c + 1)
                for h in range(NH):
                    j, q = h // 2, h % 2
                    mm = pe.matmul(ps[HD * q:HD * (q + 1), 2 + j // 4,
                                      (j % 4) * P:(j % 4 + 1) * P],
                                   XDT[:, h * HD:(h + 1) * HD], LP[0][:, h, :],
                                   start=True, stop=True)
                mm.then_inc(y_mm, 1)

            LP = [None]

            def two_chunks(i):
                for p in range(2):
                    LP[0] = L[p]
                    chunk(i * 2 + p)

            two_chunks(0)
            with pe.Fori(1, 4) as i:
                two_chunks(i)
            pe.wait_ge(yll_done, 8)
            pe.wait_ge(xdt_ready, 8)
            pe.wait_ge(yt_done, 8)
            pe.wait_ge(st_upd, 8)

            def product(n, t, bank, parts, w):
                cols = slice(t * P, (t + 1) * P)
                k = n % KT
                for m, (y, wp) in enumerate(((parts[0], w[0]), (parts[0], w[1]),
                                             (parts[1], w[0]))):
                    mm = pe.matmul(ps[:, bank, :], y[:, k, cols], wp,
                                   start=(k == 0 and m == 0), stop=(k == KT - 1 and m == 2))
                return mm

            split_w = lambda n: [SW[:, n % 2, q, :] for q in range(2)]
            for k in range(2):
                pe.wait_ge(w_lo, k + 1)
                for t in range(TT - 1):
                    product(k, t, t, (YLH, YLL), split_w(k))
            pe.wait_ge(accl, 8)
            pe.wait_ge(accs, 8)
            for q, acc in enumerate((ACCL, ACCS)):
                for t in range(TT):
                    mm = pe.matmul(ps[:, 7, q * TT + t:q * TT + t + 1],
                                   acc[:, t * P:(t + 1) * P], ones[:, 0:1],
                                   start=True, stop=True)
            mm.then_inc(ss_mm, 1)
            pe.wait_ge(devo, 1)
            for k in range(2):
                product(k, TT - 1, TT - 1, (YLH, YLL), split_w(k)).then_inc(w_used, 1)
            for n in range(2, 3 * KT):
                pe.wait_ge(w_lo, W_ORDER.index(n) + 1)
                if n >= 2 * KT:
                    pe.wait_ge(ysl_done, n % KT + 1)
                for t in range(TT):
                    if n % KT == 0:
                        pe.wait_ge(evac, n - KT + t + 1)
                    mm = product(n, t, t, (YLH, YLL) if n < 2 * KT else (YSH, YSL), split_w(n))
                    if n % KT == KT - 1:
                        mm.then_inc(pass_mm, 1)
                if n % KT < KT - 1:
                    mm.then_inc(w_used, 1)

            def last_half(t, half):
                for k in range(half * KT // 2, (half + 1) * KT // 2):
                    if t == 0:
                        pe.wait_ge(w_lo, W_ORDER.index(3 * KT + k) + 1)
                    mm = product(3 * KT + k, t, t % 2, (YSH, YSL),
                                 [LW[:, q, k, :] for q in range(2)])
                if half == 1:
                    mm.then_inc(last_mm, 1)

            def turn_h2(t):
                pe.wait_ge(h2_ready, t + 1)
                if t >= 1:
                    pe.wait_ge(ht2_act, t)
                for k in range(KT):
                    mm = pe.transpose(ps[:, 4 + k // 4, (k % 4) * P:(k % 4 + 1) * P],
                                      H2[t % 2][:, k * P:(k + 1) * P], ident[:, :])
                mm.then_inc(ht2_mm, 1)

            def route(t):
                pe.wait_ge(ht2_act, t + 1)
                if t >= 1:
                    pe.wait_ge(lg_done, t)
                for k in range(KT):
                    mm = pe.matmul(ps[:, 6, 0:NR], H2T[:, k, :], wr[:, k, :],
                                   start=(k == 0), stop=(k == KT - 1))
                mm.then_inc(lg_mm, 1)

            pe.wait_ge(evac, 3 * TT)
            pe.wait_ge(late_in, 48)
            for t in range(TT + 1):
                if t < TT:
                    if t >= 2:
                        pe.wait_ge(x2_done, t - 1)
                    last_half(t, 0)
                if t >= 2:
                    turn_h2(t - 2)
                if t < TT:
                    last_half(t, 1)
                if t >= 2:
                    route(t - 2)
            turn_h2(TT - 1)
            route(TT - 1)
            pe.wait_ge(lg_done, TT)
            pe.wait_ge(rk_in, 1)
            flat = lambda t: t.rearrange("p a b -> p (a b)")
            pe.matmul(ps[:, 7, 0:TT * NE], above, flat(r_sum), start=True, stop=False)
            pe.matmul(ps[:, 7, 0:TT * NE], ones[:, :], flat(r_pre), start=False, stop=True)
            pe.matmul(ps[:, 7, TT * NE:TT * NE + NE], ones[:, :], r_tot, start=True,
                      stop=True).then_inc(rk_mm, 1)
            pe.wait_ge(ab_in, 1)
            for n in range(2 * TT):
                mm = pe.matmul(ps[:, 7, 0:NBLK], r_A[:, n, :], r_B[:, n, :],
                               start=(n == 0), stop=(n == 2 * TT - 1))
            mm.then_inc(tab_mm, 1)

            def turn_rows(count):
                pe.wait_ge(xb_in, count * 16)
                for k in range(KT):
                    mm = pe.transpose(ps[:, 2 + k // 4, (k % 4) * P:(k % 4 + 1) * P],
                                      XB[:, k * P:(k + 1) * P], ident[:, :])
                mm.then_inc(xb_mm, 1)

            def split_product(bank, hi, lo, k, at, slot, last):
                pe.wait_ge(lo_made, at + 1)
                rows = slice(k * P, (k + 1) * P)
                for n, (x, w) in enumerate(((hi, WH), (hi, WL), (lo, WH))):
                    for h in range(2):
                        mm = pe.matmul(ps[:, bank + h, :], x[:, rows],
                                       w[slot % HL][:, h * 512:(h + 1) * 512],
                                       start=(k == 0 and n == 0), stop=(last and n == 2))
                mm.then_inc(ch_used, 1)

            def gate_up(b, at, slot):
                pe.wait_ge(xt_lo, b + 1)
                wait(pe, hid_ready, b)
                for k in range(KT):
                    split_product(0, XTH, XTL, k, at + k, slot + k, k == KT - 1)

            def down(b, at, slot):
                pe.wait_ge(ht_lo, b + 1)
                wait(pe, yb_act, b)
                for k in range(KD):
                    split_product(5, HTH, HTL, k, at + k, slot + k, k == KD - 1)

            def turn_hidden(b):
                pe.wait_ge(hid_ready, b + 1)
                for k in range(KD):
                    mm = pe.transpose(ps[:, 4, k * P:(k + 1) * P], HID[:, k * P:(k + 1) * P],
                                      ident[:, :])
                mm.then_inc(hidt_mm, 1)

            turn_rows(1)
            gate_up(0, 0, 0)
            turn_rows(2)
            turn_hidden(0)

            def turn(b):
                gate_up(b, b * CH + GU_AT, GU_AT)
                turn_rows(b + 2)
                down(b - 1, b * CH + DN_AT - CH + KT, DN_AT - CH + KT)
                turn_hidden(b)

            turn(1)
            with pe.Fori(2, NE) as b:
                turn(b)
            down(NE - 1, DN_LAST, DN_LAST)
            n_over = pe.value_load(over_i[0:1, 15:16], min_val=0, max_val=MAX_OVER)

            def overflow_block(o):
                gate_up(o + NE, o * CH + OVER_AT, 0)
                turn_hidden(o + NE)
                turn_rows(o + (NE + 2))
                down(o + NE, o * CH + (OVER_AT + KT), KT)

            overflow_blocks(pe, n_over, overflow_block)
        @block.scalar
        def _(act):
            st = Steps(act, act_step)
            act.wait_ge(par_done, 1)
            for t in range(TT):
                act.wait_ge(x_in[t], 16)
                st.link(act.activation(junk, xall[:, t, :], ACT.Square,
                                       accum_out=stat[:, 0, t:t + 1]))
            link(act, act.activation(stat[:, 1, 0:TT], stat[:, 0, 0:TT], ACT.Sqrt,
                                     bias=eps[:, 0:1], scale=1.0 / D), dev_ready, 1)
            act.wait_ge(inv_ready, 1)

            def upper(t):
                act.wait_ge(hf_ready, 2 * t + 2)
                act.activation(XH[:, :, t * P:(t + 1) * P], HF[t % 2], ACT.Copy
                               ).then_inc(xh_ready, 1)

            for t in range(TT):
                if t >= 2:
                    act.wait_ge(xt_ready, t - 1)
                act.activation(xn[t % 2], xall[:, t, :], ACT.Copy,
                               scale=stat[:, 2, t:t + 1]).then_inc(xn_ready, 1)
                if t >= 1:
                    upper(t - 1)
            upper(TT - 1)
            act.dma_start(hrow, a["hpar"].partition_broadcast(P)).then_inc(hrow_in, 16)
            act.wait_ge(g_used, 2)
            link(act, act.activation(VR, pair(6)[0:NH, :], ACT.Copy), vr_ready, 1)
            act.wait_ge(hrow_in, 16)
            st.link(act.activation(hrow[:, 1, :], hrow[:, 1, :], ACT.Exp))
            act.wait_ge(sp_arg, 1)
            link(act, act.activation(sv["e"], sv["nab"], ACT.Exp), sp_exp, 1)
            act.wait_ge(sp_arg, 4)
            link(act, act.activation(colv[:, 2, :, :].rearrange("p c h -> p (c h)"),
                                     sv["p"][:, 0:NS], ACT.Exp), sp_exp, 2)
            act.activation(decb.rearrange("p c h -> p (c h)"), ps[:, 5, NS:2 * NS],
                           ACT.Exp).then_inc(sp_exp, 1)
            act.wait_ge(row_mm, 1)
            act.activation(EA, pair(6)[0:NH, :], ACT.Exp).then_inc(sp_exp, 1)
            link(act, act.activation(ACS, pair(6)[0:NH, :], ACT.Copy), sp_exp, 5)
            for rows, to in ((ACS, acs_d), (EA, ea_d)):
                act.dma_start(to, rows).then_inc(scr_out, 16)

            def z_tile(i):
                link(act, act.activation(A2, pair(2), ACT.Silu), z_act, i + 1)
                act.dma_start(z_d.rearrange("(j p) n -> j p n", p=P)[bass.ds(i, 1)].rearrange(
                    "a p n -> p (a n)"), A2).then_inc(z_out, 16)

            act.wait_ge(g_used, 4)
            z_tile(0)
            act.wait_ge(scr_out, 32)
            act.wait_ge(dt_ready, 1)

            def turn(i):
                used = i * B_PER + B_AT
                two = lambda q: XBC[:, :, :].rearrange("p (i q) n -> p i q n", q=2)[
                    :, bass.ds(i, 1), q, :].rearrange("p a n -> p (a n)")
                xbc = lambda q: XBC[:, bass.ds(i * 2 + q, 1), :].rearrange("p a n -> p (a n)")
                act.wait_ge(g_used, used + 2)
                link(act, act.activation(HR[:, bass.ds(i, 1), :].rearrange("p a n -> p (a n)"), pair(4), ACT.Identity, bias=param("lru_cb", i),
                                         scale=param("lru_cw", i, 24)), tap_u, i + 1)
                act.wait_ge(g_used, used + 4)
                link(act, act.activation(xbc(0), pair(0), ACT.Identity,
                                         bias=param("ssd_cb", i * 2),
                                         scale=param("ssd_cw", i * 2, 48)), tap_e, i + 1)
                act.wait_ge(cv_e, i + 1)
                link(act, act.activation(two(0), two(0), ACT.Silu), silu_e, i + 1)
                act.wait_ge(gt_mm, i * 2 + 1)
                link(act, act.activation(TR, pair(6), ACT.Tanh,
                                         bias=prep[:, 0, bass.ds(i, 1)], scale=0.5),
                     gate_act, i * 2 + 1)
                act.wait_ge(gt_mm, i * 2 + 2)
                link(act, act.activation(TI, pair(4), ACT.Tanh,
                                         bias=prep[:, 1, bass.ds(i, 1)], scale=0.5),
                     gate_act, i * 2 + 2)
                st.link(act.activation(AA, TR, ACT.Exp, bias=prep[:, 2, bass.ds(i, 1)],
                                       scale=prep[:, 2, bass.ds(i, 1)]))
                st.link(act.activation(TR, TR, ACT.Tanh, bias=prep[:, 3, bass.ds(i, 1)],
                                       scale=prep[:, 3, bass.ds(i, 1)]))
                act.wait_ge(z_out, i * 16 + 16)
                link(act, act.activation(A2, AA, ACT.Square), a2_act, i + 1)
                act.wait_ge(g_used, used + 6)
                link(act, act.activation(xbc(1), pair(2), ACT.Identity,
                                         bias=param("ssd_cb", i * 2, 1),
                                         scale=param("ssd_cw", i * 2, 49)), tap_o, i + 1)
                act.wait_ge(m2_ready, i + 1)
                link(act, act.activation(A2, A2, ACT.Sqrt, bias=eps[:, 1:2]), sq_act, i + 1)
                act.wait_ge(cv_o, i + 1)
                link(act, act.activation(two(1), two(1), ACT.Silu), silu_o, i + 1)
                act.wait_ge(g_used, used + 8)
                wait(act, lru_g, i)
                link(act, act.activation(G, pair(0), ACT.Gelu_apprx_tanh), g_act, i + 1)
                if not (isinstance(i, int) and i == 7):
                    act.wait_ge(g_used, used + 10)
                    act.wait_ge(lru_done, i + 1)
                    z_tile(i + 1)

            turns(act, 0, 8, turn, st, 2)
            act.wait_ge(g_used, N_GR)
            act.wait_ge(lru_g, 8)

            def decay_exp(c, p):
                act.wait_ge(diff_ready, c + 1)
                link(act, act.activation(L[p], L[p], ACT.Relu, scale=-1.0), clamped, c + 1)
                link(act, act.activation(L[p], L[p], ACT.Exp, scale=-1.0), e_ready, c + 1)

            def chunk(c, p, last=False):
                act.wait_ge(ts_mm, c + 1)
                wait(act, st_mm, c)
                link(act, act.activation(BT.rearrange("p g n -> p (g n)"), ps[:, 4, :],
                                         ACT.Copy), bt_ready, c + 1)
                wait(act, accl, c)
                y = HR[:, bass.ds(c, 1), :].rearrange("p a n -> p (a n)")
                link(act, act.activation(SQL, y, ACT.Square), sql, c + 1)
                link(act, act.activation(y, y, ACT.Copy, scale=param("lru_norm", c)),
                     lru_w, c + 1)
                act.activation(YLH[:, bass.ds(c, 1), :].rearrange("p a n -> p (a n)"), y,
                               ACT.Copy).then_inc(ylh_act, 1)
                if not last:
                    decay_exp(c + 1, 1 - p)
                    decay_loads(c + 1, 1 - p)
                act.wait_ge(comb, c + 1)
                wait(act, accs, c)
                link(act, act.activation(SQ.rearrange("p (k n) -> p k n", n=P),
                                         XBC[:, 0:KT, bass.ds(c * P, P)], ACT.Square),
                     sqs, c + 1)

            def decay_loads(c, p):
                wait(act, yt_done, c)
                for q in range(2):
                    act.dma_start(EAB[HD * q:HD * (q + 1)], ea_d.rearrange(
                        "(j q) s -> q j s", q=2)[q][:, bass.ds(c * P, P)
                        ].partition_broadcast(HD)).then_inc(ea_in, 16)
                wait(act, comb, c - 1)
                act.dma_start(ZC[p], z_d.rearrange("(j p) n -> p j n", p=P)[
                    :, :, bass.ds(c * P, P)]).then_inc(zc_in[p], 16)

            decay_loads(0, 0)
            decay_exp(0, 0)
            chunk(0, 0)
            chunk(1, 1)
            with act.Fori(1, 3) as i:
                chunk(i * 2, 0)
                chunk(i * 2 + 1, 1)
            chunk(6, 0)
            chunk(7, 1, last=True)
            act.wait_ge(ss_mm, 1)
            link(act, act.activation(stat[:, 3, :], ps[:, 7, 0:2 * TT], ACT.Sqrt,
                                     bias=eps[:, 0:1], scale=1.0 / D), devo, 1)
            act.wait_ge(ssd_w, 8)
            act.wait_ge(comb, 8)
            for k in range(KT):
                act.activation(YSH[:, k, :], XBC[:, k, :], ACT.Copy).then_inc(ysh_act, 1)
            for t in range(TT + 1):
                if t < TT:
                    act.wait_ge(x2_done, t + 1)
                    if t >= 1:
                        act.wait_ge(h2_ready, t)
                    st.link(act.activation(JUNK, X2[:, t, :], ACT.Square,
                                           accum_out=stat[:, 0, t:t + 1]))
                    link(act, act.activation(stat[:, 1, t:t + 1], stat[:, 0, t:t + 1],
                                             ACT.Sqrt, bias=eps[:, 0:1], scale=1.0 / D),
                         dev2, t + 1)
                if t >= 1:
                    act.wait_ge(ht2_mm, t)
                    if t >= 2:
                        act.wait_ge(lg_mm, t - 1)
                    link(act, act.activation(H2T.rearrange("p k n -> p (k n)"), pair(4),
                                             ACT.Copy), ht2_act, t)
            act.wait_ge(rt_arg, 1)
            link(act, act.activation(r_exp, r_exp, ACT.Exp), rt_exp, 1)

            def to_hi(j, b, at, slot):
                act.wait_ge(wch_in[j], b * 16 + 16)
                if not (isinstance(at, int) and at < HL):
                    act.wait_ge(ch_used, at + (1 - HL))
                act.activation(WH[slot % HL], ring[j], ACT.Copy).then_inc(hi_made, 1)

            def gates(b, used):
                act.wait_ge(ch_used, used)
                if not (isinstance(b, int) and b == 0):
                    act.wait_ge(hid_ready, b)
                act.activation(SG, ps[:, 0, :], ACT.Silu).then_inc(sg_act, 1)

            def rows_hi(b):
                act.wait_ge(xb_mm, b + 1)
                act.activation(XTH[:, :], pair(2), ACT.Copy).then_inc(xt_hi, 1)

            def hidden_hi(b):
                act.wait_ge(hidt_mm, b + 1)
                act.activation(HTH[:, :], ps[:, 4, :], ACT.Copy).then_inc(ht_hi, 1)

            def rows_out(b, used):
                act.wait_ge(ch_used, used)
                wait(act, y_out, b * 16)
                act.activation(YB[:, :], pair(5), ACT.Copy).then_inc(yb_act, 1)

            act.wait_ge(lg_mm, TT)
            for p in range(2):
                act.wait_ge(h2_out[p], 16 * TT // 2)
            for j in range(HL):
                to_hi(j, 0, j, j)
            rows_hi(0)
            for j in range(HL, KT):
                to_hi(j, 0, j, j)
            gates(0, KT)
            rows_hi(1)
            for j in range(KT // 2):
                to_hi(j, 1, CH + GU_AT + j, GU_AT + j)
            hidden_hi(0)

            def turn(b, last):
                for j in range(KT // 2, KT):
                    to_hi(j, b, b * CH + (GU_AT + j), GU_AT + j)
                for j in range(KT, CH):
                    to_hi(j, b - 1, b * CH + (DN_AT - CH + j), DN_AT - CH + j)
                gates(b, b * CH + (GU_AT + KT))
                rows_hi(b + 1)
                if not last:
                    for j in range(KT // 2):
                        to_hi(j, b + 1, b * CH + (CH + GU_AT + j), GU_AT + j)
                else:
                    for j in range(KT, CH):
                        to_hi(j, b, DN_LAST - KT + j, DN_LAST - KT + j)
                hidden_hi(b)
                rows_out(b - 1, b * CH + DN_AT)

            turn(1, False)
            with act.Fori(2, NE - 1) as b:
                turn(b, False)
            turn(NE - 1, True)
            n_over = act.value_load(over_i[0:1, 15:16], min_val=0, max_val=MAX_OVER)

            def overflow_block(o):
                for j in range(HL):
                    to_hi(j, o + NE, o * CH + (OVER_AT + j), j)
                rows_out(o + (NE - 1), o * CH + OVER_AT)
                for j in range(HL, KT):
                    to_hi(j, o + NE, o * CH + (OVER_AT + j), j)
                for j in range(KT, CH):
                    to_hi(j, o + NE, o * CH + (OVER_AT + j), j)
                gates(o + NE, o * CH + (OVER_AT + KT))
                hidden_hi(o + NE)
                rows_hi(o + (NE + 1))
            overflow_blocks(act, n_over, overflow_block)
            rows_out(n_over + (NE - 1), n_over * CH + OVER_AT)
            for t in range(TT):
                act.wait_ge(x3_ready, t + 1)
                st.link(act.activation(FSQ, X2[:, t, :], ACT.Square,
                                       accum_out=stat[:, 4, t:t + 1]))
                if t % 4 == 3:
                    half = slice(t - 3, t + 1)
                    link(act, act.activation(stat[:, 5, half], stat[:, 4, half], ACT.Sqrt,
                                             bias=eps[:, 0:1], scale=1.0 / D), dev3, t // 4 + 1)
                if t == 3:
                    act.wait_ge(inv3, 1)
                if 3 <= t < 7:
                    act.activation(X2[:, t - 3, :], X2[:, t - 3, :], ACT.Copy,
                                   scale=stat[:, 6, t - 3:t - 2]).then_inc(scaled, 1)

        @block.vector
        def _(dve):
            st = Steps(dve, dve_step)
            st.link(dve.memset(eps[:, 0:1], EPS))
            dve.memset(eps[:, 1:2], 1e-30).then_inc(par_done, 1)
            link(dve, dve.memset(ones[:, :], 1.0), ones_ready, 1)
            dve.wait_ge(dev_ready, 1)
            link(dve, dve.reciprocal(stat[:, 2, 0:TT], stat[:, 1, 0:TT]), inv_ready, 1)
            dve.wait_ge(const_in, 48)
            def lower(t):
                dve.wait_ge(xh_ready, t + 1)
                cols = slice(t * P, (t + 1) * P)
                dve.tensor_tensor(XL[:, :, cols], HF[t % 2], XH[:, :, cols].bitcast(F32),
                                  ALU.subtract).then_inc(xl_ready, 1)

            for t in range(TT):
                dve.wait_ge(xt_ready, t + 1)
                if t >= 2:
                    dve.wait_ge(xl_ready, t - 1)
                for j in range(2):
                    dve.tensor_tensor(
                        HF[t % 2][:, 4 * j:4 * j + 4, :],
                        ps[:, 2 * (t % 2) + j, :].rearrange("p (k n) -> p k n", n=P),
                        pv[:, PV["norm_mix"] + 4 * j:PV["norm_mix"] + 4 * j + 4].unsqueeze(2)
                        .to_broadcast([P, 4, P]), ALU.mult).then_inc(hf_ready, 1)
                if t >= 1:
                    lower(t - 1)
            lower(TT - 1)

            def softplus_tail(v, e, s, s2, p, out):
                st.link(dve.tensor_scalar(s, e, 2.0, None, ALU.add))
                st.link(dve.reciprocal(s, s))
                st.link(dve.tensor_tensor(s, s, e, ALU.mult))
                st.link(dve.tensor_tensor(s2, s, s, ALU.mult))
                st.link(dve.tensor_scalar(p, s2, 1.0 / 15, None, ALU.mult))
                for n in (13, 11, 9, 7, 5, 3):
                    st.link(dve.scalar_tensor_tensor(p, p, 1.0 / n, s2, ALU.add, ALU.mult))
                st.link(dve.scalar_tensor_tensor(p, p, 1.0, s, ALU.add, ALU.mult))
                st.link(dve.tensor_scalar(p, p, 2.0, None, ALU.mult))
                st.link(dve.scalar_tensor_tensor(out, v, 0.0, p, ALU.max, ALU.add))

            cols = lambda name: pv[:, PV[name]:PV[name] + 8]
            st.link(dve.tensor_scalar(prep[:, 0, :], cols("lru_ba"), 0.5, None, ALU.mult))
            st.link(dve.tensor_scalar(prep[:, 1, :], cols("lru_bx"), 0.5, None, ALU.mult))
            lam = slice(NS, NS + KT)
            th = lambda t: t.rearrange("p (c h) -> p c h", h=NH)
            st.link(dve.tensor_scalar(sv["v"][:, lam], cols("lam"), -1.0, None, ALU.mult))
            dve.wait_ge(vt_mm, 1)
            dve.wait_ge(hrow_in, 16)
            st.link(dve.tensor_tensor(
                th(sv["v"][:, 0:NS]), th(ps[:, 4, 0:NS]),
                hrow[:, 0, :].unsqueeze(1).to_broadcast([P, TT, NH]), ALU.add))
            link(dve, dve.scalar_tensor_tensor(sv["nab"], sv["v"], -1.0, sv["v"],
                                               ALU.mult, ALU.min), sp_arg, 1)
            dve.wait_ge(sp_exp, 1)
            softplus_tail(*(sv[n] for n in ("v", "e", "s", "s2", "p", "out")))
            dt = sv["out"][:, 0:NS]
            link(dve, dve.scalar_tensor_tensor(
                th(sv["s"][:, 0:NS]), th(dt), -1.0,
                hrow[:, 1, :].unsqueeze(1).to_broadcast([P, TT, NH]), ALU.mult, ALU.mult),
                sp_arg, 2)
            st.link(dve.tensor_scalar(prep[:, 3, :], sv["out"][:, lam], 4.0, None, ALU.mult))
            st.link(dve.tensor_scalar(prep[:, 2, :], sv["out"][:, lam], -4.0, None, ALU.mult))
            st.link(dve.tensor_copy(colv[:, 1, :, :], th(dt)))
            dve.wait_ge(acs_mm, 1)
            link(dve, dve.tensor_copy(colv[:, 0, :, :], th(ps[:, 5, 0:NS])), sp_arg, 3)
            link(dve, dve.tensor_tensor(th(sv["p"][:, 0:NS]), th(ps[:, 5, NS:2 * NS]),
                                        colv[:, 0, :, :], ALU.subtract), sp_arg, 4)
            dve.wait_ge(sp_exp, 2)
            link(dve, dve.tensor_tensor(colv[:, 2, :, :], colv[:, 2, :, :], th(dt), ALU.mult),
                 dt_ready, 1)

            def taps(acc, bank, name, i, stride, last_sem, count, col=0):
                for back in (1, 2, 3):
                    w = param(name, i, stride * (3 - back) + col)
                    ins = dve.scalar_tensor_tensor(
                        acc(back), pair(bank)[:, 0:SEQ - back], w, acc(back),
                        ALU.mult, ALU.add)
                    if back < 3:
                        st.link(ins)
                    else:
                        link(dve, ins, last_sem, count)

            def turn(i):
                part = lambda t, j: lambda n: t[:, bass.ds(j, 1), n:].rearrange(
                    "p a n -> p (a n)")
                hr = part(HR, i)
                dve.wait_ge(tap_u, i + 1)
                taps(hr, 4, "lru_cw", i, 8, u_ready, i + 1)
                dve.wait_ge(tap_e, i + 1)
                taps(part(XBC, i * 2), 0, "ssd_cw", i * 2, 16, cv_e, i + 1)
                dve.wait_ge(a2_act, i + 1)
                link(dve, dve.scalar_tensor_tensor(A2, A2, 1.0, TR, ALU.add, ALU.mult),
                     m2_ready, i + 1)
                st.link(dve.scalar_tensor_tensor(TI, TI, 1.0, hr(0), ALU.add, ALU.mult))
                dve.wait_ge(tap_o, i + 1)
                taps(part(XBC, i * 2 + 1), 2, "ssd_cw", i * 2, 16, cv_o, i + 1, 1)
                dve.wait_ge(sq_act, i + 1)
                st.link(dve.scalar_tensor_tensor(TI, TI, 0.5, A2, ALU.mult, ALU.mult))
                link(dve, dve.tensor_tensor_scan(hr(0), AA, TI, 0.0, ALU.mult, ALU.add),
                     lru_done, i + 1)
                dve.wait_ge(g_act, i + 1)
                link(dve, dve.tensor_tensor(hr(0), hr(0), G, ALU.mult), lru_g, i + 1)

            turns(dve, 0, 8, turn, st, 8)
            dve.wait_ge(g_used, N_GR)
            st.link(dve.memset(STATE, 0.0))
            s3 = lambda t, n=P: t.rearrange("p (a n) -> p a n", n=n)
            def squares(c):
                dve.wait_ge(sqs, c + 1)
                dve.tensor_reduce(ACCS[:, bass.ds(c * P, P)],
                                  SQ.rearrange("p (k n) -> p n k", n=P), AX_X, ALU.add
                                  ).then_inc(accs, 1)

            def chunk(c, p, turn):
                col = lambda q: colv[:, q, bass.ds(c, 1), :].rearrange(
                    "p a h -> p (a h)").unsqueeze(2).to_broadcast([P, NH, HD])
                dve.wait_ge(xp_mm, c + 1)
                wait(dve, y_mm, c)
                wait(dve, st_mm, c)
                link(dve, dve.tensor_tensor(s3(XW, HD), s3(pair(0), HD), col(2), ALU.mult),
                     xw_ready, c + 1)
                link(dve, dve.tensor_tensor(s3(XDT, HD), s3(pair(0), HD), col(1), ALU.mult),
                     xdt_ready, c + 1)
                dve.wait_ge(ts_mm, c + 1)
                link(dve, dve.tensor_tensor(SM, s3(ps[:, 5, :]), tri[:, :].unsqueeze(1)
                                            .to_broadcast([P, NG, P]), ALU.mult),
                     sm_ready, c + 1)
                if not (isinstance(c, int) and c == 0):
                    squares(c - 1)
                dve.wait_ge(e_ready, c + 1)
                link(dve, dve.tensor_tensor(
                    L[p].rearrange("p (g k) l -> p g k l", g=NG),
                    L[p].rearrange("p (g k) l -> p g k l", g=NG),
                    SM.unsqueeze(2).to_broadcast([P, NG, NG, P]), ALU.mult),
                    m_ready, c + 1)
                dve.wait_ge(yo_mm, c + 1)
                st.link(dve.tensor_tensor(s3(STATE, HD), s3(STATE, HD),
                                          decb[:, bass.ds(c, 1), :].rearrange(
                                              "p a h -> p (a h)").unsqueeze(2)
                                          .to_broadcast([P, NH, HD]), ALU.mult))
                dve.wait_ge(st_mm, c + 1)
                link(dve, dve.tensor_tensor(STATE, STATE, pair(6), ALU.add), st_upd, c + 1)
                dve.wait_ge(ea_in, c * 32 + 32)
                st.link(dve.tensor_tensor(s3(YT), s3(pair(4)), EAB, ALU.mult))
                dve.wait_ge(y_mm, c + 1)
                link(dve, dve.tensor_tensor(YT, YT, pair(2), ALU.add), yt_done, c + 1)
                dve.wait_ge(xd_ready, c + 1)
                y = XBC[:, 0:KT, bass.ds(c * P, P)]
                st.link(dve.tensor_tensor(s3(YT), s3(YT), y, ALU.add))
                dve.wait_ge(zc_in[p], turn * 16 + 16)
                link(dve, dve.tensor_tensor(y, s3(YT), ZC[p], ALU.mult), comb, c + 1)

            chunk(0, 0, 0)
            chunk(1, 1, 0)
            with dve.Fori(1, 3) as i:
                st.begin(i - 1, 6)
                chunk(i * 2, 0, i)
                chunk(i * 2 + 1, 1, i)
            st.end(2)
            chunk(6, 0, 3)
            chunk(7, 1, 3)
            squares(7)

            def logits(t):
                dve.wait_ge(lg_mm, t + 1)
                link(dve, dve.tensor_tensor(LG[:, t, :], ps[:, 6, 0:NR], nrow[:, 2 * D:],
                                            ALU.add), lg_done, t + 1)

            dve.wait_ge(late_in, 48)
            dve.wait_ge(devo, 1)
            st.link(dve.reciprocal(stat[:, 4, :], stat[:, 3, :]))
            for k in range(KT):
                dve.wait_ge(ysh_act, k + 1)
                dve.tensor_tensor(YSL[:, k, :], XBC[:, k, :], YSH[:, k, :].bitcast(F32),
                                  ALU.subtract).then_inc(ysl_done, 1)
            for m in range(3 * TT):
                t, cols = m % TT, slice(0, 512) if m // TT != 1 else slice(512, D)
                x2 = X2[:, t, cols]
                dve.wait_ge(pass_mm, m + 1)
                if m < 2 * TT:
                    dve.wait_ge(x_in[t], 16 * (m // TT + 2))
                    ins = dve.scalar_tensor_tensor(x2, ps[:, t, :], stat[:, 4, t:t + 1], XR[t],
                                                   ALU.mult, ALU.add)
                else:
                    dve.wait_ge(evac, m)
                    ins = dve.scalar_tensor_tensor(
                        x2, ps[:, t, :], stat[:, 4, TT + t:TT + t + 1], x2, ALU.mult, ALU.add)
                ins.then_inc(evac, 1)
            for t in range(TT):
                x2 = X2[:, t, 512:D]
                dve.wait_ge(last_mm, t + 1)
                link(dve, dve.scalar_tensor_tensor(x2, ps[:, t % 2, :],
                                                   stat[:, 4, TT + t:TT + t + 1],
                                                   x2, ALU.mult, ALU.add), x2_done, t + 1)
                dve.wait_ge(dev2, t + 1)
                st.link(dve.reciprocal(stat[:, 2, t:t + 1], stat[:, 1, t:t + 1]))
                if t >= 2:
                    dve.wait_ge(h2_out[t % 2], 16 * (t // 2))
                    dve.wait_ge(ht2_mm, t - 1)
                link(dve, dve.scalar_tensor_tensor(H2[t % 2], X2[:, t, :], stat[:, 2, t:t + 1],
                                                   nrow[:, 0:D], ALU.mult, ALU.mult),
                     h2_ready, t + 1)
                if t >= 2:
                    logits(t - 2)
            for t in (TT - 2, TT - 1):
                logits(t)
            b3 = lambda t, w: t.unsqueeze(2).to_broadcast([P, TT, w])

            def first_max(vals, w, mx, eq, pos, out):
                st.link(dve.tensor_reduce(mx, vals, AX_X, ALU.max))
                st.link(dve.tensor_tensor(eq, vals, b3(mx, w), ALU.is_equal))
                st.link(dve.tensor_tensor(pos, eq, falling[:, 0:w].unsqueeze(1)
                                          .to_broadcast([P, TT, w]), ALU.mult))
                st.link(dve.tensor_reduce(r_pm, pos, AX_X, ALU.max))
                st.link(dve.tensor_tensor(out, pos, b3(r_pm, w), ALU.is_equal))

            coarse, fine = LG[:, :, 0:MG], LG[:, :, MG:NR].rearrange("p t (g e) -> p t g e", e=EG)
            first_max(coarse, MG, r_cmax, r_eq, r_pos, r_oh)
            st.link(dve.tensor_tensor(r_exp[:, 0:TT * MG].rearrange("p (t g) -> p t g", g=MG),
                                      coarse, b3(r_cmax, MG), ALU.subtract))
            st.link(dve.tensor_tensor(r_fo, fine, r_oh.unsqueeze(3).to_broadcast(
                [P, TT, MG, EG]), ALU.mult))
            st.link(dve.tensor_reduce(r_f, r_fo.rearrange("p t g e -> p t e g"), AX_X, ALU.add))
            first_max(r_f, EG, r_m1, r_eq8, r_pos8, r_o[0])
            st.link(dve.scalar_tensor_tensor(r_f2, r_o[0], -1e30, r_f, ALU.mult, ALU.add))
            first_max(r_f2, EG, r_m2, r_eq8, r_pos8, r_o[1])
            link(dve, dve.tensor_tensor(r_exp[:, TT * MG:], r_m2, r_m1, ALU.subtract), rt_arg, 1)
            for k in range(2):
                st.link(dve.tensor_tensor(
                    r_M[k].rearrange("p t (g e) -> p t g e", e=EG),
                    r_oh.unsqueeze(3).to_broadcast([P, TT, MG, EG]),
                    r_o[k].unsqueeze(2).to_broadcast([P, TT, MG, EG]), ALU.mult))
            st.link(dve.tensor_tensor(r_sum, r_M[0], r_M[1], ALU.add))
            st.link(dve.memset(r_pre[:, 0, :], 0.0))
            for t in range(1, TT):
                st.link(dve.tensor_tensor(r_pre[:, t, :], r_pre[:, t - 1, :], r_sum[:, t - 1, :],
                                          ALU.add))
            link(dve, dve.tensor_tensor(r_tot, r_pre[:, TT - 1, :], r_sum[:, TT - 1, :],
                                        ALU.add), rk_in, 1)
            bt = lambda row: row.unsqueeze(1).to_broadcast([P, TT, NE])

            def per_choice(table, out):
                for k in range(2):
                    st.link(dve.tensor_tensor(r_tmp, r_M[k], table, ALU.mult))
                    st.link(dve.tensor_reduce(out[:, k * TT:(k + 1) * TT], r_tmp, AX_X, ALU.add))

            def multiples(vals, op, out):
                st.link(dve.tensor_scalar(out, vals, float(P), None, op))
                for m in range(2, TT):
                    st.link(dve.scalar_tensor_tensor(out, vals, float(P * m), out, op, ALU.add))

            per_choice(bt(iota[:, 0:NE]), r_eid)
            dve.wait_ge(rk_mm, 1)
            per_choice(s3(ps[:, 7, 0:TT * NE], NE), r_rk)
            st.link(dve.tensor_copy(r_cnt, ps[:, 7, TT * NE:TT * NE + NE]))
            multiples(r_rk, ALU.is_ge, r_J)
            st.link(dve.scalar_tensor_tensor(r_slot, r_J, -float(P), r_rk, ALU.mult, ALU.add))
            multiples(r_cnt, ALU.is_gt, r_nov)
            st.link(dve.tensor_tensor_scan(r_oinc, ones[:, 0:NE], r_nov, 0.0, ALU.mult, ALU.add))
            st.link(dve.tensor_tensor(r_ost, r_oinc, r_nov, ALU.subtract))
            per_choice(bt(r_ost), r_os)
            st.link(dve.tensor_tensor(r_os, r_os, r_J, ALU.add))
            st.link(dve.tensor_tensor(r_os, r_os, r_eid, ALU.subtract))
            st.link(dve.tensor_scalar(r_g, r_J, 0.0, None, ALU.is_gt))
            st.link(dve.scalar_tensor_tensor(r_os, r_os, NE - 1.0, r_g, ALU.add, ALU.mult))
            st.link(dve.tensor_tensor(r_blk, r_os, r_eid, ALU.add))
            bn = lambda t, w: t.unsqueeze(2).to_broadcast([P, 2 * TT, w])
            bi = lambda w: iota[:, 0:w].unsqueeze(1).to_broadcast([P, 2 * TT, w])
            st.link(dve.tensor_tensor(r_A, bi(P), bn(r_slot, P), ALU.is_equal))
            st.link(dve.tensor_tensor(r_B, bi(NBLK), bn(r_blk, NBLK), ALU.is_equal))
            link(dve, dve.tensor_tensor(r_B, r_B, bn(rowid1, NBLK), ALU.mult), ab_in, 1)
            dve.wait_ge(rt_exp, 1)
            st.link(dve.tensor_reduce(r_gw, r_exp[:, 0:TT * MG].rearrange(
                "p (t g) -> p t g", g=MG), AX_X, ALU.add))
            st.link(dve.scalar_tensor_tensor(r_w1, r_exp[:, TT * MG:], 1.0, r_gw, ALU.add,
                                             ALU.mult))
            st.link(dve.reciprocal(wts[:, 0, :], r_w1))
            st.link(dve.tensor_tensor(wts[:, 1, :], wts[:, 0, :], r_exp[:, TT * MG:], ALU.mult))
            st.link(dve.tensor_tensor(r_ge, iota[:, 0:16].unsqueeze(2).to_broadcast([P, 16, NE]),
                                      r_oinc.unsqueeze(1).to_broadcast([P, 16, NE]), ALU.is_ge))
            st.link(dve.tensor_reduce(over[:, :], r_ge, AX_X, ALU.add))
            st.link(dve.tensor_scalar(over[:, :], over[:, :], NE - 1.0, None, ALU.min))
            st.link(dve.tensor_copy(over[:, 15:16], r_oinc[:, NE - 1:NE]))
            st.link(dve.tensor_copy(over_i[:, :], over[:, :]))
            dve.wait_ge(tab_mm, 1)
            st.link(dve.tensor_scalar(tab_f[:, 1, :], ps[:, 7, 0:NBLK], 0.0, 8192.0,
                                      ALU.is_equal, ALU.mult))
            st.link(dve.scalar_tensor_tensor(tab_f[:, 0, :], ps[:, 7, 0:NBLK], -1.0,
                                             tab_f[:, 1, :], ALU.add, ALU.add))
            st.link(dve.tensor_scalar(tab_f[:, 1, :], tab_f[:, 0, :], float(SEQ), -float(SEQ),
                                      ALU.is_ge, ALU.mult))
            st.link(dve.tensor_tensor(tab_f[:, 1, :], tab_f[:, 1, :], tab_f[:, 0, :], ALU.add))
            link(dve, dve.tensor_copy(tab_i[:, :, :], tab_f[:, :, :]), tab_ready, 1)

            def to_lo(j, at, slot):
                dve.wait_ge(hi_made, at + 1)
                dve.tensor_tensor(WL[slot % HL], ring[j], WH[slot % HL].bitcast(F32),
                                  ALU.subtract).then_inc(lo_made, 1)

            def hidden(b):
                dve.wait_ge(sg_act, b + 1)
                dve.tensor_tensor(HID, SG, ps[:, 1, :], ALU.mult).then_inc(hid_ready, 1)

            def rows_lo(b):
                dve.wait_ge(xt_hi, b + 1)
                dve.tensor_tensor(XTL[:, :], pair(2), XTH[:, :].bitcast(F32),
                                  ALU.subtract).then_inc(xt_lo, 1)

            def hidden_lo(b):
                dve.wait_ge(ht_hi, b + 1)
                dve.tensor_tensor(HTL[:, :], ps[:, 4, :], HTH[:, :].bitcast(F32),
                                  ALU.subtract).then_inc(ht_lo, 1)

            rows_lo(0)
            dve.wait_ge(lo_made, HL)
            for j in range(HL, KT):
                to_lo(j, j, j)
            hidden(0)
            rows_lo(1)
            for j in range(KT // 2):
                to_lo(j, CH + GU_AT + j, GU_AT + j)
            hidden_lo(0)

            def turn(b, last):
                for j in range(KT // 2, KT):
                    to_lo(j, b * CH + (GU_AT + j), GU_AT + j)
                for j in range(KT, CH):
                    to_lo(j, b * CH + (DN_AT - CH + j), DN_AT - CH + j)
                hidden(b)
                rows_lo(b + 1)
                if not last:
                    for j in range(KT // 2):
                        to_lo(j, b * CH + (CH + GU_AT + j), GU_AT + j)
                else:
                    for j in range(KT, CH):
                        to_lo(j, DN_LAST - KT + j, DN_LAST - KT + j)
                hidden_lo(b)

            with dve.Fori(1, NE - 1) as b:
                turn(b, False)
            turn(NE - 1, True)
            n_over = dve.value_load(over_i[0:1, 15:16], min_val=0, max_val=MAX_OVER)

            def overflow_block(o):
                for j in range(KT):
                    to_lo(j, o * CH + (OVER_AT + j), j)
                for j in range(KT, CH):
                    to_lo(j, o * CH + (OVER_AT + j), j)
                hidden(o + NE)
                hidden_lo(o + NE)
                rows_lo(o + (NE + 1))
            overflow_blocks(dve, n_over, overflow_block)
            for t in range(TT):
                dve.wait_ge(x_in[t], 16 * 4)
                for k in range(2):
                    ins = dve.scalar_tensor_tensor(X2[:, t, :], YL[t][:, k, :],
                                                   wts[:, k, t:t + 1], X2[:, t, :],
                                                   ALU.mult, ALU.add)
                    if k == 0:
                        st.link(ins)
                    else:
                        ins.then_inc(x3_ready, 1)
                if t == 3 or t == TT - 1:
                    half = slice(t - 3, t + 1)
                    dve.wait_ge(dev3, t // 4 + 1)
                    link(dve, dve.reciprocal(stat[:, 6, half], stat[:, 5, half]), inv3,
                         t // 4 + 1)
            for t in range(TT // 2, TT):
                dve.scalar_tensor_tensor(X2[:, t, :], X2[:, t, :], stat[:, 6, t:t + 1],
                                         nrow[:, D:2 * D], ALU.mult, ALU.mult
                                         ).then_inc(o_ready, 1)

        @block.gpsimd
        def _(pool):
            st = Steps(pool, pool_step)
            def split(at, slot, loads):
                r, w = slot % RAW, slot % SPL
                pool.wait_ge(g_in[r], loads * 16)
                wait(pool, g_used, at + (1 - SPL))
                link(pool, pool.tensor_tensor(GH[:, w, :], raw[:, r, :],
                                        ones[:, 0:1].to_broadcast([P, GR]), ALU.mult),
                     g_hi, at + 1)
                pool.tensor_tensor(GL[:, w, :], raw[:, r, :], GH[:, w, :].bitcast(F32),
                                   ALU.subtract).then_inc(g_lo, 1)

            pool.wait_ge(ones_ready, 1)
            for at in range(B_AT):
                split(at, at, at // RAW + 1)

            def turn(i, count=B_PER):
                for g in range(count):
                    split(i * B_PER + (B_AT + g), B_AT + g,
                          i * (B_PER // RAW) + ((B_AT + g) // RAW + 1))

            with pool.Fori(0, 7) as i:
                turn(i)
            turn(7, B_PER - 2)
            wide = lambda name: pv[:, PV[name]:PV[name] + KT].unsqueeze(2).to_broadcast(
                [P, KT, P])

            def decays(c, p, turn):
                pool.wait_ge(l_in[p], turn * 16 + 16)
                link(pool, pool.tensor_tensor(
                    L[p], L[p], colv[:, 0, bass.ds(c, 1), :].rearrange("p a h -> p (a h)")
                    .unsqueeze(2).to_broadcast([P, NH, P]), ALU.subtract), diff_ready, c + 1)

            chunk_y = lambda c: XBC[:, 0:KT, bass.ds(c * P, P)]

            def chunk(c, p, turn, last=False):
                pool.wait_ge(xc_in, c * 16 + 16)
                y = chunk_y(c)
                link(pool, pool.tensor_tensor(y, y, wide("ssd_d"), ALU.mult), xd_ready, c + 1)
                if not last:
                    decays(c + 1, 1 - p, turn + p)
                pool.wait_ge(sql, c + 1)
                link(pool, pool.tensor_tensor(ACCL, ACCL, SQL, ALU.add), accl, c + 1)
                pool.wait_ge(ylh_act, c + 1)
                part = lambda t: t[:, bass.ds(c, 1), :].rearrange("p a n -> p (a n)")
                pool.tensor_tensor(part(YLL), part(HR), part(YLH).bitcast(F32),
                                   ALU.subtract).then_inc(yll_done, 1)
                if last:
                    split_w(0)
                    split_w(1)
                pool.wait_ge(sqs, c + 1)
                pool.tensor_tensor(pad[:, 0:1], ones[:, 0:1], ones[:, 0:1], ALU.mult)
                y = chunk_y(c)
                pool.tensor_tensor(y, y, wide("ssd_norm"), ALU.mult).then_inc(ssd_w, 1)

            def split_w(at):
                n = W_ORDER[at]
                k, last = n % KT, n >= 3 * KT
                hi, lo = ((LW[:, q2, k, :] if last else SW[:, n % 2, q2, :]) for q2 in range(2))
                pool.wait_ge(w_in3[at % 3], 16 * (at // 3 + 1))
                if n < 2:
                    pool.wait_ge(y_mm, 7)
                elif not last:
                    if (n - 2) % KT == KT - 1:
                        pool.wait_ge(pass_mm, n - 1)
                    else:
                        pool.wait_ge(w_used, (n - 2) // KT * (KT - 1) + (n - 2) % KT + 1)
                else:
                    pool.wait_ge(pass_mm, 2 * TT)
                raw_w = wraw[:, at % 3, :]
                link(pool, pool.tensor_tensor(hi, raw_w, ones[:, 0:1].to_broadcast([P, 512]),
                                              ALU.mult), w_hi, at + 1)
                pool.tensor_tensor(lo, raw_w, hi.bitcast(F32), ALU.subtract).then_inc(w_lo, 1)

            decays(0, 0, 0)
            pool.wait_ge(g_used, N_GR)
            pool.wait_ge(lru_g, 8)
            st.link(pool.memset(ACCL, 0.0))
            chunk(0, 0, 0)
            chunk(1, 1, 0)
            with pool.Fori(1, 3) as i:
                chunk(i * 2, 0, i)
                chunk(i * 2 + 1, 1, i)
            chunk(6, 0, 3)
            chunk(7, 1, 3, last=True)
            for at in range(2, 4 * KT):
                split_w(at)
            pool.wait_ge(last_mm, TT)
            for j in range(HL):
                pool.wait_ge(hi_made, j + 1)
                pool.tensor_tensor(WL[j], ring[j], WH[j].bitcast(F32), ALU.subtract
                                   ).then_inc(lo_made, 1)
            pool.wait_ge(tab_ready, 1)
            pool.wait_ge(h2_out[0], 16 * TT // 2)
            pool.wait_ge(h2_out[1], 16 * TT // 2)
            one = ones[:, 0:1]

            def gather(b):
                if not (isinstance(b, int) and b == 0):
                    pool.wait_ge(xb_mm, b)
                st.link(pool.tensor_copy(idx_g[:, :], tab_i[:, 1, bass.ds(b, 1)]))
                pool.tensor_tensor(pad[:, 0:1], one, one, ALU.mult)
                pool.indirect_dma_start(
                    out=XB[:, :], out_offset=None, in_=h2_d,
                    in_offset=bass.IndirectOffsetOnAxis(ap=idx_g[:, 0:1], axis=0),
                    bounds_check=SEQ - 1, oob_is_err=False).then_inc(xb_in, 16)

            def scatter(b):
                pool.wait_ge(yb_act, b + 1)
                wait(pool, y_out, b * 16)
                st.link(pool.tensor_copy(idx_s[:, :], tab_i[:, 0, bass.ds(b, 1)]))
                pool.tensor_tensor(pad[:, 1:2], one, one, ALU.mult)
                pool.indirect_dma_start(
                    out=y_d, out_offset=bass.IndirectOffsetOnAxis(ap=idx_s[:, 0:1], axis=0),
                    in_=YB[:, :], in_offset=None, bounds_check=2 * SEQ - 1,
                    oob_is_err=False).then_inc(y_out, 16)

            st.link(pool.memset(XB[:, :], 0.0))
            gather(0)
            gather(1)
            gather(2)
            scatter(0)
            with pool.Fori(2, NE) as b:
                st.begin(b - 2, 2)
                gather(b + 1)
                scatter(b - 1)
            st.end(NE - 2)
            n_over = pool.value_load(over_i[0:1, 15:16], min_val=0, max_val=MAX_OVER)
            links = st.done

            def overflow_block(o):
                st.done = links
                st.begin(o, 2)
                gather(o + (NE + 1))
                scatter(o + (NE - 1))
            overflow_blocks(pool, n_over, overflow_block)
            st.turn, st.done = n_over * 2, links
            scatter(n_over + (NE - 1))
            st.turn = None
            for t in range(TT // 2):
                pool.wait_ge(scaled, t + 1)
                pool.tensor_tensor(X2[:, t, :], X2[:, t, :], nrow[:, D:2 * D], ALU.mult
                                   ).then_inc(o_early, 1)
            pool.wait_ge(y_out, n_over * 16 + NE * 16)
            pool.wait_ge(scr_out, 32)


def kernel(**inputs):
    import concourse.bacc as bacc
    from concourse.bass_utils import run_bass_kernel_spmd

    f = {k: np.asarray(v) for k, v in inputs.items()}
    rows = lambda v: v.reshape(-1, P).T
    w_in = f["w_in"][0]
    w_dt = np.concatenate([w_in[:, DT_COL:], np.zeros((D, P - NH), np.float32)], axis=1)
    tiles = np.concatenate([w_in[:, :DT_COL], w_dt], axis=1).reshape(2, KT // 2, P, -1, P)
    tiles = tiles.transpose(3, 0, 2, 1, 4).reshape(-1, 2, P, GR)
    lru, gate, z, xbc, dt = 0, 8, 16, 24, 40
    order = [dt, z]
    for i in range(8):
        order += [lru + i, xbc + 2 * i, xbc + 2 * i + 1, gate + i, z + i + 1]
    win = tiles[order[:-1]].reshape(N_GR, P, GR)
    wblk = np.zeros((KT, P, 2, P), np.float32)
    for g, name in enumerate(("lru_wa", "lru_wx")):
        for q in range(2):
            s = slice(HD * q, HD * (q + 1))
            wblk[:, s, g, s] = f[name][0].reshape(KT, 2, HD, HD)[:, q]
    pv = np.concatenate([
        rows(f["norm_mix"][0]), rows(f["lru_conv_w"][0]), rows(f["lru_conv_b"][0]),
        rows(f["lru_ba"][0].reshape(-1)), rows(f["lru_bx"][0].reshape(-1)),
        rows(f["lru_lambda"][0]), rows(f["lru_norm"][0]), rows(f["ssd_norm"][0]),
        rows(f["ssd_conv_w"][0]), rows(f["ssd_conv_b"][0]),
        rows(np.repeat(f["ssd_d"][0], HD))], axis=1)
    hpar = np.stack([f["ssd_dt_bias"][0], f["ssd_a_log"][0]])
    wout = f["w_out"][0].reshape(2, KT, P, 2, 512).transpose(0, 3, 1, 2, 4).reshape(-1, P, 512)
    wout = wout[W_ORDER]
    fine = f["w_fine"][0].transpose(1, 0, 2).reshape(D, NE)
    wr = np.concatenate([f["w_coarse"][0], fine], axis=1).reshape(KT, P, NR).transpose(1, 0, 2)
    nrow = np.concatenate([f["norm_ffn"][0], f["final_norm"], f["b_coarse"][0],
                           f["b_fine"][0].reshape(-1)])
    gu = np.stack([f["w_gate"][0].reshape(NE, KT, P, DE), f["w_up"][0].reshape(NE, KT, P, DE)],
                  axis=3).reshape(NE, KT, P, 2 * DE)
    moe = np.concatenate([gu, f["w_down"][0].reshape(NE, DE // P, P, D)], axis=1)
    n = np.arange(P, dtype=np.float32)
    tok = np.arange(TT)[None, :] * P + np.arange(P)[:, None]
    cst = np.concatenate([
        np.broadcast_to(n, (P, P)), tok + 1, SEQ + tok + 1,
        np.broadcast_to(EG - np.arange(EG), (P, EG)), n[:, None] < n[None, :]],
        axis=1).astype(np.float32)
    tri = (n[None, :] >= n[:, None]).astype(np.float32)
    arrays = {
        "x": f["x"].reshape(TT, P, D), "win": win, "wblk": wblk, "pv": pv,
        "hpar": hpar, "wout": wout, "wr": wr, "nrow": nrow, "moe": moe.reshape(NE * CH, P, D),
        "cst": cst, "tri": tri, "ident": np.eye(P, dtype=np.float32)}
    nc = bacc.Bacc("TRN2", target_bir_lowering=False, num_devices=1)
    a, feeds = {}, {}
    for name, v in arrays.items():
        feeds["in_" + name] = np.ascontiguousarray(v)
        a[name] = nc.dram_tensor("in_" + name, v.shape, F32, kind="ExternalInput").ap()
    a["out"] = nc.dram_tensor("out_x", (TT, P, D), F32, kind="ExternalOutput").ap()
    build(nc, a)
    r = run_bass_kernel_spmd(nc, [feeds], core_ids=[0])
    return r.results[0]["out_x"].reshape(1, SEQ, D)
```
